# Optimizing a Trainium2 kernel written in Bass

```python
import jax
import jax.numpy as jnp
from jax import lax
import numpy as np

D_MODEL = 1024
BATCH = 1
SEQ = 1024
DEPTH = 1
DEC_BATCH = 8
DEC_SEQ = 1
PAST_LEN = 256
PAGE_SIZE = 128

HEAD_DIM = 64
N_HEADS_A = 8
WIDTH_A = N_HEADS_A * HEAD_DIM
DIL_PAIRS = ((128, 1), (512, 4), (2048, 16))
HEADS_PER_GROUP = 4
N_HEADS_B = HEADS_PER_GROUP * len(DIL_PAIRS)
WIDTH_B = N_HEADS_B * HEAD_DIM
WIDTH_B_OUT = HEADS_PER_GROUP * HEAD_DIM
IN_SPLITS = (WIDTH_A, WIDTH_A, WIDTH_A, N_HEADS_A, WIDTH_B, WIDTH_B, WIDTH_B, D_MODEL, D_MODEL)
IN_COLS = sum(IN_SPLITS)
D_FF = 2816
N_BUCKETS = 32
MAX_DISTANCE = 2048
Q_BLOCK = 128
EPS = 1e-6
NEG_INF = -1e30

kernel_name = 'fox_dilated_gated_hybrid_step'

def rmsnorm(x, g):
    xf = x.astype(jnp.float32)
    y = xf * lax.rsqrt(jnp.mean(jnp.square(xf), axis=-1, keepdims=True) + EPS)
    return (y * g.astype(jnp.float32)).astype(x.dtype)

def half_ffn(x, pre_g, post_g, w_gate, w_up, w_down):
    h = rmsnorm(x, pre_g)
    u = jax.nn.silu(h @ w_gate) * (h @ w_up)
    return x + 0.5 * rmsnorm(u @ w_down, post_g)

def t5_buckets(dist):
    dist = np.asarray(dist)
    max_exact = N_BUCKETS // 2
    large = max_exact + (np.log(np.maximum(dist, 1) / max_exact)
                         / np.log(MAX_DISTANCE / max_exact) * (N_BUCKETS - max_exact)).astype(np.int32)
    large = np.minimum(large, N_BUCKETS - 1)
    return np.where(dist < max_exact, dist, large).astype(np.int32)

def group_bias(rel_bias, g, window, dil):
    buckets = t5_buckets(np.arange(window // dil + 1) * dil)
    hs = slice(g * HEADS_PER_GROUP, (g + 1) * HEADS_PER_GROUP)
    return rel_bias[buckets][:, hs].T.astype(jnp.float32)

def in_projection(h, w_in, b_f):
    b, t, _ = h.shape
    offs = [int(o) for o in np.cumsum(IN_SPLITS)[:-1]]
    qa, ka, va, fa, qb, kb, vb, ga, gb = jnp.split(h @ w_in, offs, axis=-1)
    heads = lambda z, n: z.reshape(b, t, n, HEAD_DIM)
    logf = jax.nn.log_sigmoid((fa + b_f).astype(jnp.float32))
    scale = HEAD_DIM ** -0.5
    return (heads(qa, N_HEADS_A) * scale, heads(ka, N_HEADS_A), heads(va, N_HEADS_A), logf,
            heads(qb, N_HEADS_B) * scale, heads(kb, N_HEADS_B), heads(vb, N_HEADS_B),
            jax.nn.sigmoid(ga), jax.nn.sigmoid(gb))

def merge_branches(x, o_a, o_b, g_a, g_b, post_g, w_proj_a, w_proj_b, w_out):
    y = (g_a * (o_a @ w_proj_a) + g_b * (o_b @ w_proj_b)) @ w_out
    return x + rmsnorm(y, post_g)

def fox_prompt(q, k, v, logf):
    b, t, h, dh = q.shape
    n_blk = t // Q_BLOCK
    c_t = jnp.cumsum(logf, axis=1).transpose(0, 2, 1)
    q_blk = q.reshape(b, n_blk, Q_BLOCK, h, dh).transpose(1, 0, 2, 3, 4)
    c_blk = c_t.reshape(b, h, n_blk, Q_BLOCK).transpose(2, 0, 1, 3)
    k_pos = jnp.arange(t)

    def block(args):
        i, q_i, c_i = args
        s = jnp.einsum('bqhd,bkhd->bhqk', q_i, k).astype(jnp.float32)
        s = s + (c_i[..., :, None] - c_t[:, :, None, :])
        q_pos = i * Q_BLOCK + jnp.arange(Q_BLOCK)
        s = jnp.where(k_pos[None, :] <= q_pos[:, None], s, NEG_INF)
        p = jax.nn.softmax(s, axis=-1)
        return jnp.einsum('bhqk,bkhd->bqhd', p.astype(v.dtype), v)

    o = lax.map(block, (jnp.arange(n_blk), q_blk, c_blk))
    return o.transpose(1, 0, 2, 3, 4).reshape(b, t, h * dh)

def fox_sample(q, k_new, v_new, logf_new, cache_k, cache_v, cache_logf, page_table):
    nb, sn, h, dh = q.shape
    k_past = cache_k[page_table].reshape(nb, -1, h, dh)
    v_past = cache_v[page_table].reshape(nb, -1, h, dh)
    lf_past = cache_logf[page_table].reshape(nb, -1, h).astype(jnp.float32)
    c_past = jnp.cumsum(lf_past, axis=1)
    c_new = c_past[:, -1:, :] + jnp.cumsum(logf_new, axis=1)
    c_past_t, c_new_t = c_past.transpose(0, 2, 1), c_new.transpose(0, 2, 1)
    s_past = (jnp.einsum('bqhd,bkhd->bhqk', q, k_past).astype(jnp.float32)
              + (c_new_t[..., :, None] - c_past_t[:, :, None, :]))
    s_new = (jnp.einsum('bqhd,bkhd->bhqk', q, k_new).astype(jnp.float32)
             + (c_new_t[..., :, None] - c_new_t[:, :, None, :]))
    s_new = jnp.where(np.tril(np.ones((sn, sn), dtype=bool)), s_new, NEG_INF)
    p = jax.nn.softmax(jnp.concatenate([s_past, s_new], axis=-1), axis=-1).astype(v_new.dtype)
    n_past = k_past.shape[1]
    o = (jnp.einsum('bhqk,bkhd->bqhd', p[..., :n_past], v_past)
         + jnp.einsum('bhqk,bkhd->bqhd', p[..., n_past:], v_new))
    return o.reshape(nb, sn, h * dh)

def dilated_core(q, kv_g, bias, valid):
    s = jnp.einsum('bqhd,bqjhd->bqhj', q, kv_g[:, :, :, 0]).astype(jnp.float32) + bias
    s = jnp.where(valid[None, :, None, :], s, NEG_INF)
    m = jnp.max(s, axis=-1)
    e = jnp.exp(s - m[..., None])
    num = jnp.einsum('bqhj,bqjhd->bqhd', e, kv_g[:, :, :, 1].astype(jnp.float32))
    return num, jnp.sum(e, axis=-1), m

def dilated_prompt(q, k, v, bias, window, dil):
    b, t, h, dh = q.shape
    n_blk = t // Q_BLOCK
    n_slots = window // dil + 1
    kv = jnp.pad(jnp.stack([k, v], axis=2), ((0, 0), (window, 0), (0, 0), (0, 0), (0, 0)))
    rel = np.arange(Q_BLOCK)[:, None] - np.arange(n_slots)[None, :] * dil
    idx = window + rel
    q_blk = q.reshape(b, n_blk, Q_BLOCK, h, dh).transpose(1, 0, 2, 3, 4)

    def block(args):
        i, q_i = args
        t0 = i * Q_BLOCK
        slab = lax.dynamic_slice_in_dim(kv, t0, window + Q_BLOCK, axis=1)
        valid = (t0 + rel) >= 0
        return dilated_core(q_i, slab[:, idx], bias, valid)

    num, den, m = lax.map(block, (jnp.arange(n_blk), q_blk))
    unblk = lambda z: jnp.moveaxis(z, 0, 1).reshape((b, t) + z.shape[3:])
    return unblk(num), unblk(den), unblk(m)

def dilated_sample(q, k_new, v_new, buf_kv, bias, window, dil):
    sn = q.shape[1]
    n_buf = buf_kv.shape[1]
    n_slots = window // dil + 1
    kv_all = jnp.concatenate([buf_kv, jnp.stack([k_new, v_new], axis=2)], axis=1)
    pos = n_buf + np.arange(sn)[:, None] - np.arange(n_slots)[None, :] * dil
    part = dilated_core(q, kv_all[:, np.maximum(pos, 0)], bias, pos >= 0)
    new_buf = kv_all[:, -min(window, n_buf + sn):]
    return part, new_buf

def combine_groups(parts, dtype):
    m_all = jnp.stack([m for _, _, m in parts])
    w = jnp.exp(m_all - jnp.max(m_all, axis=0))
    num = sum(w[g][..., None] * parts[g][0] for g in range(len(parts)))
    den = sum(w[g] * parts[g][1] for g in range(len(parts)))
    o = num / den[..., None]
    return o.reshape(o.shape[:2] + (-1,)).astype(dtype)

def layer_prompt(x, p, rel_bias):
    t = x.shape[1]
    x = half_ffn(x, p['ffn1_pre_g'], p['ffn1_post_g'], p['ffn1_w_gate'], p['ffn1_w_up'], p['ffn1_w_down'])
    h = rmsnorm(x, p['mix_pre_g'])
    qa, ka, va, logf, qb, kb, vb, ga, gb = in_projection(h, p['w_in'], p['b_f'])
    o_a = fox_prompt(qa, ka, va, logf)
    parts, bufs = [], []
    for g, (window, dil) in enumerate(DIL_PAIRS):
        hs = slice(g * HEADS_PER_GROUP, (g + 1) * HEADS_PER_GROUP)
        parts.append(dilated_prompt(qb[:, :, hs], kb[:, :, hs], vb[:, :, hs],
                                    group_bias(rel_bias, g, window, dil), window, dil))
        n_keep = min(window, t)
        bufs.append(jnp.stack([kb[:, t - n_keep:, hs], vb[:, t - n_keep:, hs]], axis=2))
    o_b = combine_groups(parts, x.dtype)
    x = merge_branches(x, o_a, o_b, ga, gb, p['mix_post_g'], p['w_proj_a'], p['w_proj_b'], p['w_out'])
    x = half_ffn(x, p['ffn2_pre_g'], p['ffn2_post_g'], p['ffn2_w_gate'], p['ffn2_w_up'], p['ffn2_w_down'])
    return x, (ka, va, logf, bufs[0], bufs[1], bufs[2])

def layer_sample(x, p, rel_bias, cache_k, cache_v, cache_logf, bufs_in, page_table):
    x = half_ffn(x, p['ffn1_pre_g'], p['ffn1_post_g'], p['ffn1_w_gate'], p['ffn1_w_up'], p['ffn1_w_down'])
    h = rmsnorm(x, p['mix_pre_g'])
    qa, ka, va, logf, qb, kb, vb, ga, gb = in_projection(h, p['w_in'], p['b_f'])
    o_a = fox_sample(qa, ka, va, logf, cache_k, cache_v, cache_logf, page_table)
    parts, bufs = [], []
    for g, (window, dil) in enumerate(DIL_PAIRS):
        hs = slice(g * HEADS_PER_GROUP, (g + 1) * HEADS_PER_GROUP)
        part, new_buf = dilated_sample(qb[:, :, hs], kb[:, :, hs], vb[:, :, hs], bufs_in[g],
                                       group_bias(rel_bias, g, window, dil), window, dil)
        parts.append(part)
        bufs.append(new_buf)
    o_b = combine_groups(parts, x.dtype)
    x = merge_branches(x, o_a, o_b, ga, gb, p['mix_post_g'], p['w_proj_a'], p['w_proj_b'], p['w_out'])
    x = half_ffn(x, p['ffn2_pre_g'], p['ffn2_post_g'], p['ffn2_w_gate'], p['ffn2_w_up'], p['ffn2_w_down'])
    return x, (ka, va, logf, bufs[0], bufs[1], bufs[2])

def setup_inputs(seed: int = 0) -> dict:
    key = jax.random.key(seed)
    ks = iter(list(jax.random.split(key, 32)))

    def nrm(shape, scale):
        return scale * jax.random.normal(next(ks), shape, jnp.float32)

    def gain(shape):
        return 1.0 + 0.05 * jax.random.normal(next(ks), shape, jnp.float32)

    n_pages = PAST_LEN // PAGE_SIZE
    n_used = DEC_BATCH * n_pages
    n_pool = n_used + n_used // 4
    d = D_MODEL
    return {
        'x_prompt': nrm((BATCH, SEQ, d), 1.0),
        'x_sample': nrm((DEC_BATCH, DEC_SEQ, d), 1.0),
        'cache_a_k': nrm((DEPTH, n_pool, PAGE_SIZE, N_HEADS_A, HEAD_DIM), 1.0),
        'cache_a_v': nrm((DEPTH, n_pool, PAGE_SIZE, N_HEADS_A, HEAD_DIM), 1.0),
        'cache_a_logf': jax.nn.log_sigmoid(2.0 + nrm((DEPTH, n_pool, PAGE_SIZE, N_HEADS_A), 1.0)),
        'cache_b1_kv': nrm((DEPTH, DEC_BATCH, min(DIL_PAIRS[0][0], PAST_LEN), 2, HEADS_PER_GROUP, HEAD_DIM), 1.0),
        'cache_b2_kv': nrm((DEPTH, DEC_BATCH, min(DIL_PAIRS[1][0], PAST_LEN), 2, HEADS_PER_GROUP, HEAD_DIM), 1.0),
        'cache_b3_kv': nrm((DEPTH, DEC_BATCH, min(DIL_PAIRS[2][0], PAST_LEN), 2, HEADS_PER_GROUP, HEAD_DIM), 1.0),
        'page_table': jax.random.permutation(next(ks), n_pool)[:n_used].reshape(DEC_BATCH, n_pages).astype(jnp.int32),
        'rel_bias': nrm((N_BUCKETS, N_HEADS_B), 0.5),
        'ffn1_pre_g': gain((DEPTH, d)),
        'ffn1_post_g': gain((DEPTH, d)),
        'ffn1_w_gate': nrm((DEPTH, d, D_FF), d ** -0.5),
        'ffn1_w_up': nrm((DEPTH, d, D_FF), d ** -0.5),
        'ffn1_w_down': nrm((DEPTH, D_FF, d), D_FF ** -0.5),
        'mix_pre_g': gain((DEPTH, d)),
        'mix_post_g': gain((DEPTH, d)),
        'w_in': nrm((DEPTH, d, IN_COLS), d ** -0.5),
        'b_f': 2.0 + nrm((DEPTH, N_HEADS_A), 0.5),
        'w_proj_a': nrm((DEPTH, WIDTH_A, d), WIDTH_A ** -0.5),
        'w_proj_b': nrm((DEPTH, WIDTH_B_OUT, d), WIDTH_B_OUT ** -0.5),
        'w_out': nrm((DEPTH, d, d), d ** -0.5),
        'ffn2_pre_g': gain((DEPTH, d)),
        'ffn2_post_g': gain((DEPTH, d)),
        'ffn2_w_gate': nrm((DEPTH, d, D_FF), d ** -0.5),
        'ffn2_w_up': nrm((DEPTH, d, D_FF), d ** -0.5),
        'ffn2_w_down': nrm((DEPTH, D_FF, d), D_FF ** -0.5),
    }

def reference(x_prompt, x_sample, cache_a_k, cache_a_v, cache_a_logf, cache_b1_kv, cache_b2_kv,
              cache_b3_kv, page_table, rel_bias, ffn1_pre_g, ffn1_post_g, ffn1_w_gate, ffn1_w_up,
              ffn1_w_down, mix_pre_g, mix_post_g, w_in, b_f, w_proj_a, w_proj_b, w_out,
              ffn2_pre_g, ffn2_post_g, ffn2_w_gate, ffn2_w_up, ffn2_w_down):
    prompt_states, sample_states = [], []
    for l in range(DEPTH):
        p = {
            'ffn1_pre_g': ffn1_pre_g[l], 'ffn1_post_g': ffn1_post_g[l], 'ffn1_w_gate': ffn1_w_gate[l],
            'ffn1_w_up': ffn1_w_up[l], 'ffn1_w_down': ffn1_w_down[l],
            'mix_pre_g': mix_pre_g[l], 'mix_post_g': mix_post_g[l], 'w_in': w_in[l], 'b_f': b_f[l],
            'w_proj_a': w_proj_a[l], 'w_proj_b': w_proj_b[l], 'w_out': w_out[l],
            'ffn2_pre_g': ffn2_pre_g[l], 'ffn2_post_g': ffn2_post_g[l], 'ffn2_w_gate': ffn2_w_gate[l],
            'ffn2_w_up': ffn2_w_up[l], 'ffn2_w_down': ffn2_w_down[l],
        }
        x_prompt, st_p = layer_prompt(x_prompt, p, rel_bias)
        x_sample, st_s = layer_sample(x_sample, p, rel_bias, cache_a_k[l], cache_a_v[l], cache_a_logf[l],
                                      (cache_b1_kv[l], cache_b2_kv[l], cache_b3_kv[l]), page_table)
        prompt_states.append(st_p)
        sample_states.append(st_s)
    k_a_p, v_a_p, lf_a_p, kv_b1_p, kv_b2_p, kv_b3_p = [jnp.stack(z) for z in zip(*prompt_states)]
    k_a_s, v_a_s, lf_a_s, kv_b1_s, kv_b2_s, kv_b3_s = [jnp.stack(z) for z in zip(*sample_states)]
    return (x_prompt, x_sample, k_a_p, v_a_p, lf_a_p, kv_b1_p, kv_b2_p, kv_b3_p,
            k_a_s, v_a_s, lf_a_s, kv_b1_s, kv_b2_s, kv_b3_s)


_drawn_inputs = setup_inputs


def setup_inputs(seed=0):
    import zlib

    import numpy as np

    out = dict(_drawn_inputs(seed))
    spreads = {}
    factors = {'ffn2_post_g': 3.664}
    for name, (base, spread) in spreads.items():
        noise = np.random.default_rng([zlib.crc32(name.encode()), seed]).standard_normal(out[name].shape)
        drawn = base * np.exp(spread * noise) if base else spread * noise
        out[name] = jnp.asarray(drawn.astype(out[name].dtype))
    for name, factor in factors.items():
        out[name] = (out[name] * factor).astype(out[name].dtype)
    return out
```

```python
from contextlib import ExitStack

import numpy as np
import concourse.bass as bass
from concourse import mybir

F32, F32R, BF16, I32 = mybir.dt.float32, mybir.dt.float32r, mybir.dt.bfloat16, mybir.dt.int32
ALU, ACT, AX = mybir.AluOpType, mybir.ActivationFunctionType, mybir.AxisListType

P = 128
D = 1024
KD = D // P
SEQ, NB = 1024, 8
T = SEQ + NB
PARTS = ((0, 352), (352, 352), (704, 328))
DFF = 2816
HD = 64
NHA, WA = 8, 512
DIL = (1, 4, 16)
HPG = 4
WB = 768
PAIRS_A, PAIRS_B = NHA // 2, HPG // 2
COL_QA, COL_KA, COL_VA, COL_FA = 0, 512, 1024, 1536
COL_QB = 1544
COL_KB, COL_VB = COL_QB + WB, COL_QB + 2 * WB
COL_GA = COL_QB + 3 * WB
COL_GB = COL_GA + D
NQ = SEQ // P
PAGE, NPAGE = 128, 2
CH = 1024
RING = 3
FFN_ITERS = DFF // P // 2
MERGE_ITERS = KD // 2
SCALE = HD ** -0.5
EPS = 1e-6
NEG = -1e30
LREL = 384
N_BUCKETS, MAX_DISTANCE = 32, 2048
SAMPLE_KEYS = (128, 64, 16)

PHASES = ("ffn1", "forget", "fox", "dil", "merge", "ffn2")
ITERS = dict(ffn1=FFN_ITERS, forget=1, fox=PAIRS_A, dil=PAIRS_B * 3, merge=MERGE_ITERS, ffn2=FFN_ITERS)
CHUNKS = dict(ffn1=6, forget=1, fox=3, dil=3, merge=9, ffn2=6)
FFN_BLOCKS = [(0, 0, 128, 8, "act"), (1, 0, 128, 8, "u"), (2, 0, 128, 8, "act"), (3, 0, 128, 8, "u")] + \
             [(4 + m // 4, 128 * (m % 4), 512, 2, "dve") for m in range(8)]
QKV_BLOCKS = [(0, 0, 128, 8, "dve"), (1, 0, 128, 8, "dve"), (2, 0, 128, 8, "act")]
MERGE_BLOCKS = [(0, 0, 128, 8, "act"), (1, 0, 128, 8, "act"), (2, 0, 256, 4, "dve"), (2, 128, 256, 4, "dve"),
                (3, 0, 128, 8, "act"), (4, 0, 128, 8, "act"), (5, 0, 256, 2, "dve"), (5, 128, 256, 2, "dve")] + \
               [(6 + m // 3, 128 * (m % 3), 384, 2, "dve") for m in range(8)]
BLOCKS = dict(ffn1=FFN_BLOCKS, ffn2=FFN_BLOCKS, forget=[(0, 0, 128, 8, "act")], fox=QKV_BLOCKS, dil=QKV_BLOCKS,
              merge=MERGE_BLOCKS)


class Counts:

    def __init__(self, chunks, chunk_of, block_of, free_of, before, last_block):
        self.chunks, self.chunk_of, self.block_of = chunks, chunk_of, block_of
        self.free_of, self.before, self.last_block = free_of, before, last_block


def plan():
    chunk = block = 0
    freed = dict(act=0, dve=0, u=0)
    chunk_of, block_of, free_of, before, last_block = {}, {}, {}, {}, {}
    user = [None, None]
    for ph in PHASES:
        for i in range(ITERS[ph]):
            for j, (c, _, _, _, who) in enumerate(BLOCKS[ph]):
                key = (ph, i, j)
                chunk_of[key] = chunk + c
                last_block[chunk + c] = block
                block_of[key] = block
                free_of[key] = (who, freed[who])
                before[key] = user[j % 2]
                user[j % 2] = key
                freed[who] += 3
                block += 1
            chunk += CHUNKS[ph]
    return Counts(chunk, chunk_of, block_of, free_of, before, last_block)


PLAN = plan()
FIRST_CHUNK = {}
for _ph in PHASES:
    FIRST_CHUNK[_ph] = PLAN.chunk_of[_ph, 0, 0]


def lin(f, i, lo, hi):
    if isinstance(i, int):
        return f(i)
    a, d = f(lo), (f(lo + 1) - f(lo) if hi > lo + 1 else 0)
    assert all(f(x) == a + d * (x - lo) for x in range(lo, hi))
    return (i * d + (a - d * lo)) if d else a


def t5_buckets(dist):
    dist = np.asarray(dist)
    exact = N_BUCKETS // 2
    large = exact + (np.log(np.maximum(dist, 1) / exact) / np.log(MAX_DISTANCE / exact)
                     * (N_BUCKETS - exact)).astype(np.int32)
    return np.where(dist < exact, dist, np.minimum(large, N_BUCKETS - 1)).astype(np.int32)


def shape_constants():
    c = {}
    sel = np.zeros((P, NHA, P), np.float32)
    for h in range(NHA):
        sel[h, h] = sel[32 + h, h] = 1.0
    c["head_sel"] = sel.reshape(P, -1)
    c["ident"] = np.eye(P, dtype=np.float32)
    q, k = np.arange(P)[:, None], np.arange(P)[None, :]
    c["causal"] = np.where(k <= q, 0.0, NEG).astype(np.float32)
    c["upto"] = (q <= k).astype(np.float32)
    prompt = np.zeros((N_BUCKETS + 1, 3, LREL), np.float32)
    sample = np.zeros((N_BUCKETS + 1, 3, P), np.float32)
    for g, dil in enumerate(DIL):
        most = min(128, SEQ // dil - 1)
        for y in range(LREL):
            d = 255 - y
            if 0 <= d <= most:
                prompt[t5_buckets(d * dil), g, y] = 1.0
            else:
                prompt[N_BUCKETS, g, y] = NEG
        for p in range(P):
            if p < SAMPLE_KEYS[g]:
                sample[t5_buckets((SAMPLE_KEYS[g] - p) * dil), g, p] = 1.0
            else:
                sample[N_BUCKETS, g, p] = NEG
    new = np.zeros((N_BUCKETS + 1, NB), np.float32)
    new[t5_buckets(0)] = 1.0
    c["sel_prompt"], c["sel_sample"], c["sel_new"] = prompt.reshape(33, -1), sample.reshape(33, -1), new
    own = np.where(np.arange(NB)[:, None] == np.arange(NB)[None, :], 0.0, NEG).astype(np.float32)
    c["own_a"] = np.repeat(own, NHA, axis=0)
    c["own_b"] = np.repeat(own, HPG, axis=0)
    return c


def build(nc, A):
    ctx = ExitStack()
    with ctx:
        class Place:

            def __init__(self, at, end):
                self.at, self.end = at, end

            def __call__(self, name, shape, dt):
                n = int(np.prod(shape[1:])) * (2 if dt == BF16 else 4)
                t = nc.alloc_sbuf_tensor_at(name, shape, dt, offset=self.at)
                self.at += -(-n // 32) * 32
                assert self.at <= self.end, (name, self.at, self.end)
                return t

        base = -(-nc.sbuf_base // 32) * 32
        ring = Place(base, base + 3 * RING * 4 * CH)
        w_raw = ring("w_raw", [P, RING, CH], F32)
        w_hi = ring("w_hi", [P, RING, CH], F32R)
        w_lo = ring("w_lo", [P, RING, CH], F32R)
        hidden = Place(ring.end, ring.end + 2 * 4 * KD * T)
        h_hi = hidden("h_hi", [P, KD, T], F32R)
        h_lo = hidden("h_lo", [P, KD, T], F32R)
        R0 = hidden.end
        R1, R2, R3, R4, R5 = R0 + 33024, R0 + 57792, R0 + 66048, R0 + 90816, R0 + 115584
        x_res = Place(R0, R1)("x_res", [P, KD, T], F32)
        acc = Place(R1, R3)("acc", [P, KD, T], F32)
        pu = Place(R3, R4)
        u_hi, u_lo = pu("u_hi", [P, 2, T], F32R), pu("u_lo", [P, 2, T], F32R)
        sg2 = pu("sg2", [P, 2, T], F32)
        gate_f, u_f = sg2[:, 0, :], sg2[:, 1, :]
        PW = PARTS[0][1]
        pn = Place(R4, R5)
        norm_buf = [Place(R3, R4)("norm_buf0", [P, KD, PW], F32), pn("norm_buf1", [P, KD, PW], F32)]
        root, rinv = pn("root", [P, 2, PW], F32), pn("rinv", [P, 2, PW], F32)
        o_hi, z_f = Place(R0, R2)("o_hi", [P, 6, T], F32R), Place(R0 + 24768, R1)("z_f", [P, 2, T], F32)
        o_lo = Place(R4, R5)("o_lo", [P, 6, T], F32R)
        t1 = Place(R0, R1)
        q_hi, q_lo = t1("q_hi", [P, SEQ], F32R), t1("q_lo", [P, SEQ], F32R)
        k_hi, k_lo = t1("k_hi", [P, SEQ], F32R), t1("k_lo", [P, SEQ], F32R)
        vt_hi, vt_lo = t1("vt_hi", [P, NQ, P], F32R), t1("vt_lo", [P, NQ, P], F32R)
        prob = t1("prob", [P, 2, SEQ], F32)
        prob_b = prob[:, :, :].rearrange("p a (s c) -> p (a s) c", c=256)
        o_st = Place(R1, R2)("o_st", [P, 6, T], F32)
        t2 = Place(R2, R5)
        pt_hi, pt_lo = t2("pt_hi", [P, NQ, 256], F32R), t2("pt_lo", [P, NQ, 256], F32R)
        k_f, v_f = t2("k_f", [P, T], F32), t2("v_f", [P, T], F32)
        v_g = t2("v_g", [P, SEQ], F32)
        score_b = v_g[:, :].rearrange("p (s c) -> p s c", c=256)
        q_s = t2("q_s", [P, NB], F32)
        tok = t2("tok", [NB, 3, P], F32)
        R2b = t2.at
        ncum = t2("neg_cum", [P, SEQ], F32R)
        head_sel = t2("head_sel_r", [P, NHA, P], F32R)
        pair_sel = t2("pair_sel", [P, 2, P], F32R)
        lf_z, lf_a, lf_e = (t2(n, [NHA, T], F32) for n in ("lf_z", "lf_a", "lf_e"))
        cum, cum_one = lf_z[:, 0:SEQ], lf_e[:, 0:SEQ]
        t3 = Place(R2b, R5)
        o_g = t3("o_g", [P, 3, SEQ], F32)
        bias_t = t3("bias_t", [P, 2, 2, 256], F32)
        mx, nmx, den = (t3(n, [P, 3, 2, NQ], F32) for n in ("mx", "nmx", "den"))
        wide = t3("wide", [P, NQ, 2, HD], F32)
        wg = Place(R0, R1)("wg", [P, 3, SEQ], F32)
        mxall, tsum = k_f[:, 0:SEQ], v_f[:, 0:SEQ]
        bias_row = Place(R2b, R5)("bias_row", [P, 3 * HPG, LREL], F32)
        t5 = Place(R2, R5)
        kc_a, kc_b = t5("kc_a", [P, 2, NPAGE, WA], F32), t5("kc_b", [P, 2, 3, 256], F32)
        qb = t5("qb", [P, 2, WA + WB], F32)
        prod = t5("prod", [P, NPAGE * WA + WB], F32)
        kn, vn = t5("kn", [NB, WA + WB], F32), t5("vn", [NB, WA + WB], F32)
        prn = t5("prn", [NB, WA + WB], F32)
        lfp = t5("lfp", [P, NPAGE, NB, NHA], F32)
        s_a, s_b = t5("s_a", [P, NPAGE, NB, NHA], F32), t5("s_b", [P, 3, NB, HPG], F32)
        sn_a, sn_b = t5("sn_a", [NB, NB, NHA], F32), t5("sn_b", [NB, 3, NB, HPG], F32)
        p_a, p_b = t5("p_a", [P, NPAGE, NB, NHA], F32), t5("p_b", [P, 3, NB, HPG], F32)
        pn_a, pn_b = t5("pn_a", [NB, NB, NHA], F32), t5("pn_b", [NB, 3, NB, HPG], F32)
        t5b = Place(R0, R1)
        upto = t5b("upto_c", [P, P], F32)
        row_a, row_b = t5b("row_a", [64, 264], F32), t5b("row_b", [32, 408], F32)
        crow = t5b("crow", [64, 256], F32)
        cols = t5b("cols", [64, 8], F32)
        lf_new = t5b("lf_new", [64, 1], F32)
        own_a, own_b = t5b("own_a_c", [64, NB], F32), t5b("own_b_c", [32, NB], F32)
        pc = Place(R5, nc.sbuf_usable_end)
        ident, ones = pc("ident_c", [P, P], F32), pc("ones", [P, P], F32)
        causal_f = pc("causal_c", [P, P], F32)
        ident_b, causal_b = pc("ident_b", [P, P], BF16), pc("causal_b", [P, P], BF16)
        gains = pc("gains_c", [P, 6, KD], F32)
        eps_c, one_c, bf_c = pc("eps_c", [P, 1], F32), pc("one_c", [P, 1], F32), pc("b_f_c", [NHA, 1], F32)
        rb = pc("rel_bias_c", [N_BUCKETS + 1, 3 * HPG], F32)
        rbw = pc("rel_bias_wide", [N_BUCKETS + 1, P], F32)
        bs, bn = pc("bias_sample", [P, 3, HPG], F32), pc("bias_new", [NB, 3, HPG], F32)
        pages = pc("pages_c", [1, NB * NPAGE], I32)
        nmax, rowsum, rsum = pc("nmax", [P, 2], F32), pc("rowsum", [P, 2], F32), pc("rsum", [P, 2], F32)
        t6 = Place(R2, R2b)
        sel_p, sel_s, sel_n = t6("sel_prompt_c", [33, 3, LREL], F32), t6("sel_sample_c", [33, 3, P], F32), \
            t6("sel_new_c", [33, NB], F32)
        sel_stage = k_f[:, 0:NHA * P]

        ps = ctx.enter_context(nc.psum_tensor("ps", [P, 8, 512], F32))
        psf = ps[:, :, :].rearrange("p b c -> p (b c)")

        def bank(n, w=512):
            return ps[:, n, 0:w]

        x_spill = nc.dram_tensor("x_spill", [P, KD, T], F32).ap()
        bias_rows_t = nc.dram_tensor("bias_rows", [3 * HPG, P, LREL], F32)
        bias_rows = bias_rows_t.ap()
        qkv_s = nc.dram_tensor("qkv_s", [NB, 3, WA + WB], F32).ap()

        sem = {}

        def S(name):
            if name not in sem:
                sem[name] = ctx.enter_context(nc.semaphore(name))
            return sem[name]

        w_loaded = [S(f"w_loaded{n}") for n in range(RING)]
        w_hi_done, w_lo_done, mm_done = S("w_hi_done"), S("w_lo_done"), S("mm_done")
        u_f_done = S("u_f_done")
        freed = dict(act=S("banks_freed_by_act"), dve=S("banks_freed_by_dve"), u=u_f_done)
        const_in, x_in, misc_in = S("const_in"), S("x_in"), S("misc_in")

        def chunk_no(ph, c):
            return lambda s: FIRST_CHUNK[ph] + s * CHUNKS[ph] + c

        def act_split(act, ph, i, c, lo, hi):
            f = chunk_no(ph, c + 2)
            i0 = i if isinstance(i, int) else lo
            slot = f(i0) % RING
            if isinstance(i, int) and f(i) >= PLAN.chunks:
                return
            act.wait_ge(w_loaded[slot], lin(lambda s: 16 * (f(s) // RING + 1), i, lo, hi))
            if f(i0) >= RING:
                act.wait_ge(mm_done, lin(lambda s: 3 * PLAN.last_block[f(s) - RING] + 3, i, lo, hi))
            act.activation(w_hi[:, slot, :], w_raw[:, slot, :], ACT.Copy).then_inc(w_hi_done, 1)

        def dve_split(dve, ph, i, c, lo, hi):
            f = chunk_no(ph, c + 2)
            slot = f(i if isinstance(i, int) else lo) % RING
            if isinstance(i, int) and f(i) >= PLAN.chunks:
                return
            dve.wait_ge(w_hi_done, lin(lambda s: f(s) + 1, i, lo, hi))
            dve.tensor_tensor(w_lo[:, slot, :], w_raw[:, slot, :], w_hi[:, slot, :].bitcast(F32),
                              ALU.subtract).then_inc(w_lo_done, 1)

        def first_splits(eng, split):
            for c in (-2, -1):
                split(eng, "ffn1", 0, c, 0, 1)

        def pe_block(pe, ph, i, j, lo, hi, rhs_hi, rhs_lo, rhs_wait=None):
            c, off, width, k_tiles, _ = BLOCKS[ph][j]
            i0 = i if isinstance(i, int) else lo
            slot = PLAN.chunk_of[ph, i0, j] % RING
            hi_w = w_hi[:, slot, 0:k_tiles * width].rearrange("p (k c) -> p k c", c=width)
            lo_w = w_lo[:, slot, 0:k_tiles * width].rearrange("p (k c) -> p k c", c=width)
            pe.wait_ge(w_lo_done, lin(lambda s: PLAN.chunk_of[ph, s, j] + 1, i, lo, hi))
            for part, (s0, w) in enumerate(PARTS):
                if PLAN.before[ph, i0, j] is not None:
                    who = PLAN.free_of[PLAN.before[ph, i0, j]][0]
                    pe.wait_ge(freed[who], lin(lambda s: PLAN.free_of[PLAN.before[ph, s, j]][1] + part + 1,
                                               i, lo, hi))
                if rhs_wait:
                    rhs_wait(part)
                out = bank(3 * (j % 2) + part, w)
                for k in range(k_tiles):
                    for n, (a, b) in enumerate(((hi_w, rhs_hi), (hi_w, rhs_lo), (lo_w, rhs_hi))):
                        last = pe.matmul(out, a[:, k, off:off + P], b[:, k, s0:s0 + w],
                                         start=(k == 0 and n == 0), stop=(k == k_tiles - 1 and n == 2))
                last.then_inc(mm_done, 1)

        def product(eng, ph, i, j, part, lo, hi):
            eng.wait_ge(mm_done, lin(lambda s: 3 * PLAN.block_of[ph, s, j] + part + 1, i, lo, hi))
            return bank(3 * (j % 2) + part, PARTS[part][1])

        GROUPS = [[(0, 0), (0, 1), (0, 2)],
                  [(1, 0), (1, 1), (2, 0), (1, 2), (2, 1), (2, 2)],
                  [(3, 0), (3, 1), (4, 0), (3, 2), (4, 1), (4, 2)],
                  [(5, 0), (5, 1), (5, 2)]]
        EVENTS = [e for g in GROUPS for e in g]
        EV = {e: n for n, e in enumerate(EVENTS)}
        x_count = {e: n + 1 for n, e in enumerate(e for e in EVENTS if e[0] % 2)}
        h_count = {e: n + 1 for n, e in enumerate(e for e in EVENTS if e[0] % 2 == 0)}
        squares, sums, roots, normed_f, h_hi_done, x_done, h_ready, norm_step, x_back = (S(n) for n in (
            "squares", "sums", "roots", "normed_f", "h_hi_done", "x_done", "h_ready", "norm_step", "x_back"))
        AFTER = {1: "ffn1", 3: "merge", 5: "ffn2"}

        def act_square(act, e):
            t, part = e
            s0, w = PARTS[part]
            n = EV[e]
            if t == 0:
                act.wait_ge(x_in, 16)
            elif t % 2:
                ph = AFTER[t]
                last = (ph, ITERS[ph] - 1, len(BLOCKS[ph]) - 1)
                act.wait_ge(freed["dve"], PLAN.free_of[last][1] + part + 1)
                act.wait_ge(mm_done, 3 * PLAN.block_of[last] + 3)
            else:
                act.wait_ge(x_done, x_count[t - 1, part])
            if n >= 2:
                b = EVENTS[n - 2]
                act.wait_ge(x_done if b[0] % 2 else h_ready, (x_count if b[0] % 2 else h_count)[b])
            act.activation(norm_buf[n % 2][:, :, 0:w], (acc if t % 2 else x_res)[:, :, s0:s0 + w],
                           ACT.Square).then_inc(squares, 1)

        def act_norms(act, group):
            es = GROUPS[group]
            act_square(act, es[0])
            for a, e in enumerate(es):
                n, (s0, w) = EV[e], PARTS[e[1]]
                if a + 1 < len(es) and not (es[a + 1][0] % 2 == 0 and es[a + 1][0] > 0 and
                                            es[a + 1] == (e[0] + 1, e[1])):
                    act_square(act, es[a + 1])
                act.wait_ge(sums, n + 1)
                act.activation(root[:, n % 2, 0:w], bank(6 + n % 2, w), ACT.Sqrt, bias=eps_c[:, 0:1],
                               scale=1.0 / D).then_inc(roots, 1)
                if e[0] % 2 == 0:
                    act.wait_ge(normed_f, h_count[e])
                    act.activation(h_hi[:, :, s0:s0 + w], norm_buf[n % 2][:, :, 0:w],
                                   ACT.Copy).then_inc(h_hi_done, 1)

        def pe_norms(pe, group):
            for e in GROUPS[group]:
                n, w = EV[e], PARTS[e[1]][1]
                if n == 0:
                    pe.wait_ge(S("ones_set"), 3)
                pe.wait_ge(squares, n + 1)
                if n >= 2:
                    pe.wait_ge(roots, n - 1)
                for k in range(KD):
                    last = pe.matmul(bank(6 + n % 2, w), ones[:, :], norm_buf[n % 2][:, k, 0:w],
                                     start=(k == 0), stop=(k == KD - 1))
                last.then_inc(sums, 1)

        norm_steps = [0]

        def dve_norms(dve, group):
            for e in GROUPS[group]:
                t, part = e
                s0, w = PARTS[part]
                n = EV[e]
                buf = norm_buf[n % 2]
                src = acc if t % 2 else x_res
                dve.wait_ge(roots, n + 1)
                dve.reciprocal(rinv[:, n % 2, 0:w], root[:, n % 2, 0:w]).then_inc(norm_step, 1)
                norm_steps[0] += 1
                dve.wait_ge(norm_step, norm_steps[0])
                for k in range(KD):
                    last = dve.scalar_tensor_tensor(out=buf[:, k, 0:w], in0=src[:, k, s0:s0 + w],
                                                    scalar=gains[:, t, k:k + 1], in1=rinv[:, n % 2, 0:w],
                                                    op0=ALU.mult, op1=ALU.mult)
                if t % 2:
                    last.then_inc(norm_step, 1)
                    norm_steps[0] += 1
                    dve.wait_ge(norm_step, norm_steps[0])
                    if t == 3:
                        dve.wait_ge(x_back, 16)
                    dve.tensor_tensor(x_res[:, :, s0:s0 + w], x_res[:, :, s0:s0 + w], buf[:, :, 0:w],
                                      ALU.add).then_inc(x_done, 1)
                    dve.wait_ge(x_done, x_count[e])
                else:
                    last.then_inc(normed_f, 1)
                    dve.wait_ge(h_hi_done, h_count[e])
                    dve.tensor_tensor(h_lo[:, :, s0:s0 + w], buf[:, :, 0:w],
                                      h_hi[:, :, s0:s0 + w].bitcast(F32), ALU.subtract).then_inc(h_ready, 1)

        u_hi_done, u_lo_done = S("u_hi_done"), S("u_lo_done")
        U_STEP = dict(ffn1=0, merge=FFN_ITERS, ffn2=FFN_ITERS + MERGE_ITERS)

        def u_parts(ph, f, part):
            return lambda s: 3 * (2 * (U_STEP[ph] + s) + f) + part + 1

        def uf_parts(ph, f, part):
            return lambda s: 3 * (2 * ((0 if ph == "ffn1" else FFN_ITERS) + s) + f) + part + 1

        def pe_down(pe, ph, i, lo, hi, j0):
            for j in range(j0, j0 + 8):
                pe_block(pe, ph, i, j, lo, hi, u_hi, u_lo,
                         (lambda part: pe.wait_ge(u_lo_done, lin(u_parts(ph, 1, part), i, lo, hi)))
                         if j == j0 else None)

        def dve_down(dve, ph, i, lo, hi, first, j0, ms):
            for m in ms:
                for part, (s0, w) in enumerate(PARTS):
                    src = product(dve, ph, i, j0 + m, part, lo, hi)
                    dst = acc[:, m, s0:s0 + w]
                    if first:
                        dve.tensor_copy(dst, src).then_inc(freed["dve"], 1)
                    else:
                        dve.tensor_tensor(dst, dst, src, ALU.add).then_inc(freed["dve"], 1)

        def pe_ffn(pe, ph, i, lo, hi):
            if isinstance(i, int) and i == 0:
                pe.wait_ge(h_ready, h_count[(0 if ph == "ffn1" else 4), 2])
            for j in range(4):
                pe_block(pe, ph, i, j, lo, hi, h_hi, h_lo)
            pe_down(pe, ph, i, lo, hi, 4)

        def act_ffn(act, ph, i, lo, hi):
            for j in range(6):
                act_split(act, ph, i, j, lo, hi)
                f = j // 2
                if j in (0, 2):
                    for part, (s0, w) in enumerate(PARTS):
                        src = product(act, ph, i, j, part, lo, hi)
                        if ph != "ffn1" or f or not isinstance(i, int) or i:
                            act.wait_ge(u_f_done, lin(lambda s: uf_parts(ph, f, part)(s) - 3, i, lo, hi))
                        act.activation(gate_f[:, s0:s0 + w], src, ACT.Silu).then_inc(freed["act"], 1)
                if j in (1, 3):
                    for part, (s0, w) in enumerate(PARTS):
                        act.wait_ge(u_f_done, lin(uf_parts(ph, f, part), i, lo, hi))
                        act.activation(u_hi[:, f, s0:s0 + w], u_f[:, s0:s0 + w], ACT.Copy).then_inc(u_hi_done, 1)

        def dve_ffn(dve, ph, i, lo, hi, first):
            for j in range(6):
                dve_split(dve, ph, i, j, lo, hi)
                f = j // 2
                if j in (1, 3):
                    for part, (s0, w) in enumerate(PARTS):
                        src = product(dve, ph, i, j, part, lo, hi)
                        dve.wait_ge(freed["act"], lin(lambda s: PLAN.free_of[ph, s, j - 1][1] + part + 1, i, lo, hi))
                        if ph != "ffn1" or f or not isinstance(i, int) or i:
                            dve.wait_ge(u_lo_done, lin(lambda s: u_parts(ph, f, part)(s) - 3, i, lo, hi))
                        dve.tensor_tensor(u_f[:, s0:s0 + w], src, gate_f[:, s0:s0 + w],
                                          ALU.mult).then_inc(u_f_done, 1)
                    for part, (s0, w) in enumerate(PARTS):
                        dve.wait_ge(u_hi_done, lin(u_parts(ph, f, part), i, lo, hi))
                        dve.tensor_tensor(u_lo[:, f, s0:s0 + w], u_f[:, s0:s0 + w],
                                          u_hi[:, f, s0:s0 + w].bitcast(F32), ALU.subtract).then_inc(u_lo_done, 1)
                if j >= 4:
                    dve_down(dve, ph, i, lo, hi, first, 4, range(4 * (j - 4), 4 * (j - 3)))

        def steps(eng, n, body, last_apart=False):
            body(0, 0, 1, True)
            end = n - 1 if last_apart else n
            with eng.Fori(1, end) as i:
                body(i, 1, end, False)
            if last_apart:
                body(n - 1, n - 1, n, False)

        bias_mm, bias_ev, bias_out = S("bias_mm"), S("bias_ev"), S("bias_out")
        sel_in, hsel_in = S("sel_in"), S("hsel_in")

        def pe_bias(pe):
            pe.wait_ge(sel_in, 48)
            for h in range(3 * HPG):
                pe.wait_ge(S("rbw_set"), h + 1)
                if h >= 2:
                    pe.wait_ge(bias_ev, h - 1)
                pe.matmul(bank(6 + h % 2, LREL), rbw[:, :], sel_p[:, h // HPG, :],
                          start=True, stop=True).then_inc(bias_mm, 1)
            pe.wait_ge(bias_ev, 3 * HPG)
            for g in range(3):
                pe.matmul(ps[:, 6, g * HPG:(g + 1) * HPG], sel_s[:, g, :], rb[:, g * HPG:(g + 1) * HPG],
                          start=True, stop=True)
            pe.matmul(ps[0:NB, 6, 16:28], sel_n[:, :], rb[:, :], start=True, stop=True).then_inc(bias_mm, 1)

        def dve_bias(dve):
            dve.wait_ge(sel_in, 48)
            dve.wait_ge(h_ready, 6)
            for h in range(3 * HPG):
                if h:
                    dve.wait_ge(bias_mm, h)
                dve.tensor_copy(rbw[:, :], rb[:, h:h + 1].broadcast_to([N_BUCKETS + 1, P])).then_inc(S("rbw_set"), 1)
                dve.wait_ge(bias_mm, h + 1)
                dve.tensor_copy(bias_row[:, h, :], bank(6 + h % 2, LREL)).then_inc(bias_ev, 1)
            dve.wait_ge(bias_mm, 3 * HPG + 1)
            dve.tensor_copy(bs[:, :, :], ps[:, 6, 0:12].rearrange("p (g h) -> p g h", h=HPG)).then_inc(bias_ev, 1)
            dve.tensor_copy(bn[:, :, :], ps[0:NB, 6, 16:28].rearrange("p (g h) -> p g h", h=HPG)).then_inc(bias_ev, 1)

        z_done, az_done, ez_done, l1_done, lf_done, cum_done, nc_hi, nc_done = (S(n) for n in (
            "z_done", "az_done", "ez_done", "l1_done", "lf_done", "cum_done", "nc_hi", "nc_done"))
        sel_r_done, ncum_zero = S("sel_r_done"), S("ncum_zero")

        def act_forget(act):
            act_split(act, "forget", 0, 0, 0, 1)
            act.wait_ge(bias_out, 16)
            for part, (s0, w) in enumerate(PARTS):
                src = product(act, "forget", 0, 0, part, 0, 1)
                act.activation(lf_z[:, s0:s0 + w], src[0:NHA, :], ACT.Identity,
                               bias=bf_c[:, 0:1]).then_inc(freed["act"], 1)
            act.wait_ge(hsel_in, 16)
            act.activation(head_sel[:, :, :], sel_stage.rearrange("p (h c) -> p h c", c=P),
                           ACT.Copy).then_inc(sel_r_done, 1)
            act.wait_ge(az_done, 1)
            act.activation(lf_e[:, :], lf_a[:, :], ACT.Exp, scale=-1.0).then_inc(ez_done, 1)
            act.wait_ge(ez_done, 1)
            act.activation(lf_a[:, :], lf_e[:, :], ACT.Ln, bias=one_c[0:NHA, 0:1]).then_inc(l1_done, 1)
            act.wait_ge(cum_done, 1)
            act.wait_ge(ncum_zero, 1)
            act.activation(ncum[0:NHA, :], cum, ACT.Copy, scale=-1.0).then_inc(nc_hi, 1)

        def dve_forget(dve):
            dve_split(dve, "forget", 0, 0, 0, 1)
            dve.wait_ge(bias_out, 16)
            dve.memset(ncum[:, :].bitcast(F32), 0.0).then_inc(ncum_zero, 1)
            dve.wait_ge(freed["act"], PLAN.free_of["forget", 0, 0][1] + 3)
            dve.scalar_tensor_tensor(out=lf_a[:, :], in0=lf_z[:, :], scalar=-1.0, in1=lf_z[:, :],
                                     op0=ALU.mult, op1=ALU.max).then_inc(az_done, 1)
            dve.wait_ge(l1_done, 1)
            dve.scalar_tensor_tensor(out=lf_a[:, :], in0=lf_z[:, :], scalar=0.0, in1=lf_a[:, :],
                                     op0=ALU.min, op1=ALU.subtract).then_inc(lf_done, 1)
            dve.memset(cum_one, 1.0).then_inc(lf_done, 1)
            dve.wait_ge(lf_done, 2)
            dve.tensor_tensor_scan(cum, cum_one, lf_a[:, 0:SEQ], 0.0, ALU.mult, ALU.add).then_inc(cum_done, 1)
            dve.wait_ge(nc_hi, 1)
            dve.scalar_tensor_tensor(out=ncum[32:32 + NHA, :], in0=cum, scalar=-1.0,
                                     in1=ncum[0:NHA, :].bitcast(F32), op0=ALU.mult,
                                     op1=ALU.subtract).then_inc(nc_done, 1)

        k_out, v_out, kf_done, vf_done, qs_done, vt_mm, vt_hi_done, vt_lo_done = (S(n) for n in (
            "k_out", "v_out", "kf_done", "vf_done", "qs_done", "vt_mm", "vt_hi_done", "vt_lo_done"))
        qk_hi, tok_mm, tok_done, tok_out, combined = (S(n) for n in (
            "qk_hi", "tok_mm", "tok_done", "tok_out", "combined"))
        FIRST_A = dict(fox=0, dil=PAIRS_A)

        def grouped(ap, dil, s0, w):
            return ap.rearrange("p (r a) -> p a r", r=dil)[:, s0 // dil:(s0 + w) // dil, :]

        def in_tokens(ap, dil):
            return ap.rearrange("p (a r) -> p a r", r=dil)

        def act_qkv(act, ph, i, lo, hi, dil):
            A0 = FIRST_A[ph]
            plain = isinstance(i, int)
            a0 = A0 + (i if plain else lo)
            for j in range(3):
                act_split(act, ph, i, j, lo, hi)
                if j == 0 and a0 == PAIRS_A + 3:
                    act.wait_ge(combined, 1)
                if j == 1 and a0 > 0:
                    act.wait_ge(k_out, lin(lambda s: 16 * (A0 + s), i, lo, hi))
                    act.wait_ge(v_out, lin(lambda s: 16 * (A0 + s), i, lo, hi))
                    act.wait_ge(tok_mm, lin(lambda s: A0 + s, i, lo, hi))
                for part, (s0, w) in enumerate(PARTS):
                    src = product(act, ph, i, j, part, lo, hi)
                    pw = min(w, SEQ - s0)
                    if j == 0:
                        if part == 2:
                            act.activation(q_s[:, :], src[:, pw:w], ACT.Copy, scale=SCALE).then_inc(qs_done, 1)
                        act.activation(grouped(q_hi[:, :], dil, s0, pw), in_tokens(src[:, 0:pw], dil), ACT.Copy,
                                       scale=SCALE).then_inc(qk_hi, 1)
                    if j == 1:
                        act.activation(k_f[:, s0:s0 + w], src, ACT.Copy).then_inc(kf_done, 1)
                        act.activation(grouped(k_hi[:, :], dil, s0, pw), in_tokens(src[:, 0:pw], dil),
                                       ACT.Copy).then_inc(qk_hi, 1)
                    if j == 2:
                        act.activation(v_f[:, s0:s0 + w], src, ACT.Copy).then_inc(vf_done, 1)
                        act.activation(grouped(v_g[:, :], dil, s0, pw), in_tokens(src[:, 0:pw], dil),
                                       ACT.Copy).then_inc(freed["act"], 1)
            act.wait_ge(tok_mm, lin(lambda s: A0 + s + 1, i, lo, hi))
            if a0 > 0:
                act.wait_ge(tok_out, lin(lambda s: 16 * (A0 + s), i, lo, hi))
            act.activation(tok[:, :, :], ps[0:NB, 5, 0:3 * P].rearrange("p (c f) -> p c f", c=3),
                           ACT.Copy).then_inc(tok_done, 1)
            for n in range(2):
                act.wait_ge(vt_mm, lin(lambda s: 2 * (A0 + s) + n + 1, i, lo, hi))
                act.activation(vt_hi[:, 4 * n:4 * n + 4, :], bank(6 + n).rearrange("p (n c) -> p n c", c=P),
                               ACT.Copy).then_inc(vt_hi_done, 1)

        def dve_qkv(dve, ph, i, lo, hi, dil):
            A0 = FIRST_A[ph]
            for j in range(3):
                dve_split(dve, ph, i, j, lo, hi)
                for part, (s0, w) in enumerate(PARTS):
                    pw = min(w, SEQ - s0)
                    if j < 2:
                        src = product(dve, ph, i, j, part, lo, hi)
                        dve.wait_ge(qk_hi, lin(lambda s: 6 * (A0 + s) + 3 * j + part + 1, i, lo, hi))
                    if j == 0:
                        dve.scalar_tensor_tensor(out=grouped(q_lo[:, :], dil, s0, pw),
                                                 in0=in_tokens(src[:, 0:pw], dil), scalar=SCALE,
                                                 in1=grouped(q_hi[:, :].bitcast(F32), dil, s0, pw),
                                                 op0=ALU.mult, op1=ALU.subtract).then_inc(freed["dve"], 1)
                    if j == 1:
                        dve.tensor_tensor(grouped(k_lo[:, :], dil, s0, pw), in_tokens(src[:, 0:pw], dil),
                                          grouped(k_hi[:, :].bitcast(F32), dil, s0, pw),
                                          ALU.subtract).then_inc(freed["dve"], 1)
            for n in range(2):
                dve.wait_ge(vt_hi_done, lin(lambda s: 2 * (A0 + s) + n + 1, i, lo, hi))
                dve.tensor_tensor(vt_lo[:, 4 * n:4 * n + 4, :], bank(6 + n).rearrange("p (n c) -> p n c", c=P),
                                  vt_hi[:, 4 * n:4 * n + 4, :].bitcast(F32), ALU.subtract).then_inc(vt_lo_done, 1)

        def pe_qkv(pe, ph, i, lo, hi):
            A0 = FIRST_A[ph]
            for j in range(3):
                pe_block(pe, ph, i, j, lo, hi, h_hi, h_lo)
            pe.wait_ge(freed["dve"], lin(lambda s: PLAN.free_of[ph, s, 1][1] + 3, i, lo, hi))
            pe.wait_ge(freed["act"], lin(lambda s: PLAN.free_of[ph, s, 2][1] + 3, i, lo, hi))
            for n, src in enumerate((q_s[:, :], k_f[:, SEQ:T], v_f[:, SEQ:T])):
                last = pe.transpose(ps[0:NB, 5, n * P:(n + 1) * P], src, ident[:, :])
            last.then_inc(tok_mm, 1)
            for n in range(NQ):
                last = pe.transpose(ps[:, 6 + n // 4, (n % 4) * P:(n % 4 + 1) * P], v_g[:, n * P:(n + 1) * P],
                                    ident[:, :])
                if n % 4 == 3:
                    last.then_inc(vt_mm, 1)
            pe.wait_ge(vt_lo_done, lin(lambda s: 2 * (A0 + s) + 2, i, lo, hi))
            pe.wait_ge(tok_done, lin(lambda s: A0 + s + 1, i, lo, hi))

        sc_done, mx_done, ex_done, rs_done, nr_done, tr_done, pth_done, ptl_done, ov_done, oev_done, psel_done = (
            S("fox_" + n) for n in ("scores", "max", "exp", "rsum", "normed", "turned", "pt_hi", "pt_lo", "ov",
                                    "ov_read", "pair_sel"))
        TILES = [(hh, i) for hh in range(2) for i in range(NQ)]
        TURNS = [(s, half) for s, (_, i) in enumerate(TILES) for half in range(1 + (i >= 4))]
        TURN_NO = {t: n for n, t in enumerate(TURNS)}
        N_TILE, N_TURN, N_OV = len(TILES), len(TURNS), 8

        def turns_of(s):
            return [(n, half) for n, (s_, half) in enumerate(TURNS) if s_ == s]

        def pe_fox(pe, p, lo, hi):
            def scores(s):
                hh, i = TILES[s]
                rows, n = slice(HD * hh, HD * hh + HD), P * (i + 1)
                if s >= 2:
                    pe.wait_ge(ex_done, lin(lambda x: N_TILE * x + s - 1, p, lo, hi))
                for c0 in range(0, n, 512):
                    c1 = min(c0 + 512, n)
                    out = ps[:, 2 * (s % 2) + c0 // 512, 0:c1 - c0]
                    qs = slice(i * P, (i + 1) * P)
                    pe.matmul(out, q_hi[rows, qs], k_hi[rows, c0:c1], start=True, stop=False)
                    pe.matmul(out, q_hi[rows, qs], k_lo[rows, c0:c1], start=False, stop=False)
                    pe.matmul(out, q_lo[rows, qs], k_hi[rows, c0:c1], start=False, stop=False)
                    if c1 == n:
                        pe.matmul(out[:, c1 - c0 - P:c1 - c0], ident_b[:, :], causal_b[:, :],
                                  start=False, stop=False, skip_group_check=True)
                    last = pe.matmul(out, pair_sel[:, hh, :], ncum[:, c0:c1], start=False, stop=True)
                last.then_inc(sc_done, 1)

            def turn(s):
                hh, i = TILES[s]
                pe.wait_ge(nr_done, lin(lambda x: N_TILE * x + s + 1, p, lo, hi))
                for e, half in turns_of(s):
                    if e >= 2:
                        pe.wait_ge(ptl_done, lin(lambda x: N_TURN * x + e - 1, p, lo, hi))
                    for n in range(4 * half, min(4 * half + 4, i + 1)):
                        last = pe.transpose(ps[:, 4 + e % 2, (n % 4) * P:(n % 4 + 1) * P],
                                            prob[:, s % 2, n * P:(n + 1) * P], ident[:, :])
                    last.then_inc(tr_done, 1)

            def values(s):
                hh, i = TILES[s]
                b = 4 * hh + i // 2
                pe.wait_ge(ptl_done, lin(lambda x: N_TURN * x + turns_of(s)[-1][0] + 1, p, lo, hi))
                if b >= 2:
                    pe.wait_ge(oev_done, lin(lambda x: N_OV * x + b - 1, p, lo, hi))
                for j in range(i + 1):
                    c0 = P if j == i else 0
                    out = ps[:, 6 + b % 2, c0:256]
                    for n, (v, t) in enumerate(((vt_hi, pt_hi), (vt_hi, pt_lo), (vt_lo, pt_hi))):
                        last = pe.matmul(out, v[:, j, :], t[:, j, c0:256], start=(j == 0 and n == 0),
                                         stop=(j == i and n == 2), skip_group_check=True)
                last.then_inc(ov_done, 1)

            pe.wait_ge(psel_done, lin(lambda x: x + 1, p, lo, hi))
            pe.wait_ge(nc_done, 1)
            scores(0)
            for s in range(N_TILE):
                if s + 1 < N_TILE:
                    scores(s + 1)
                turn(s)
                if TILES[s][1] % 2:
                    values(s)
            pe.wait_ge(oev_done, lin(lambda x: N_OV * x + N_OV, p, lo, hi))

        def act_fox(act, p, lo, hi):
            def exp(s):
                n = P * (TILES[s][1] + 1)
                act.wait_ge(mx_done, lin(lambda x: N_TILE * x + s + 1, p, lo, hi))
                act.activation(prob[:, s % 2, 0:n], psf[:, 1024 * (s % 2):1024 * (s % 2) + n], ACT.Exp,
                               bias=nmax[:, s % 2:s % 2 + 1],
                               accum_out=rowsum[:, s % 2:s % 2 + 1]).then_inc(ex_done, 1)

            def out(s):
                hh, i = TILES[s]
                b = 4 * hh + i // 2
                rows = slice(HD * hh, HD * hh + HD)
                act.wait_ge(ov_done, lin(lambda x: N_OV * x + b + 1, p, lo, hi))
                dst = o_st[rows, p, P * (i - 1):P * (i + 1)] if isinstance(p, int) else \
                    o_st[rows, bass.ds(p, 1), P * (i - 1):P * (i + 1)].rearrange("p a c -> p (a c)")
                act.activation(dst, ps[rows, 6 + b % 2, 0:256], ACT.Copy).then_inc(oev_done, 1)

            sel = head_sel[:, 2 * p:2 * p + 2, :] if isinstance(p, int) else head_sel[:, bass.ds(2 * p, 2), :]
            act.activation(pair_sel[:, :, :], sel.bitcast(F32), ACT.Copy).then_inc(psel_done, 1)
            exp(0)
            for s in range(N_TILE):
                if s + 1 < N_TILE:
                    if s >= 1:
                        act.wait_ge(tr_done, lin(lambda x: N_TURN * x + turns_of(s - 1)[-1][0] + 1, p, lo, hi))
                    exp(s + 1)
                if s >= 1 and TILES[s - 1][1] % 2:
                    out(s - 1)
                i = TILES[s][1]
                for e, half in turns_of(s):
                    nb = min(4, i + 1 - 4 * half)
                    act.wait_ge(tr_done, lin(lambda x: N_TURN * x + e + 1, p, lo, hi))
                    act.activation(pt_hi[:, 4 * half:4 * half + nb, (i % 2) * P:(i % 2 + 1) * P],
                                   bank(4 + e % 2, nb * P).rearrange("p (n c) -> p n c", c=P),
                                   ACT.Copy).then_inc(pth_done, 1)
            out(N_TILE - 1)

        def dve_fox(dve, p, lo, hi):
            def biggest(s):
                n = P * (TILES[s][1] + 1)
                dve.wait_ge(sc_done, lin(lambda x: N_TILE * x + s + 1, p, lo, hi))
                dve.tensor_reduce(nmax[:, s % 2:s % 2 + 1], psf[:, 1024 * (s % 2):1024 * (s % 2) + n], AX.X,
                                  ALU.max, negate=True).then_inc(mx_done, 1)

            biggest(0)
            for s in range(N_TILE):
                if s + 1 < N_TILE:
                    biggest(s + 1)
                i = TILES[s][1]
                n = P * (i + 1)
                c = slice(s % 2, s % 2 + 1)
                dve.wait_ge(ex_done, lin(lambda x: N_TILE * x + s + 1, p, lo, hi))
                dve.reciprocal(rsum[:, c], rowsum[:, c]).then_inc(rs_done, 1)
                dve.wait_ge(rs_done, lin(lambda x: N_TILE * x + s + 1, p, lo, hi))
                dve.tensor_scalar(prob[:, s % 2, 0:n], prob[:, s % 2, 0:n], rsum[:, c], None,
                                  ALU.mult).then_inc(nr_done, 1)
                for e, half in turns_of(s):
                    nb = min(4, i + 1 - 4 * half)
                    sl = (slice(None), slice(4 * half, 4 * half + nb), slice((i % 2) * P, (i % 2 + 1) * P))
                    dve.wait_ge(pth_done, lin(lambda x: N_TURN * x + e + 1, p, lo, hi))
                    dve.tensor_tensor(pt_lo[sl], bank(4 + e % 2, nb * P).rearrange("p (n c) -> p n c", c=P),
                                      pt_hi[sl].bitcast(F32), ALU.subtract).then_inc(ptl_done, 1)

        d_sc, d_mt, d_mx, d_ex, d_tr, d_pth, d_ptl, d_ov, d_oev, bias_in = (S("dil_" + n) for n in (
            "scores", "biased", "max", "exp", "turned", "pt_hi", "pt_lo", "ov", "ov_read", "bias"))

        def has_prev(g, n):
            per = SEQ // DIL[g] // P
            return per > 0 and n % per != 0

        def pe_dil(pe, d, g):
            def scores(s):
                hh, n = s // NQ, s % NQ
                rows = slice(HD * hh, HD * hh + HD)
                if s >= 4:
                    pe.wait_ge(d_mt, 16 * d + s - 3)
                k0, c0 = ((n - 1) * P, 0) if has_prev(g, n) else (n * P, P)
                out = ps[:, s % 4, c0:256]
                for m, (a, b) in enumerate(((q_hi, k_hi), (q_hi, k_lo), (q_lo, k_hi))):
                    last = pe.matmul(out, a[rows, n * P:(n + 1) * P], b[rows, k0:(n + 1) * P],
                                     start=(m == 0), stop=(m == 2))
                last.then_inc(d_sc, 1)

            def turn(s):
                n = s % NQ
                pe.wait_ge(d_ex, 16 * d + s + 1)
                if s >= 2:
                    pe.wait_ge(d_ptl, 16 * d + s - 1)
                for c0 in ((0, P) if has_prev(g, n) else (P,)):
                    last = pe.transpose(ps[:, 4 + s % 2, c0:c0 + P], prob_b[:, s % 4, c0:c0 + P], ident[:, :])
                last.then_inc(d_tr, 1)

            def values(hh):
                pe.wait_ge(d_ptl, 16 * d + NQ * (hh + 1))
                if hh:
                    pe.wait_ge(d_oev, 2 * d + hh)
                begun = set()
                for j in range(NQ):
                    end = j + 1 + (j + 1 < NQ and has_prev(g, j + 1))
                    for b0, b1 in ([(j, end)] if j // 4 == (end - 1) // 4 else [(j, j + 1), (j + 1, end)]):
                        out = ps[:, 6 + b0 // 4, (b0 % 4) * P:(b0 % 4) * P + (b1 - b0) * P]
                        cs = slice((b0 - j) * P, (b1 - j) * P)
                        for v, t in ((vt_hi, pt_hi), (vt_hi, pt_lo), (vt_lo, pt_hi)):
                            last = pe.matmul(out, v[:, j, :], t[:, j, cs], start=(b0 // 4 not in begun),
                                             stop=True, skip_group_check=True)
                            begun.add(b0 // 4)
                last.then_inc(d_ov, 1)

            for s in range(3):
                scores(s)
            for s in range(16):
                if s + 3 < 16:
                    scores(s + 3)
                turn(s)
                if s % NQ == NQ - 1:
                    values(s // NQ)
            pe.wait_ge(d_oev, 2 * d + 2)

        def act_dil(act, d, g):
            def exp(s):
                hh, n = s // NQ, s % NQ
                c0 = 0 if has_prev(g, n) else P
                act.wait_ge(d_mx, 16 * d + s + 1)
                if s >= 4:
                    act.wait_ge(d_tr, 16 * d + s - 3)
                act.activation(prob_b[:, s % 4, c0:256], score_b[:, s % 4, c0:256], ACT.Exp,
                               bias=nmx[:, g, hh, n:n + 1], accum_out=den[:, g, hh, n:n + 1]).then_inc(d_ex, 1)

            def out(hh):
                rows = slice(HD * hh, HD * hh + HD)
                act.wait_ge(d_ov, 2 * d + hh + 1)
                act.activation(o_g[rows, g, :], psf[rows, 6 * 512:8 * 512], ACT.Copy).then_inc(d_oev, 1)

            ptf = pt_hi[:, :, :].rearrange("p n c -> p (n c)")
            exp(0)
            for s in range(16):
                if s + 1 < 16:
                    exp(s + 1)
                n = s % NQ
                if s == NQ:
                    out(0)
                w = 256 if has_prev(g, n) else P
                act.wait_ge(d_tr, 16 * d + s + 1)
                act.activation(ptf[:, n * 256 + P - w:n * 256 + P], ps[:, 4 + s % 2, 256 - w:256],
                               ACT.Copy).then_inc(d_pth, 1)
            out(1)

        def dve_dil(dve, d, g):
            def biased(s):
                hh, n = s // NQ, s % NQ
                c0 = 0 if has_prev(g, n) else P
                if s == 0:
                    dve.wait_ge(S(f"bias_dma{d % 2}"), 32 * (d // 2 + 1))
                    if g == 2:
                        dve.wait_ge(bias_in, d // 3 + 1)
                dve.wait_ge(d_sc, 16 * d + s + 1)
                if s >= 4:
                    dve.wait_ge(d_ex, 16 * d + s - 3)
                dve.tensor_tensor_reduce(score_b[:, s % 4, c0:256], ps[:, s % 4, c0:256],
                                         bias_t[:, d % 2, hh, c0:256], 1.0, -3.0e38, ALU.add, ALU.max,
                                         mx[:, g, hh, n:n + 1]).then_inc(d_mt, 1)
                dve.wait_ge(d_mt, 16 * d + s + 1)
                dve.tensor_scalar(nmx[:, g, hh, n:n + 1], mx[:, g, hh, n:n + 1], -1.0, None,
                                  ALU.mult).then_inc(d_mx, 1)

            lof = pt_lo[:, :, :].rearrange("p n c -> p (n c)")
            hif = pt_hi[:, :, :].rearrange("p n c -> p (n c)").bitcast(F32)
            biased(0)
            biased(1)
            for s in range(16):
                if s + 2 < 16:
                    biased(s + 2)
                n = s % NQ
                w = 256 if has_prev(g, n) else P
                sl = slice(n * 256 + P - w, n * 256 + P)
                dve.wait_ge(d_pth, 16 * d + s + 1)
                dve.tensor_tensor(lof[:, sl], ps[:, 4 + s % 2, 256 - w:256], hif[:, sl],
                                  ALU.subtract).then_inc(d_ptl, 1)

        wide_set, wide_mm, m_ev, w_sub, w_exp, cb_step = (S("cb_" + n) for n in (
            "wide", "spread", "max_ev", "sub", "exp", "step"))

        def pe_combine(pe, pair):
            for kind in range(2):
                for g in range(3):
                    pe.wait_ge(wide_set, 6 * pair + 3 * kind + g + 1)
                    if kind:
                        pe.wait_ge(m_ev, 3 * pair + g + 1)
                    for n in range(NQ):
                        last = pe.matmul(ps[:, 2 * g + n // 4, (n % 4) * P:(n % 4 + 1) * P],
                                         wide[:, n, :, :].rearrange("p h d -> p (h d)"), ident[:, :],
                                         start=True, stop=True)
                    last.then_inc(wide_mm, 1)
            pe.wait_ge(combined, pair + 1)

        def group_view(g, ap):
            return ap.rearrange("p (r a) -> p a r", r=DIL[g])

        def act_combine(act, pair):
            for g in range(3):
                act.wait_ge(wide_mm, 6 * pair + g + 1)
                act.activation(in_tokens(wg[:, g, :], DIL[g]), group_view(g, psf[:, 1024 * g:1024 * (g + 1)]),
                               ACT.Copy).then_inc(m_ev, 1)
            act.wait_ge(w_sub, pair + 1)
            act.activation(wg[:, :, :], wg[:, :, :], ACT.Exp).then_inc(w_exp, 1)

        def dve_combine(dve, pair):
            cnt = [13 * pair]

            def link(ins):
                cnt[0] += 1
                ins.then_inc(cb_step, 1)
                dve.wait_ge(cb_step, cnt[0])

            dve.wait_ge(d_ex, 16 * 3 * (pair + 1))
            for kind, src in enumerate((mx, den)):
                for g in range(3):
                    if kind + g:
                        dve.wait_ge(wide_mm, 6 * pair + 3 * kind + g)
                    dve.tensor_copy(wide[:, :, :, :], src[:, g, :, :].rearrange("p h n -> p n h").unsqueeze(3)
                                    .broadcast_to([P, NQ, 2, HD])).then_inc(wide_set, 1)
                if kind == 0:
                    dve.wait_ge(m_ev, 3 * pair + 3)
                    dve.wait_ge(k_out, 16 * (PAIRS_A + 3 * pair + 3))
                    dve.wait_ge(v_out, 16 * (PAIRS_A + 3 * pair + 3))
                    link(dve.tensor_tensor(mxall, wg[:, 0, :], wg[:, 1, :], ALU.max))
                    link(dve.tensor_tensor(mxall, mxall, wg[:, 2, :], ALU.max))
                    dve.tensor_tensor(wg[:, :, :], wg[:, :, :], mxall.unsqueeze(1).broadcast_to([P, 3, SEQ]),
                                      ALU.subtract).then_inc(w_sub, 1)
                    dve.wait_ge(w_sub, pair + 1)
            dve.wait_ge(w_exp, pair + 1)
            for g in range(3):
                dve.wait_ge(wide_mm, 6 * pair + 4 + g)
                dst = mxall if g else tsum
                link(dve.tensor_tensor(in_tokens(dst, DIL[g]), in_tokens(wg[:, g, :], DIL[g]),
                                       group_view(g, psf[:, 1024 * g:1024 * (g + 1)]), ALU.mult))
                if g:
                    link(dve.tensor_tensor(tsum, tsum, mxall, ALU.add))
            link(dve.reciprocal(tsum, tsum))
            link(dve.tensor_tensor(wg[:, :, :], wg[:, :, :], tsum.unsqueeze(1).broadcast_to([P, 3, SEQ]), ALU.mult))
            dve.wait_ge(d_oev, 2 * 3 * (pair + 1))
            for g in range(3):
                link(dve.tensor_tensor(in_tokens(wg[:, g, :], DIL[g]), in_tokens(wg[:, g, :], DIL[g]),
                                       group_view(g, o_g[:, g, :]), ALU.mult))
            link(dve.tensor_tensor(wg[:, 0, :], wg[:, 0, :], wg[:, 1, :], ALU.add))
            dve.tensor_tensor(o_st[:, PAIRS_A + pair, 0:SEQ], wg[:, 0, :], wg[:, 2, :], ALU.add)\
                .then_inc(combined, 1)

        kc_in = [S("kc_in0"), S("kc_in1")]
        kc_used, kc_zero, s_in, s_dot, s_step, s_rows, s_mm, s_ev, p_ready, v_mul, v_mm, s_out = (S("smp_" + n) for n in (
            "kc_used", "kc_zero", "in", "dot", "step", "rows", "mm", "ev", "p_ready", "v_mul", "v_mm", "out"))
        lf_out = S("lf_out")
        A_LAST = PAIRS_A + 3 * PAIRS_B

        def pool_cache(pool, kv):
            def load(b, slot, used):
                if used is not None:
                    pool.wait_ge(kc_used, used)
                if isinstance(b, int):
                    bsl = lambda t: t[b:b + 1]
                else:
                    bsl = lambda t: t[bass.ds(b, 1)]
                src = A["cache_a_v"] if kv else A["cache_a_k"]
                for pg in range(NPAGE):
                    page = pool.value_load(pages[0:1, bass.ds(b * NPAGE + pg, 1)] if not isinstance(b, int) else
                                           pages[0:1, b * NPAGE + pg:b * NPAGE + pg + 1],
                                           min_val=0, max_val=A["cache_a_k"].shape[0] - 1)
                    pool.dma_start(kc_a[:, slot, pg, :], src[bass.ds(page, 1)].rearrange("a p c -> (a p) c")
                                   ).then_inc(kc_in[slot], 16)
                    if not kv:
                        dst = lfp[:, pg, b, :] if isinstance(b, int) else \
                            lfp[:, pg, bass.ds(b, 1), :].rearrange("p a c -> p (a c)")
                        pool.dma_start(dst, A["cache_a_logf"][bass.ds(page, 1)].rearrange("a p c -> (a p) c")
                                       ).then_inc(kc_in[slot], 16)
                for g, (name, n) in enumerate(zip(("b1", "b2", "b3"), SAMPLE_KEYS)):
                    cache = A["cache_" + name]
                    step = cache.shape[1] // n
                    one = bsl(cache).rearrange("a (n s) c -> (a n) s c", s=step)[:, 0, kv * 256:(kv + 1) * 256]
                    pool.dma_start(kc_b[0:n, slot, g, :], one).then_inc(kc_in[slot], 16)
                if not kv:
                    pool.dma_start(qb[:, slot, :], bsl(qkv_s)[:, 0, :].broadcast_to([P, WA + WB])
                                   ).then_inc(kc_in[slot], 16)
            for b in range(NB):
                load(b, b % 2, NB * kv + b - 1 if NB * kv + b >= 2 else None)

        def pool_samples(pool):
            pool.wait_ge(tok_out, 16 * A_LAST)
            pool.wait_ge(lf_out, 16)
            pool.wait_ge(combined, PAIRS_B)
            pool.wait_ge(tok_done, A_LAST)
            pool.dma_start(kn[:, :], qkv_s[:, 1, :]).then_inc(s_in, 16)
            pool.dma_start(vn[:, :], qkv_s[:, 2, :]).then_inc(s_in, 16)
            pool.dma_start(lf_new[:, :], A["lf_t"][:, SEQ:T].rearrange("h b -> b h").unsqueeze(2),
                           allow_slow_non_contiguous=True).then_inc(s_in, 16)
            pool.dma_start(upto[:, :], A["upto"]).then_inc(s_in, 16)
            pool.dma_start(own_a[:, :], A["own_a"]).then_inc(s_in, 16)
            pool.dma_start(own_b[:, :], A["own_b"]).then_inc(s_in, 16)
            pool.memset(kc_b[:, :, :, :], 0.0).then_inc(kc_zero, 1)
            pool.wait_ge(kc_zero, 1)
            pool_cache(pool, 0)
            pool_cache(pool, 1)

        K_IN, V_IN = 16 * (2 * NPAGE + 3 + 1), 16 * (NPAGE + 3)

        def dve_samples(dve):
            cnt = [0]
            dve.wait_ge(s_in, 96)

            def dot(b, slot, i):
                dve.wait_ge(kc_in[slot], i * K_IN + K_IN)
                s3 = (lambda t, n: t[:, :, b, :]) if isinstance(b, int) else \
                    (lambda t, n: t[:, :, bass.ds(b, 1), :].rearrange("p g a h -> p g (a h)"))
                s2 = (lambda t: t[:, b, :]) if isinstance(b, int) else \
                    (lambda t: t[:, bass.ds(b, 1), :].rearrange("p a h -> p (a h)"))
                dve.tensor_tensor(prod[:, 0:NPAGE * WA].rearrange("p (g c) -> p g c", c=WA), kc_a[:, slot, :, :],
                                  qb[:, slot, 0:WA].unsqueeze(1).broadcast_to([P, NPAGE, WA]), ALU.mult)
                dve.tensor_tensor(prod[:, NPAGE * WA:NPAGE * WA + WB],
                                  kc_b[:, slot, :, :].rearrange("p g c -> p (g c)"), qb[:, slot, WA:WA + WB], ALU.mult)
                dve.tensor_tensor(prn[:, :], kn[:, :], qb[0:NB, slot, :], ALU.mult).then_inc(s_dot, 1)
                dve.wait_ge(s_dot, lin(lambda s: 2 * s + (slot + 1), i, 1, NB // 2))
                dve.tensor_reduce(s3(s_a, 0), prod[:, 0:NPAGE * WA].rearrange("p (g h d) -> p g h d", g=NPAGE, d=HD),
                                  AX.X, ALU.add)
                dve.tensor_reduce(s3(s_b, 0), prod[:, NPAGE * WA:].rearrange("p (g h d) -> p g h d", g=3, d=HD),
                                  AX.X, ALU.add)
                dve.tensor_reduce(s2(sn_a), prn[:, 0:WA].rearrange("p (h d) -> p h d", d=HD), AX.X, ALU.add)
                dve.tensor_reduce(s3(sn_b, 0), prn[:, WA:].rearrange("p (g h d) -> p g h d", g=3, d=HD),
                                  AX.X, ALU.add).then_inc(kc_used, 1)
                dve.wait_ge(kc_used, lin(lambda s: 2 * s + (slot + 1), i, 1, NB // 2))
            for b in range(2):
                dot(b, b, 0)
            with dve.Fori(1, NB // 2) as i:
                for b in range(2):
                    dot(2 * i + b, b, i)

            def link(ins):
                cnt[0] += 1
                ins.then_inc(s_step, 1)
                dve.wait_ge(s_step, cnt[0])

            link(dve.tensor_tensor(s_b[:, :, :, :], s_b[:, :, :, :],
                                   bs[:, :, :].unsqueeze(2).broadcast_to([P, 3, NB, HPG]), ALU.add))
            dve.tensor_tensor(sn_b[:, :, :, :], sn_b[:, :, :, :],
                              bn[:, :, :].unsqueeze(2).broadcast_to([NB, 3, NB, HPG]), ALU.add).then_inc(s_rows, 1)
            dve.wait_ge(s_ev, 1)
            dve.wait_ge(s_mm, 1)
            link(dve.tensor_tensor(cols[:, 0:1], crow[:, 255:256], lf_new[:, :], ALU.add))
            link(dve.tensor_scalar(crow[:, :], crow[:, :], cols[:, 0:1], -1.0, ALU.subtract, ALU.mult))
            link(dve.tensor_tensor(row_a[:, 0:256], row_a[:, 0:256], crow[:, :], ALU.add))
            link(dve.tensor_tensor(row_a[:, 256:264], row_a[:, 256:264], own_a[:, :], ALU.add))
            link(dve.tensor_tensor(row_b[:, 384:408].rearrange("p (g b) -> p g b", g=3),
                                   row_b[:, 384:408].rearrange("p (g b) -> p g b", g=3),
                                   own_b[:, :].unsqueeze(1).broadcast_to([32, 3, NB]), ALU.add))
            link(dve.tensor_reduce(cols[:, 1:2], row_a[:, :], AX.X, ALU.max, negate=True))
            dve.tensor_reduce(cols[0:32, 2:3], row_b[:, :], AX.X, ALU.max, negate=True).then_inc(s_rows, 1)
            dve.wait_ge(s_ev, 3)
            link(dve.reciprocal(cols[:, 5:6], cols[:, 3:4]))
            link(dve.reciprocal(cols[0:32, 6:7], cols[0:32, 4:5]))
            dve.tensor_scalar(row_a[:, :], row_a[:, :], cols[:, 5:6], None, ALU.mult)
            dve.tensor_scalar(row_b[:, :], row_b[:, :], cols[0:32, 6:7], None, ALU.mult).then_inc(s_rows, 1)
            dve.wait_ge(p_ready, 1)

            def weigh(b, slot, i):
                dve.wait_ge(kc_in[slot], i * V_IN + (V_IN + NB // 2 * K_IN))
                if isinstance(i, int) and i == 0 and slot == 0:
                    pass
                else:
                    dve.wait_ge(v_mm, lin(lambda s: 2 * s + slot, i, 1, NB // 2))
                s3 = (lambda t: t[:, :, b, :]) if isinstance(b, int) else \
                    (lambda t: t[:, :, bass.ds(b, 1), :].rearrange("p g a h -> p g (a h)"))
                s2 = (lambda t: t[:, b, :]) if isinstance(b, int) else \
                    (lambda t: t[:, bass.ds(b, 1), :].rearrange("p a h -> p (a h)"))
                for g in range(NPAGE):
                    s2g = p_a[:, g, b, :] if isinstance(b, int) else \
                        p_a[:, g, bass.ds(b, 1), :].rearrange("p a h -> p (a h)")
                    dve.tensor_tensor(prod[:, g * WA:(g + 1) * WA].rearrange("p (h d) -> p h d", d=HD),
                                      kc_a[:, slot, g, :].rearrange("p (h d) -> p h d", d=HD),
                                      s2g.unsqueeze(2).broadcast_to([P, NHA, HD]), ALU.mult)
                for g in range(3):
                    o = NPAGE * WA + g * 256
                    for rows, dst, src, pr in ((P, prod[:, o:o + 256], kc_b[:, slot, g, :], p_b),
                                               (NB, prn[:, WA + g * 256:WA + (g + 1) * 256],
                                                vn[:, WA + g * 256:WA + (g + 1) * 256], pn_b)):
                        pv = pr[:, g, b, :] if isinstance(b, int) else \
                            pr[:, g, bass.ds(b, 1), :].rearrange("p a h -> p (a h)")
                        dve.tensor_tensor(dst.rearrange("p (h d) -> p h d", d=HD),
                                          src.rearrange("p (h d) -> p h d", d=HD),
                                          pv.unsqueeze(2).broadcast_to([rows, HPG, HD]), ALU.mult)
                dve.tensor_tensor(prn[:, 0:WA].rearrange("p (h d) -> p h d", d=HD),
                                  vn[:, 0:WA].rearrange("p (h d) -> p h d", d=HD),
                                  s2(pn_a).unsqueeze(2).broadcast_to([NB, NHA, HD]), ALU.mult).then_inc(kc_used, 1)
            for b in range(2):
                weigh(b, b, 0)
            with dve.Fori(1, NB // 2) as i:
                for b in range(2):
                    weigh(2 * i + b, b, i)

        def pe_samples(pe):
            pe.wait_ge(s_rows, 1)
            flat = lambda t: t.rearrange("p b h -> p (b h)")
            for pg in range(NPAGE):
                pe.transpose(ps[0:64, 0, pg * P:(pg + 1) * P], flat(s_a[:, pg, :, :]), ident[:, :])
            pe.transpose(ps[0:64, 0, 256:264], flat(sn_a[:, :, :]), ident[0:NB, 0:NB])
            for g in range(3):
                pe.transpose(ps[0:32, 2, g * P:(g + 1) * P], flat(s_b[:, g, :, :]), ident[:, :])
                pe.transpose(ps[0:32, 2, 384 + g * NB:384 + (g + 1) * NB], flat(sn_b[:, g, :, :]),
                             ident[0:NB, 0:NB])
            pe.matmul(ps[0:64, 1, 0:P], flat(lfp[:, 0, :, :]), upto[:, :], start=True, stop=True)
            pe.matmul(ps[0:64, 1, P:2 * P], flat(lfp[:, 0, :, :]), ones[:, :], start=True, stop=False)
            pe.matmul(ps[0:64, 1, P:2 * P], flat(lfp[:, 1, :, :]), upto[:, :], start=False,
                      stop=True).then_inc(s_mm, 1)
            pe.wait_ge(s_rows, 3)
            i64, i32 = ident[0:64, 0:64], ident[0:32, 0:32]
            for pg in range(NPAGE):
                pe.transpose(ps[:, 3, pg * 64:(pg + 1) * 64], row_a[:, pg * P:(pg + 1) * P], i64)
            pe.transpose(ps[0:NB, 4, 0:64], row_a[:, 256:264], i64)
            for g in range(3):
                pe.transpose(ps[:, 3, P + g * 32:P + (g + 1) * 32], row_b[:, g * P:(g + 1) * P], i32)
                last = pe.transpose(ps[0:NB, 4, 64 + g * 32:96 + g * 32],
                                    row_b[:, 384 + g * NB:384 + (g + 1) * NB], i32)
            last.then_inc(s_mm, 1)

            def summed(b):
                pe.wait_ge(kc_used, NB + b + 1)
                for ch in range(6):
                    if ch < 4:
                        terms = [(prod[:, pg * WA + ch * P:pg * WA + (ch + 1) * P], P) for pg in range(NPAGE)] + \
                                [(prn[:, ch * P:(ch + 1) * P], NB)]
                    else:
                        o = (ch - 4) * P
                        terms = [(prod[:, NPAGE * WA + g * 256 + o:NPAGE * WA + g * 256 + o + P], P)
                                 for g in range(3)] + \
                                [(prn[:, WA + g * 256 + o:WA + g * 256 + o + P], NB) for g in range(3)]
                    for n, (t, rows) in enumerate(terms):
                        last = pe.matmul(ps[:, 5, ch * NB + b:ch * NB + b + 1], t, ones[0:rows, 0:1],
                                         start=(n == 0), stop=(n == len(terms) - 1))
                last.then_inc(v_mm, 1)
            for b in range(NB):
                summed(b)
            pe.wait_ge(s_out, 1)

        def act_samples(act):
            act.wait_ge(s_mm, 1)
            act.activation(row_a[:, :], ps[0:64, 0, 0:264], ACT.Copy)
            act.activation(crow[:, :], ps[0:64, 1, 0:256], ACT.Copy)
            act.activation(row_b[:, :], ps[0:32, 2, 0:408], ACT.Copy).then_inc(s_ev, 1)
            act.wait_ge(s_rows, 2)
            act.activation(row_a[:, :], row_a[:, :], ACT.Exp, bias=cols[:, 1:2],
                           accum_out=cols[:, 3:4]).then_inc(s_ev, 1)
            act.activation(row_b[:, :], row_b[:, :], ACT.Exp, bias=cols[0:32, 2:3],
                           accum_out=cols[0:32, 4:5]).then_inc(s_ev, 1)
            act.wait_ge(s_mm, 2)
            act.activation(p_a[:, :, :, :], ps[:, 3, 0:P].rearrange("p (g b h) -> p g b h", g=2, h=NHA), ACT.Copy)
            act.activation(p_b[:, :, :, :], ps[:, 3, P:P + 96].rearrange("p (g b h) -> p g b h", g=3, h=HPG), ACT.Copy)
            act.activation(pn_a[:, :, :], ps[0:NB, 4, 0:64].rearrange("p (b h) -> p b h", h=NHA), ACT.Copy)
            act.activation(pn_b[:, :, :, :], ps[0:NB, 4, 64:160].rearrange("p (g b h) -> p g b h", g=3, h=HPG),
                           ACT.Copy).then_inc(p_ready, 1)
            act.wait_ge(v_mm, NB)
            act.activation(o_st[:, :, SEQ:T], ps[:, 5, 0:6 * NB].rearrange("p (c b) -> p c b", b=NB),
                           ACT.Copy).then_inc(s_out, 1)

        o_hi_done, o_lo_done, za_done, zt_done, z_done2, x_freed = (S("mg_" + n) for n in (
            "o_hi", "o_lo", "za", "zt", "z", "x_freed"))

        def pe_merge(pe, i, lo, hi):
            if isinstance(i, int) and i == 0:
                pe.wait_ge(o_lo_done, 1)
            for j in range(8):
                if j in (2, 3):
                    pe_block(pe, "merge", i, j, lo, hi, o_hi, o_lo)
                elif j in (6, 7):
                    pe_block(pe, "merge", i, j, lo, hi, o_hi[:, PAIRS_A:, :], o_lo[:, PAIRS_A:, :])
                else:
                    pe_block(pe, "merge", i, j, lo, hi, h_hi, h_lo)
            pe_down(pe, "merge", i, lo, hi, 8)

        MERGE_SPLITS = {0: (0,), 1: (1,), 2: (2,), 4: (3,), 5: (4,), 6: (5,), 8: (6,), 11: (7,), 14: (8,)}

        def act_merge(act, i, lo, hi):
            for j in range(16):
                for c in MERGE_SPLITS.get(j, ()):
                    act_split(act, "merge", i, c, lo, hi)
                if j in (0, 1, 4, 5):
                    m = j % 2
                    for part, (s0, w) in enumerate(PARTS):
                        src = product(act, "merge", i, j, part, lo, hi)
                        if j >= 4:
                            act.wait_ge(za_done, lin(lambda s: 6 * s + 3 * m + part + 1, i, lo, hi))
                        elif not isinstance(i, int) or i:
                            act.wait_ge(z_done2, lin(lambda s: 6 * (s - 1) + 3 * m + part + 1, i, lo, hi))
                        act.activation(sg2[:, m, s0:s0 + w], src, ACT.Sigmoid).then_inc(freed["act"], 1)
                if j in (6, 7):
                    m = j - 6
                    for part, (s0, w) in enumerate(PARTS):
                        act.wait_ge(z_done2, lin(lambda s: 6 * s + 3 * m + part + 1, i, lo, hi))
                        act.activation(u_hi[:, m, s0:s0 + w], z_f[:, m, s0:s0 + w], ACT.Copy).then_inc(u_hi_done, 1)

        def dve_merge(dve, i, lo, hi, first):
            for j in range(16):
                for c in MERGE_SPLITS.get(j, ()):
                    dve_split(dve, "merge", i, c, lo, hi)
                m = j % 2
                if j in (2, 3):
                    for part, (s0, w) in enumerate(PARTS):
                        src = product(dve, "merge", i, j, part, lo, hi)
                        dve.wait_ge(freed["act"], lin(lambda s: PLAN.free_of["merge", s, m][1] + part + 1, i, lo, hi))
                        if part == 0 and m == 0 and (not isinstance(i, int) or i):
                            dve.wait_ge(u_lo_done, lin(lambda s: u_parts("merge", 1, 2)(s) - 6, i, lo, hi))
                        dve.tensor_tensor(z_f[:, m, s0:s0 + w], src, sg2[:, m, s0:s0 + w],
                                          ALU.mult).then_inc(freed["dve"], 1)
                    dve.wait_ge(freed["dve"], lin(lambda s: PLAN.free_of["merge", s, j][1] + 3, i, lo, hi))
                    for part in range(3):
                        dve.sem_inc(za_done, 1)
                if j in (6, 7):
                    for part, (s0, w) in enumerate(PARTS):
                        src = product(dve, "merge", i, j, part, lo, hi)
                        dve.wait_ge(freed["act"], lin(lambda s: PLAN.free_of["merge", s, 4 + m][1] + part + 1,
                                                      i, lo, hi))
                        dve.tensor_tensor(sg2[:, m, s0:s0 + w], src, sg2[:, m, s0:s0 + w],
                                          ALU.mult).then_inc(freed["dve"], 1)
                        dve.wait_ge(freed["dve"], lin(lambda s: PLAN.free_of["merge", s, j][1] + part + 1, i, lo, hi))
                        dve.tensor_tensor(z_f[:, m, s0:s0 + w], z_f[:, m, s0:s0 + w], sg2[:, m, s0:s0 + w],
                                          ALU.add).then_inc(z_done2, 1)
                    for part, (s0, w) in enumerate(PARTS):
                        dve.wait_ge(u_hi_done, lin(u_parts("merge", m, part), i, lo, hi))
                        dve.tensor_tensor(u_lo[:, m, s0:s0 + w], z_f[:, m, s0:s0 + w],
                                          u_hi[:, m, s0:s0 + w].bitcast(F32), ALU.subtract).then_inc(u_lo_done, 1)
                if j >= 8:
                    dve_down(dve, "merge", i, lo, hi, first, 8, [j - 8])

        block = ctx.enter_context(nc.Block())

        @block.sync
        def _(sp):
            for n in range(RING):
                sp.dma_start(w_raw[:, n, :], A["w_chunks"][n]).then_inc(w_loaded[n], 16)
            with sp.Fori(1, PLAN.chunks // RING) as i:
                for n in range(RING):
                    sp.wait_ge(w_lo_done, RING * i + (n - RING + 1))
                    sp.dma_start(w_raw[:, n, :], A["w_chunks"][bass.ds(RING * i + n, 1)]
                                 .rearrange("a p c -> (a p) c")).then_inc(w_loaded[n], 16)
            for n in range(PLAN.chunks // RING * RING, PLAN.chunks):
                sp.wait_ge(w_lo_done, n - RING + 1)
                sp.dma_start(w_raw[:, n % RING, :], A["w_chunks"][n]).then_inc(w_loaded[n % RING], 16)

        @block.gpsimd
        def _(pool):
            pool.memset(ones[:, :], 1.0).then_inc(S("ones_set"), 1)
            pool.memset(eps_c[:, :], EPS).then_inc(S("ones_set"), 1)
            pool.memset(one_c[:, :], 1.0).then_inc(S("ones_set"), 1)
            pool.wait_ge(S("ones_set"), 3)
            pool.memset(rb[N_BUCKETS:N_BUCKETS + 1, :], 1.0).then_inc(S("rb_one"), 1)
            pool.dma_start(x_res[:, :, :], A["x_t"].rearrange("(k p) t -> p k t", p=P)).then_inc(x_in, 16)
            for dst, name in ((ident, "ident"), (causal_f, "causal"), (pages, "page_table"), (bf_c, "b_f")):
                pool.dma_start(dst[:, :], A[name]).then_inc(const_in, 16)
            pool.dma_start(gains[:, :, :], A["gains"].rearrange("p (n k) -> p n k", n=6)).then_inc(const_in, 16)
            pool.dma_start(rb[0:N_BUCKETS, :], A["rel_bias"]).then_inc(const_in, 16)
            pool.wait_ge(x_done, x_count[1, 2])
            pool.dma_start(x_spill, x_res[:, :, :]).then_inc(S("x_spilled"), 16)
            pool.wait_ge(h_ready, h_count[2, 2])
            for dst, name in ((sel_p, "sel_prompt"), (sel_s, "sel_sample")):
                pool.dma_start(dst[:, :, :].rearrange("p g y -> p (g y)"), A[name]).then_inc(sel_in, 16)
            pool.dma_start(sel_n[:, :], A["sel_new"]).then_inc(sel_in, 16)
            pool.dma_start(sel_stage, A["head_sel"]).then_inc(hsel_in, 16)
            pool.wait_ge(bias_ev, 3 * HPG)
            pool.dma_start(bias_rows.rearrange("h p y -> p h y"), bias_row[:, :, :]).then_inc(bias_out, 16)
            pool.wait_ge(lf_done, 1)
            pool.dma_start(A["lf_t"], lf_a[:, :]).then_inc(lf_out, 16)
            pool.wait_ge(S("x_spilled"), 16)

            def out_qkv(a, col, k_dst, v_dst):
                pool.wait_ge(kf_done, 3 * a + 3)
                pool.dma_start(k_dst, k_f[:, :]).then_inc(k_out, 16)
                pool.wait_ge(vf_done, 3 * a + 3)
                pool.dma_start(v_dst, v_f[:, :]).then_inc(v_out, 16)
                pool.wait_ge(tok_done, a + 1)
                pool.dma_start(qkv_s[:, :, col:col + P] if isinstance(col, int) else
                               qkv_s[:, :, bass.ds(col, P)], tok[:, :, :]).then_inc(tok_out, 16)

            for p in range(PAIRS_A):
                out_qkv(p, p * P, A["ka_t"][p * P:(p + 1) * P, :], A["va_t"][p * P:(p + 1) * P, :])
            for a in range(PAIRS_A, A_LAST):
                d = a - PAIRS_A
                pair, g = d // 3, d % 3
                if d >= 2:
                    pool.wait_ge(d_mt, 16 * (d - 1))
                if d == 0:
                    pool.wait_ge(oev_done, N_OV * PAIRS_A)
                for hh in range(2):
                    src = bass.AP(bias_rows_t, (g * HPG + 2 * pair + hh) * P * LREL + 127, [[LREL - 1, P], [1, 256]])
                    pool.dma_start(bias_t[:, d % 2, hh, :], src).then_inc(S(f"bias_dma{d % 2}"), 16)
                if g == 2:
                    pool.wait_ge(S(f"bias_dma{d % 2}"), 32 * (d // 2 + 1))
                    pool.memset(bias_t[HD:P, d % 2, :, P:P + HD], NEG).then_inc(bias_in, 1)
                col = g * 256 + pair * P
                out_qkv(a, WA + col, A["kb_t"][col:col + P, :], A["vb_t"][col:col + P, :])
            for n, (name, keep) in enumerate((("b1", 127), ("b2", 256), ("b3", 256))):
                c = A["cache_" + name]
                pool.dma_start(A["buf_" + name], c[:, c.shape[1] - keep:, :]).then_inc(S("buf_out"), 16)
            pool_samples(pool)
            last = ("merge", MERGE_ITERS - 1, 15)
            pool.wait_ge(mm_done, 3 * PLAN.block_of[last] + 3)
            pool.wait_ge(u_lo_done, u_parts("merge", 1, 2)(MERGE_ITERS - 1))
            pool.dma_start(x_res[:, :, :], x_spill).then_inc(x_back, 16)
            pool.wait_ge(x_done, x_count[5, 2])
            pool.dma_start(A["y_t"].rearrange("(k p) t -> p k t", p=P), x_res[:, :, :]).then_inc(S("y_out"), 16)
            pool.wait_ge(S("y_out"), 16)
            pool.wait_ge(S("buf_out"), 48)
            pool.wait_ge(lf_out, 16)
            pool.wait_ge(k_out, 16 * A_LAST)
            pool.wait_ge(v_out, 16 * A_LAST)
            pool.wait_ge(tok_out, 16 * A_LAST)
            pool.wait_ge(bias_out, 16)



        @block.scalar
        def _(act):
            act.wait_ge(S("ones_set"), 3)
            first_splits(act, act_split)
            act_norms(act, 0)
            steps(act, FFN_ITERS, lambda i, lo, hi, first: act_ffn(act, "ffn1", i, lo, hi))
            act_norms(act, 1)
            act_forget(act)
            act.wait_ge(S("x_spilled"), 16)

            def fox(i, lo, hi, first):
                act_qkv(act, "fox", i, lo, hi, 1)
                act_fox(act, i, lo, hi)
            steps(act, PAIRS_A, fox)
            for d in range(3 * PAIRS_B):
                act_qkv(act, "dil", d, d, d + 1, DIL[d % 3])
                act_dil(act, d, d % 3)
                if d % 3 == 2:
                    act_combine(act, d // 3)
            act_samples(act)
            act.wait_ge(combined, PAIRS_B)
            act.wait_ge(s_out, 1)
            act.activation(o_hi[:, :, :], o_st[:, :, :], ACT.Copy).then_inc(o_hi_done, 1)
            steps(act, MERGE_ITERS, lambda i, lo, hi, first: act_merge(act, i, lo, hi))
            act_norms(act, 2)
            steps(act, FFN_ITERS, lambda i, lo, hi, first: act_ffn(act, "ffn2", i, lo, hi), last_apart=True)
            act_norms(act, 3)

        @block.vector
        def _(dve):
            dve.wait_ge(const_in, 96)
            dve.tensor_copy(ident_b[:, :], ident[:, :]).then_inc(S("bf_set"), 1)
            dve.tensor_copy(causal_b[:, :], causal_f[:, :]).then_inc(S("bf_set"), 1)
            dve.tensor_scalar(gains[:, 1, :], gains[:, 1, :], 0.5, None, ALU.mult).then_inc(S("bf_set"), 1)
            dve.tensor_scalar(gains[:, 5, :], gains[:, 5, :], 0.5, None, ALU.mult).then_inc(S("bf_set"), 1)
            dve.wait_ge(S("bf_set"), 4)
            first_splits(dve, dve_split)
            dve_norms(dve, 0)
            steps(dve, FFN_ITERS, lambda i, lo, hi, first: dve_ffn(dve, "ffn1", i, lo, hi, first))
            dve_norms(dve, 1)
            dve.wait_ge(S("rb_one"), 1)
            dve_bias(dve)
            dve_forget(dve)

            def fox(i, lo, hi, first):
                dve_qkv(dve, "fox", i, lo, hi, 1)
                dve_fox(dve, i, lo, hi)
            steps(dve, PAIRS_A, fox)
            for d in range(3 * PAIRS_B):
                dve_qkv(dve, "dil", d, d, d + 1, DIL[d % 3])
                dve_dil(dve, d, d % 3)
                if d % 3 == 2:
                    dve_combine(dve, d // 3)
            dve_samples(dve)
            dve.wait_ge(o_hi_done, 1)
            dve.tensor_tensor(o_lo[:, :, :], o_st[:, :, :], o_hi[:, :, :].bitcast(F32),
                              ALU.subtract).then_inc(o_lo_done, 1)
            dve.wait_ge(o_lo_done, 1)
            steps(dve, MERGE_ITERS, lambda i, lo, hi, first: dve_merge(dve, i, lo, hi, first))
            dve_norms(dve, 2)
            steps(dve, FFN_ITERS, lambda i, lo, hi, first: dve_ffn(dve, "ffn2", i, lo, hi, first), last_apart=True)
            dve_norms(dve, 3)

        @block.tensor
        def _(pe):
            pe_norms(pe, 0)
            steps(pe, FFN_ITERS, lambda i, lo, hi, first: pe_ffn(pe, "ffn1", i, lo, hi))
            pe_norms(pe, 1)
            pe.wait_ge(S("bf_set"), 4)
            pe_bias(pe)
            pe.wait_ge(h_ready, h_count[2, 2])
            pe_block(pe, "forget", 0, 0, 0, 1, h_hi, h_lo)

            def fox(i, lo, hi, first):
                pe_qkv(pe, "fox", i, lo, hi)
                pe_fox(pe, i, lo, hi)
            steps(pe, PAIRS_A, fox)
            for d in range(3 * PAIRS_B):
                pe_qkv(pe, "dil", d, d, d + 1)
                pe_dil(pe, d, d % 3)
                if d % 3 == 2:
                    pe_combine(pe, d // 3)
            pe_samples(pe)
            steps(pe, MERGE_ITERS, lambda i, lo, hi, first: pe_merge(pe, i, lo, hi))
            pe_norms(pe, 2)
            steps(pe, FFN_ITERS, lambda i, lo, hi, first: pe_ffn(pe, "ffn2", i, lo, hi), last_apart=True)
            pe_norms(pe, 3)


def lay_out_weights(w):
    out = np.zeros((PLAN.chunks, P, CH), np.float32)

    def put(n, block):
        k = block.shape[0] // P
        out[n, :, :k * block.shape[1]] = block.reshape(k, P, -1).transpose(1, 0, 2).reshape(P, -1)

    for ph, pre in (("ffn1", "ffn1_"), ("ffn2", "ffn2_")):
        for i in range(FFN_ITERS):
            c = FIRST_CHUNK[ph] + CHUNKS[ph] * i
            for f in range(2):
                cols = slice((2 * i + f) * P, (2 * i + f + 1) * P)
                put(c + 2 * f, w[pre + "w_gate"][:, cols])
                put(c + 2 * f + 1, w[pre + "w_up"][:, cols])
            down = w[pre + "w_down"][2 * i * P:(2 * i + 2) * P]
            put(c + 4, down[:, 0:512])
            put(c + 5, down[:, 512:1024])
    w_in = w["w_in"]
    put(FIRST_CHUNK["forget"], w_in[:, COL_FA:COL_FA + P])
    for p in range(PAIRS_A):
        for n, col in enumerate((COL_QA, COL_KA, COL_VA)):
            put(FIRST_CHUNK["fox"] + 3 * p + n, w_in[:, col + p * P:col + (p + 1) * P])
    for d in range(3 * PAIRS_B):
        for n, col in enumerate((COL_QB, COL_KB, COL_VB)):
            at = col + (d % 3) * 256 + (d // 3) * P
            put(FIRST_CHUNK["dil"] + 3 * d + n, w_in[:, at:at + P])
    for i in range(MERGE_ITERS):
        c = FIRST_CHUNK["merge"] + CHUNKS["merge"] * i
        cols = slice(2 * i * P, (2 * i + 2) * P)
        for m in range(2):
            put(c + m, w_in[:, COL_GA + (2 * i + m) * P:COL_GA + (2 * i + m + 1) * P])
            put(c + 3 + m, w_in[:, COL_GB + (2 * i + m) * P:COL_GB + (2 * i + m + 1) * P])
        put(c + 2, w["w_proj_a"][:, cols])
        put(c + 5, w["w_proj_b"][:, cols])
        down = w["w_out"][cols]
        for n, (a, b) in enumerate(((0, 384), (384, 768), (768, 1024))):
            block = np.zeros((2 * P, 384), np.float32)
            block[:, :b - a] = down[:, a:b]
            put(c + 6 + n, block)
    return out


OUTS = {"y_t": (D, T), "ka_t": (WA, T), "va_t": (WA, T), "lf_t": (NHA, T), "kb_t": (WB, T), "vb_t": (WB, T),
        "buf_b1": (NB, 127, 512), "buf_b2": (NB, 256, 512), "buf_b3": (NB, 256, 512)}


def kernel(**inputs):
    import concourse.bacc as bacc
    from concourse.bass_utils import run_bass_kernel_spmd

    x = {k: np.asarray(v) for k, v in inputs.items()}
    w = {k: x[k][0] for k in x if k.endswith(("w_gate", "w_up", "w_down", "w_out", "w_proj_a", "w_proj_b"))
         or k == "w_in"}
    arrays = dict(shape_constants())
    arrays["x_t"] = np.concatenate([x["x_prompt"][0].T, x["x_sample"][:, 0].T], axis=1)
    gains = [x[n][0] for n in ("ffn1_pre_g", "ffn1_post_g", "mix_pre_g", "mix_post_g", "ffn2_pre_g", "ffn2_post_g")]
    arrays["gains"] = np.stack([g.reshape(KD, P).T for g in gains], axis=1).reshape(P, -1)
    arrays["w_chunks"] = lay_out_weights(w)
    arrays["b_f"] = x["b_f"].reshape(NHA, 1)
    arrays["rel_bias"] = x["rel_bias"]
    arrays["page_table"] = x["page_table"].reshape(1, -1)
    arrays["cache_a_k"] = x["cache_a_k"][0].reshape(-1, PAGE, WA)
    arrays["cache_a_v"] = x["cache_a_v"][0].reshape(-1, PAGE, WA)
    arrays["cache_a_logf"] = x["cache_a_logf"][0]
    for g in (1, 2, 3):
        arrays[f"cache_b{g}"] = x[f"cache_b{g}_kv"][0].reshape(NB, -1, 512)
    nc = bacc.Bacc("TRN2", target_bir_lowering=False, num_devices=1, dynamic_dma_scratch_size=4096)
    A = {}
    for name, a in arrays.items():
        arrays[name] = a = np.ascontiguousarray(a)
        A[name] = nc.dram_tensor(name, a.shape, mybir.dt.from_np(a.dtype), kind="ExternalInput").ap()
    for name, shape in OUTS.items():
        A[name] = nc.dram_tensor(name, shape, F32, kind="ExternalOutput").ap()
    build(nc, A)
    r = run_bass_kernel_spmd(nc, [arrays], core_ids=[0]).results[0]

    def tokens(a, heads):
        a = np.asarray(a).T
        return a[:SEQ].reshape(1, 1, SEQ, heads, -1), a[SEQ:].reshape(1, NB, 1, heads, -1)

    y = np.asarray(r["y_t"]).T
    ka, ka_s = tokens(r["ka_t"], NHA)
    va, va_s = tokens(r["va_t"], NHA)
    lf, lf_s = tokens(r["lf_t"], NHA)
    kb, kb_s = tokens(r["kb_t"], 3 * HPG)
    vb, vb_s = tokens(r["vb_t"], 3 * HPG)
    prompt, sample = [], []
    for g, window in enumerate((128, 512, 2048)):
        hs = slice(g * HPG, (g + 1) * HPG)
        keep = min(window, SEQ)
        prompt.append(np.stack([kb[:, :, SEQ - keep:, hs], vb[:, :, SEQ - keep:, hs]], axis=3))
        old = np.asarray(r[f"buf_b{g + 1}"]).reshape(1, NB, -1, 2, HPG, HD)
        new = np.stack([kb_s[:, :, :, hs], vb_s[:, :, :, hs]], axis=3)
        sample.append(np.concatenate([old, new], axis=2))
    return (y[:SEQ][None], y[SEQ:][:, None], ka, va, lf[..., 0], *prompt, ka_s, va_s, lf_s[..., 0], *sample)
```

```python
from contextlib import ExitStack

import numpy as np
import concourse.bass as bass
from concourse import mybir

F32, F32R, BF16, I32 = mybir.dt.float32, mybir.dt.float32r, mybir.dt.bfloat16, mybir.dt.int32
ALU, ACT, AX = mybir.AluOpType, mybir.ActivationFunctionType, mybir.AxisListType

P = 128
D = 1024
KD = D // P
SEQ, NB = 1024, 8
T = SEQ + NB
PARTS = ((0, 352), (352, 352), (704, 328))
DFF = 2816
HD = 64
NHA, WA = 8, 512
DIL = (1, 4, 16)
HPG = 4
WB = 768
PAIRS_A, PAIRS_B = NHA // 2, HPG // 2
COL_QA, COL_KA, COL_VA, COL_FA = 0, 512, 1024, 1536
COL_QB = 1544
COL_KB, COL_VB = COL_QB + WB, COL_QB + 2 * WB
COL_GA = COL_QB + 3 * WB
COL_GB = COL_GA + D
NQ = SEQ // P
PAGE, NPAGE = 128, 2
CH = 1024
RING = 3
FFN_ITERS = DFF // P // 2
PROJ_ITERS = KD // 4
SCALE = HD ** -0.5
EPS = 1e-6
NEG = -1e30
LREL = 384
N_BUCKETS, MAX_DISTANCE = 32, 2048
GATE_SLOTS = 4
UNITS = [(0, 3, 0), (1, 0, 8), (0, 2, 0), (1, 1, 6), (1, 2, 0), (0, 1, 6), (0, 0, 0), (1, 3, 2)]
PT_SLOTS = 10
SAMPLE_KEYS = (128, 64, 16)

PHASES = ("ffn1", "forget", "fox", "dil", "gates", "proj", "out", "ffn2")
ITERS = dict(ffn1=FFN_ITERS, forget=1, fox=PAIRS_A, dil=PAIRS_B * 3, gates=1, proj=PROJ_ITERS, out=1, ffn2=FFN_ITERS)
CHUNKS = dict(ffn1=6, forget=1, fox=3, dil=3, gates=2 * KD, proj=3, out=KD, ffn2=6)
FFN_BLOCKS = [(0, 0, 128, 8, "act"), (1, 0, 128, 8, "u"), (2, 0, 128, 8, "act"), (3, 0, 128, 8, "u")] + \
             [(4 + m // 4, 128 * (m % 4), 512, 2, "dve") for m in range(8)]
QKV_BLOCKS = [(0, 0, 128, 8, "dve"), (1, 0, 128, 8, "dve"), (2, 0, 128, 8, "act")]
PROJ_BLOCKS = [(m // 2, 128 * (m % 2), 256, 4, "dve") if branch == 0 else (2, 128 * m, 512, 2, "dve")
               for m in range(4) for branch in range(2)]
BLOCKS = dict(ffn1=FFN_BLOCKS, ffn2=FFN_BLOCKS, forget=[(0, 0, 128, 8, "act")], fox=QKV_BLOCKS, dil=QKV_BLOCKS,
              gates=[(n, 0, 128, 8, "act") for n in range(2 * KD)], proj=PROJ_BLOCKS,
              out=[(n, 0, 128, 8, "dve") for n in range(KD)])


class Counts:

    def __init__(self, chunks, chunk_of, block_of, free_of, before, last_block):
        self.chunks, self.chunk_of, self.block_of = chunks, chunk_of, block_of
        self.free_of, self.before, self.last_block = free_of, before, last_block


def plan():
    chunk = block = 0
    freed = dict(act=0, dve=0, u=0)
    chunk_of, block_of, free_of, before, last_block = {}, {}, {}, {}, {}
    user = [None, None]
    for ph in PHASES:
        for i in range(ITERS[ph]):
            for j, (c, _, _, _, who) in enumerate(BLOCKS[ph]):
                key = (ph, i, j)
                chunk_of[key] = chunk + c
                last_block[chunk + c] = block
                block_of[key] = block
                free_of[key] = (who, freed[who])
                before[key] = user[j % 2]
                user[j % 2] = key
                freed[who] += 3
                block += 1
            chunk += CHUNKS[ph]
    return Counts(chunk, chunk_of, block_of, free_of, before, last_block)


PLAN = plan()
FIRST_CHUNK = {}
for _ph in PHASES:
    FIRST_CHUNK[_ph] = PLAN.chunk_of[_ph, 0, 0]


def lin(f, i, lo, hi):
    if isinstance(i, int):
        return f(i)
    a, d = f(lo), (f(lo + 1) - f(lo) if hi > lo + 1 else 0)
    assert all(f(x) == a + d * (x - lo) for x in range(lo, hi))
    return (i * d + (a - d * lo)) if d else a


def t5_buckets(dist):
    dist = np.asarray(dist)
    exact = N_BUCKETS // 2
    large = exact + (np.log(np.maximum(dist, 1) / exact) / np.log(MAX_DISTANCE / exact)
                     * (N_BUCKETS - exact)).astype(np.int32)
    return np.where(dist < exact, dist, np.minimum(large, N_BUCKETS - 1)).astype(np.int32)


def shape_constants():
    c = {}
    sel = np.zeros((P, NHA), np.float32)
    for h in range(NHA):
        sel[h, h] = sel[32 + h, h] = 1.0
    c["head_sel"] = sel
    c["ident"] = np.eye(P, dtype=np.float32)
    q, k = np.arange(P)[:, None], np.arange(P)[None, :]
    c["causal"] = np.where(k <= q, 0.0, NEG).astype(np.float32)
    c["upto"] = (q <= k).astype(np.float32)
    prompt = np.zeros((N_BUCKETS + 1, 3, LREL), np.float32)
    sample = np.zeros((N_BUCKETS + 1, 3, P), np.float32)
    for g, dil in enumerate(DIL):
        most = min(128, SEQ // dil - 1)
        for y in range(LREL):
            d = 255 - y
            if 0 <= d <= most:
                prompt[t5_buckets(d * dil), g, y] = 1.0
            else:
                prompt[N_BUCKETS, g, y] = NEG
        for p in range(P):
            if p < SAMPLE_KEYS[g]:
                sample[t5_buckets((SAMPLE_KEYS[g] - p) * dil), g, p] = 1.0
            else:
                sample[N_BUCKETS, g, p] = NEG
    new = np.zeros((N_BUCKETS + 1, NB), np.float32)
    new[t5_buckets(0)] = 1.0
    c["sel_prompt"], c["sel_sample"], c["sel_new"] = prompt.reshape(33, -1), sample.reshape(33, -1), new
    own = np.where(np.arange(NB)[:, None] == np.arange(NB)[None, :], 0.0, NEG).astype(np.float32)
    c["own_a"] = np.repeat(own, NHA, axis=0)
    c["own_b"] = np.repeat(own, HPG, axis=0)
    c["head_a"] = np.tile(np.eye(NHA, dtype=np.float32), (NB, 1))
    c["head_b"] = np.tile(np.eye(HPG, dtype=np.float32), (NB, 1))
    return c


def build(nc, A):
    ctx = ExitStack()
    with ctx:
        class Place:

            def __init__(self, at, end):
                self.at, self.end = at, end

            def __call__(self, name, shape, dt):
                n = int(np.prod(shape[1:])) * (2 if dt == BF16 else 4)
                t = nc.alloc_sbuf_tensor_at(name, shape, dt, offset=self.at)
                self.at += -(-n // 32) * 32
                assert self.at <= self.end, (name, self.at, self.end)
                return t

        base = -(-nc.sbuf_base // 32) * 32
        ring = Place(base, base + 3 * RING * 4 * CH)
        w_raw = ring("w_raw", [P, RING, CH], F32)
        w_hi = ring("w_hi", [P, RING, CH], F32R)
        w_lo = ring("w_lo", [P, RING, CH], F32R)
        hidden = Place(ring.end, ring.end + 2 * 4 * KD * T)
        h_hi = hidden("h_hi", [P, KD, T], F32R)
        h_lo = hidden("h_lo", [P, KD, T], F32R)
        R0 = hidden.end
        R1, R2, R3, R4, R5 = R0 + 33024, R0 + 57792, R0 + 66048, R0 + 90816, R0 + 115584
        x_res = Place(R0, R1)("x_res", [P, KD, T], F32)
        acc = Place(R1, R3)("acc", [P, KD, T], F32)
        pu = Place(R3, R4)
        u_hi, u_lo = pu("u_hi", [P, 2, T], F32R), pu("u_lo", [P, 2, T], F32R)
        sg2 = pu("sg2", [P, 2, T], F32)
        gate_f, u_f = sg2[:, 0, :], sg2[:, 1, :]
        PW = PARTS[0][1]
        pn = Place(R4, R5)
        pn2 = Place(R3, R4)
        norm_buf = [pn2("norm_buf0", [P, KD, PW], F32), pn("norm_buf1", [P, KD, PW], F32),
                    pn2("norm_buf2", [P, KD, PW], F32)]
        sq_sum = pn("sq_sum", [P, T], F32)
        sq_tile = Place(R4, R5)("sq_tile", [P, 2, T], F32)
        root, rinv = pn("root", [P, 3, PW], F32), pn("rinv", [P, 3, PW], F32)
        o_hi, z_f = Place(R0, R2)("o_hi", [P, 6, T], F32R), Place(R0 + 24768, R1)("z_f", [P, 2, T], F32)
        gate_in = Place(R3, R4)("gate_in", [P, 2, 2, T], F32)
        o_lo = Place(R4, R5)("o_lo", [P, 6, T], F32R)
        t1 = Place(R0, R1)
        q_hi, q_lo = t1("q_hi", [P, SEQ], F32R), t1("q_lo", [P, SEQ], F32R)
        k_hi, k_lo = t1("k_hi", [P, SEQ], F32R), t1("k_lo", [P, SEQ], F32R)
        v_g, k_f = t1("v_g", [P, SEQ], F32), t1("k_f", [P, T], F32)
        prob = t1("prob", [P, 2, SEQ], F32)
        prob_b = prob[:, :, :].rearrange("p a (s c) -> p (a s) c", c=256)
        o_st = Place(R1, R2)("o_st", [P, 6, T], F32)
        t2 = Place(R2, R5)
        pt_hi, pt_lo = t2("pt_hi", [P, PT_SLOTS, 256], F32R), t2("pt_lo", [P, PT_SLOTS, 256], F32R)
        vt_hi, vt_lo = t2("vt_hi", [P, NQ, 3, HD], F32R), t2("vt_lo", [P, NQ, 3, HD], F32R)
        v_f = t2("v_f", [P, T], F32)
        score_b = v_g[:, :].rearrange("p (s c) -> p s c", c=256)
        q_s = t2("q_s", [P, NB], F32)
        R2b = t2.at
        ncum = t2("neg_cum", [P, SEQ], F32R)
        pair_sel = t2("pair_sel", [P, 2, P], F32R)
        lf_at = t2.at
        lf_z, lf_e, lf_a = (t2(n, [NHA, T], F32) for n in ("lf_z", "lf_e", "lf_a"))
        bias_row = Place(lf_at, R5)("bias_row", [3 * HPG, 3, LREL], F32)
        cum, cum_one = lf_z[:, 0:SEQ], lf_e[:, 0:SEQ]
        t3 = Place(R2b, R5)
        o_g = t3("o_g", [P, 3, SEQ], F32)
        bias_t = t3("bias_t", [P, 2, 2, 256], F32)
        wide = t3("wide", [P, NQ, 2, HD], F32)
        wg = Place(R0, R1)("wg", [P, 3, SEQ], F32)
        mxall, tsum = k_f[:, 0:SEQ], v_f[:, 0:SEQ]
        t5 = Place(R2, R5)
        kc_a, kc_b = t5("kc_a", [P, 2, NPAGE, WA], F32), t5("kc_b", [P, 2, 3, 256], F32)
        qb = t5("qb", [P, 2, WA + WB], F32)
        prod = t5("prod", [P, NPAGE * WA + WB], F32)
        kn, vn = t5("kn", [NB, WA + WB], F32), t5("vn", [NB, WA + WB], F32)
        prn = t5("prn", [NB, WA + WB], F32)
        lfp = t5("lfp", [P, NPAGE, NB, NHA], F32)
        s_a, s_b = t5("s_a", [P, NPAGE, NB, NHA], F32), t5("s_b", [P, 3, NB, HPG], F32)
        sn_a, sn_b = t5("sn_a", [NB, NB, NHA], F32), t5("sn_b", [NB, 3, NB, HPG], F32)
        p_a, p_b = t5("p_a", [P, NPAGE, NB * 72], F32), t5("p_b", [P, 3, NB * 36], F32)
        t5b = Place(R0, R1)
        upto = t5b("upto_c", [P, P], F32)
        row_a, row_b = t5b("row_a", [64, 264], F32), t5b("row_b", [32, 408], F32)
        crow = t5b("crow", [64, 256], F32)
        cols = t5b("cols", [64, 8], F32)
        head_a, head_b = t5b("head_a_c", [64, NHA], F32), t5b("head_b_c", [32, HPG], F32)
        pn_a, pn_b = t5b("pn_a", [NB, NB, NHA], F32), t5b("pn_b", [NB, 3, NB, HPG], F32)
        o_rows = t5b("o_rows", [64, 2, HD], F32)
        masked = t5b("masked", [64, WA + 256], F32)
        lf_new = t5b("lf_new", [64, 1], F32)
        gate_st = t5b("gate_st", [P, GATE_SLOTS, T], F32)
        own_a, own_b = t5b("own_a_c", [64, NB], F32), t5b("own_b_c", [32, NB], F32)
        pc = Place(R5, nc.sbuf_usable_end)
        ident, ones = pc("ident_c", [P, P], F32), pc("ones", [P, P], F32)
        causal_f = pc("causal_c", [P, P], F32)
        ident_b, causal_b = pc("ident_b", [P, P], BF16), pc("causal_b", [P, P], BF16)
        head_sel = pc("head_sel_c", [P, NHA], F32)
        gains = pc("gains_c", [P, 6, KD], F32)
        eps_c, one_c, bf_c = pc("eps_c", [P, 1], F32), pc("one_c", [P, 1], F32), pc("b_f_c", [NHA, 1], F32)
        rb = pc("rel_bias_c", [N_BUCKETS + 1, 3 * HPG], F32)
        bs, bn = pc("bias_sample", [P, 3, HPG], F32), pc("bias_new", [NB, 3, HPG], F32)
        pages = pc("pages_c", [1, NB * NPAGE], I32)
        nmax, rsum = pc("nmax", [P, 2], F32), pc("rsum", [P, 256], F32)
        tok = pc("tok", [NB, 3, P], F32)
        mx, nmx, den = (pc(n, [P, 3, 2, NQ], F32) for n in ("mx", "nmx", "den"))
        t6 = Place(R2, R2b)
        sel_p, sel_s, sel_n = t6("sel_prompt_c", [33, 3, LREL], F32), t6("sel_sample_c", [33, 3, P], F32), \
            t6("sel_new_c", [33, NB], F32)

        ps = ctx.enter_context(nc.psum_tensor("ps", [P, 8, 512], F32))
        psf = ps[:, :, :].rearrange("p b c -> p (b c)")

        def bank(n, w=512):
            return ps[:, n, 0:w]

        x_spill = nc.dram_tensor("x_spill", [P, KD, T], F32).ap()
        gates_s = nc.dram_tensor("gates_s", [2 * KD, P, T], F32).ap()
        bias_rows_t = nc.dram_tensor("bias_rows", [3 * HPG, P, LREL], F32)
        bias_rows = bias_rows_t.ap()
        qkv_s = nc.dram_tensor("qkv_s", [NB, 3, WA + WB], F32).ap()

        sem = {}

        def S(name):
            if name not in sem:
                sem[name] = ctx.enter_context(nc.semaphore(name))
            return sem[name]

        w_loaded = [S(f"w_loaded{n}") for n in range(RING)]
        w_hi_done, w_lo_done, mm_done = S("w_hi_done"), S("w_lo_done"), S("mm_done")
        u_f_done = S("u_f_done")
        freed = dict(act=S("banks_freed_by_act"), dve=S("banks_freed_by_dve"), u=u_f_done)
        const_in, x_in = S("const_in"), [S(f"x_in{part}") for part in range(3)]

        def chunk_no(ph, c):
            return lambda s: FIRST_CHUNK[ph] + s * CHUNKS[ph] + c

        def act_split(act, ph, i, c, lo, hi):
            f = chunk_no(ph, c + 2)
            i0 = i if isinstance(i, int) else lo
            slot = f(i0) % RING
            if isinstance(i, int) and f(i) >= PLAN.chunks:
                return
            act.wait_ge(w_loaded[slot], lin(lambda s: 16 * (f(s) // RING + 1), i, lo, hi))
            if f(i0) >= RING:
                act.wait_ge(mm_done, lin(lambda s: 3 * PLAN.last_block[f(s) - RING] + 3, i, lo, hi))
            act.activation(w_hi[:, slot, :], w_raw[:, slot, :], ACT.Copy).then_inc(w_hi_done, 1)

        def dve_split(dve, ph, i, c, lo, hi):
            f = chunk_no(ph, c + 2)
            slot = f(i if isinstance(i, int) else lo) % RING
            if isinstance(i, int) and f(i) >= PLAN.chunks:
                return
            dve.wait_ge(w_hi_done, lin(lambda s: f(s) + 1, i, lo, hi))
            dve.tensor_tensor(w_lo[:, slot, :], w_raw[:, slot, :], w_hi[:, slot, :].bitcast(F32),
                              ALU.subtract).then_inc(w_lo_done, 1)

        def first_splits(eng, split):
            for c in (-2, -1):
                split(eng, "ffn1", 0, c, 0, 1)

        def pe_block(pe, ph, i, j, lo, hi, rhs_hi, rhs_lo, rhs_wait=None):
            c, off, width, k_tiles, _ = BLOCKS[ph][j]
            i0 = i if isinstance(i, int) else lo
            slot = PLAN.chunk_of[ph, i0, j] % RING
            hi_w = w_hi[:, slot, 0:k_tiles * width].rearrange("p (k c) -> p k c", c=width)
            lo_w = w_lo[:, slot, 0:k_tiles * width].rearrange("p (k c) -> p k c", c=width)
            pe.wait_ge(w_lo_done, lin(lambda s: PLAN.chunk_of[ph, s, j] + 1, i, lo, hi))
            for part, (s0, w) in enumerate(PARTS):
                if PLAN.before[ph, i0, j] is not None:
                    who = PLAN.free_of[PLAN.before[ph, i0, j]][0]
                    pe.wait_ge(freed[who], lin(lambda s: PLAN.free_of[PLAN.before[ph, s, j]][1] + part + 1,
                                               i, lo, hi))
                if rhs_wait:
                    rhs_wait(part)
                out = bank(3 * (j % 2) + part, w)
                for k in range(k_tiles):
                    for n, (a, b) in enumerate(((hi_w, rhs_hi), (hi_w, rhs_lo), (lo_w, rhs_hi))):
                        last = pe.matmul(out, a[:, k, off:off + P], b[:, k, s0:s0 + w],
                                         start=(k == 0 and n == 0), stop=(k == k_tiles - 1 and n == 2))
                last.then_inc(mm_done, 1)

        def product(eng, ph, i, j, part, lo, hi):
            eng.wait_ge(mm_done, lin(lambda s: 3 * PLAN.block_of[ph, s, j] + part + 1, i, lo, hi))
            return bank(3 * (j % 2) + part, PARTS[part][1])

        GROUPS = [[(0, 0), (0, 1), (0, 2)],
                  [(1, 0), (1, 1), (1, 2), (2, 0), (2, 1), (2, 2)],
                  [(3, 0), (3, 1), (3, 2), (4, 0), (4, 1), (4, 2)],
                  [(5, 0), (5, 1), (5, 2)]]
        EVENTS = [e for g in GROUPS for e in g]
        EV = {e: n for n, e in enumerate(EVENTS)}
        post_sq, post_sum = S("post_squares"), S("post_square_sums")
        x_count = {e: n + 1 for n, e in enumerate(e for e in EVENTS if e[0] % 2)}
        h_count = {e: n + 1 for n, e in enumerate(e for e in EVENTS if e[0] % 2 == 0)}
        squares, sums, roots, normed_f, h_hi_done, x_done, h_ready, recips, x_back = (S(n) for n in (
            "squares", "sums", "roots", "normed_f", "h_hi_done", "x_done", "h_ready", "recips", "x_back"))
        post_normed = S("post_normed")
        AFTER = {1: "ffn1", 3: "out", 5: "ffn2"}

        def act_square(act, e):
            t, part = e
            s0, w = PARTS[part]
            n = EV[e]
            if t == 0:
                act.wait_ge(x_in[part], 16)
            else:
                act.wait_ge(x_done, x_count[t - 1, part])
            if n >= 3:
                b = EVENTS[n - 3]
                act.wait_ge(x_done if b[0] % 2 else h_ready, (x_count if b[0] % 2 else h_count)[b])
            act.activation(norm_buf[n % 3][:, :, 0:w], x_res[:, :, s0:s0 + w],
                           ACT.Square).then_inc(squares, 1)

        def act_post_square(act, t, m):
            ph = AFTER[t]
            last = ITERS[ph] - 1, len(BLOCKS[ph]) - KD + m
            if m >= 3:
                act.wait_ge(post_sum, 3 * (KD * (t // 2) + m - 2))
            for part, (s0, w) in enumerate(PARTS):
                act.wait_ge(freed["dve"], PLAN.free_of[ph, last[0], last[1]][1] + part + 1)
                dst = sq_tile[:, m % 2, s0:s0 + w] if m else sq_sum[:, s0:s0 + w]
                act.activation(dst, acc[:, m, s0:s0 + w], ACT.Square).then_inc(post_sq, 1)

        def dve_post_add(dve, t, m):
            for part, (s0, w) in enumerate(PARTS):
                done = 3 * (KD * (t // 2) + m) + part + 1
                dve.wait_ge(post_sq, done)
                if m > 1:
                    dve.wait_ge(post_sum, done - 3)
                if m:
                    dve.tensor_tensor(sq_sum[:, s0:s0 + w], sq_sum[:, s0:s0 + w], sq_tile[:, m % 2, s0:s0 + w],
                                      ALU.add).then_inc(post_sum, 1)
                else:
                    dve.sem_inc(post_sum, 1)

        def act_root(act, e):
            n, w = EV[e], PARTS[e[1]][1]
            act.wait_ge(sums, n + 1)
            if n >= 3:
                act.wait_ge(recips, n - 2)
            act.activation(root[:, n % 3, 0:w], bank(6 + n % 2, w), ACT.Sqrt, bias=eps_c[:, 0:1],
                           scale=1.0 / D).then_inc(roots, 1)

        def act_high(act, e):
            s0, w = PARTS[e[1]]
            act.wait_ge(normed_f, h_count[e])
            act.activation(h_hi[:, :, s0:s0 + w], norm_buf[EV[e] % 3][:, :, 0:w], ACT.Copy).then_inc(h_hi_done, 1)

        def act_norms(act, group):
            post = [e for e in GROUPS[group] if e[0] % 2]
            pre = [e for e in GROUPS[group] if e[0] % 2 == 0]
            for part in range(3):
                if post:
                    act_root(act, post[part])
                if pre and part < (2 if post else 3):
                    if not post or part:
                        act_square(act, pre[part - 1 if post else part])
            if pre and post:
                act_square(act, pre[1])
            for part, e in enumerate(pre):
                act_root(act, e)
                if post and part == 0:
                    act_square(act, pre[2])
                act_high(act, e)

        def pe_norms(pe, group):
            for e in GROUPS[group]:
                n, w = EV[e], PARTS[e[1]][1]
                if n == 0:
                    pe.wait_ge(S("ones_set"), 3)
                if e[0] % 2:
                    pe.wait_ge(post_sum, 3 * (KD * (e[0] // 2 + 1) - 1) + e[1] + 1)
                else:
                    pe.wait_ge(squares, h_count[e])
                if n >= 2:
                    pe.wait_ge(roots, n - 1)
                s0 = PARTS[e[1]][0]
                terms = [sq_sum[:, s0:s0 + w]] if e[0] % 2 else [norm_buf[n % 3][:, k, 0:w] for k in range(KD)]
                for k, term in enumerate(terms):
                    last = pe.matmul(bank(6 + n % 2, w), ones[:, :], term, start=(k == 0), stop=(k == len(terms) - 1))
                last.then_inc(sums, 1)

        def dve_norms(dve, group):
            for e in GROUPS[group]:
                t, part = e
                s0, w = PARTS[part]
                n = EV[e]
                buf = norm_buf[n % 3]
                src = acc if t % 2 else x_res
                dve.wait_ge(roots, n + 1)
                dve.reciprocal(rinv[:, n % 3, 0:w], root[:, n % 3, 0:w]).then_inc(recips, 1)
                dve.wait_ge(recips, n + 1)
                if n >= 3:
                    b = EVENTS[n - 3]
                    dve.wait_ge(x_done if b[0] % 2 else h_ready, (x_count if b[0] % 2 else h_count)[b])
                for k in range(KD):
                    last = dve.scalar_tensor_tensor(out=buf[:, k, 0:w], in0=src[:, k, s0:s0 + w],
                                                    scalar=gains[:, t, k:k + 1], in1=rinv[:, n % 3, 0:w],
                                                    op0=ALU.mult, op1=ALU.mult)
                if t % 2:
                    last.then_inc(post_normed, 1)
                    dve.wait_ge(post_normed, x_count[e])
                    if t == 3:
                        dve.wait_ge(x_back, 16)
                    dve.tensor_tensor(x_res[:, :, s0:s0 + w], x_res[:, :, s0:s0 + w], buf[:, :, 0:w],
                                      ALU.add).then_inc(x_done, 1)
                    dve.wait_ge(x_done, x_count[e])
                else:
                    last.then_inc(normed_f, 1)

        def pool_norms(pool, group):
            for t, part in GROUPS[group]:
                e, (s0, w) = (t, part), PARTS[part]
                if t % 2 == 0:
                    if h_count[e] > 1:
                        pool.wait_ge(h_ready, h_count[e] - 1)
                    else:
                        pool.wait_ge(S("rb_one"), 1)
                    pool.wait_ge(h_hi_done, h_count[e])
                    pool.tensor_tensor(h_lo[:, :, s0:s0 + w], norm_buf[EV[e] % 3][:, :, 0:w],
                                       h_hi[:, :, s0:s0 + w].bitcast(F32), ALU.subtract).then_inc(h_ready, 1)

        u_hi_done, u_lo_done = S("u_hi_done"), S("u_lo_done")
        U_STEP = dict(ffn1=0, ffn2=FFN_ITERS)

        def u_parts(ph, f, part):
            return lambda s: 3 * (2 * (U_STEP[ph] + s) + f) + part + 1

        def pe_down(pe, ph, i, lo, hi, j0):
            for j in range(j0, j0 + 8):
                pe_block(pe, ph, i, j, lo, hi, u_hi, u_lo,
                         (lambda part: pe.wait_ge(u_lo_done, lin(u_parts(ph, 1, part), i, lo, hi)))
                         if j == j0 else None)

        def post_of(ph, i):
            for t, name in AFTER.items():
                if name == ph and isinstance(i, int) and i == ITERS[ph] - 1:
                    return t
            return None

        def dve_down(dve, ph, i, lo, hi, first, j0, ms):
            for m in ms:
                for part, (s0, w) in enumerate(PARTS):
                    src = product(dve, ph, i, j0 + m, part, lo, hi)
                    dst = acc[:, m, s0:s0 + w]
                    if first:
                        dve.tensor_copy(dst, src).then_inc(freed["dve"], 1)
                    else:
                        dve.tensor_tensor(dst, dst, src, ALU.add).then_inc(freed["dve"], 1)
                t = post_of(ph, i)
                if t is not None and m:
                    dve_post_add(dve, t, m - 1)
                if t is not None and m == KD - 1:
                    dve_post_add(dve, t, m)

        def pe_ffn(pe, ph, i, lo, hi):
            first = isinstance(i, int) and i == 0
            norm = 0 if ph == "ffn1" else 4
            for j in range(4):
                pe_block(pe, ph, i, j, lo, hi, h_hi, h_lo,
                         (lambda part: pe.wait_ge(h_ready, h_count[norm, part])) if first and j == 0 else None)
            pe_down(pe, ph, i, lo, hi, 4)

        def act_ffn(act, ph, i, lo, hi):
            t = post_of(ph, i)
            if isinstance(i, int) and i == 0:
                act.wait_ge(h_ready, h_count[0 if ph == "ffn1" else 4, 2])
            for j in range(6):
                act_split(act, ph, i, j, lo, hi)
                f = j // 2
                if j in (0, 2):
                    for part, (s0, w) in enumerate(PARTS):
                        src = product(act, ph, i, j, part, lo, hi)
                        if ph != "ffn1" or f or not isinstance(i, int) or i:
                            act.wait_ge(u_f_done, lin(lambda s: u_parts(ph, f, part)(s) - 3, i, lo, hi))
                        act.activation(gate_f[:, s0:s0 + w], src, ACT.Silu).then_inc(freed["act"], 1)
                if j in (1, 3):
                    for part, (s0, w) in enumerate(PARTS):
                        act.wait_ge(u_f_done, lin(u_parts(ph, f, part), i, lo, hi))
                        act.activation(u_hi[:, f, s0:s0 + w], u_f[:, s0:s0 + w], ACT.Copy).then_inc(u_hi_done, 1)
                if t is not None and j >= 4:
                    for m in range(4 * (j - 4), 4 * (j - 3)):
                        act_post_square(act, t, m)

        def dve_ffn(dve, ph, i, lo, hi, first):
            for j in range(6):
                dve_split(dve, ph, i, j, lo, hi)
                f = j // 2
                if j in (1, 3):
                    for part, (s0, w) in enumerate(PARTS):
                        src = product(dve, ph, i, j, part, lo, hi)
                        dve.wait_ge(freed["act"], lin(lambda s: PLAN.free_of[ph, s, j - 1][1] + part + 1, i, lo, hi))
                        if ph != "ffn1" or f or not isinstance(i, int) or i:
                            dve.wait_ge(u_lo_done, lin(lambda s: u_parts(ph, f, part)(s) - 3, i, lo, hi))
                        dve.tensor_tensor(u_f[:, s0:s0 + w], src, gate_f[:, s0:s0 + w],
                                          ALU.mult).then_inc(u_f_done, 1)
                    for part, (s0, w) in enumerate(PARTS):
                        dve.wait_ge(u_hi_done, lin(u_parts(ph, f, part), i, lo, hi))
                        dve.tensor_tensor(u_lo[:, f, s0:s0 + w], u_f[:, s0:s0 + w],
                                          u_hi[:, f, s0:s0 + w].bitcast(F32), ALU.subtract).then_inc(u_lo_done, 1)
                if j >= 4:
                    dve_down(dve, ph, i, lo, hi, first, 4, range(4 * (j - 4), 4 * (j - 3)))

        def steps(eng, n, body, last_apart=False):
            body(0, 0, 1, True)
            end = n - 1 if last_apart else n
            with eng.Fori(1, end) as i:
                body(i, 1, end, False)
            if last_apart:
                body(n - 1, n - 1, n, False)

        bias_mm, bias_ev, bias_out = S("bias_mm"), S("bias_ev"), S("bias_out")
        sel_in = S("sel_in")

        def pe_bias(pe):
            pe.wait_ge(sel_in, 48)
            pe.wait_ge(S("rb_one"), 1)
            pe.wait_ge(const_in, 112)
            for g in range(3):
                if g == 2:
                    pe.wait_ge(bias_ev, 1)
                pe.matmul(ps[0:3 * HPG, 6 + g % 2, 0:LREL], rb[:, :], sel_p[:, g, :],
                          start=True, stop=True).then_inc(bias_mm, 1)
            pe.wait_ge(bias_ev, 2)
            for g in range(3):
                pe.matmul(ps[:, 7, g * HPG:(g + 1) * HPG], sel_s[:, g, :], rb[:, g * HPG:(g + 1) * HPG],
                          start=True, stop=True)
            pe.matmul(ps[0:NB, 7, 16:28], sel_n[:, :], rb[:, :], start=True, stop=True).then_inc(bias_mm, 1)
            pe.wait_ge(bias_ev, 5)

        def dve_bias(dve):
            for g in range(3):
                dve.wait_ge(bias_mm, g + 1)
                dve.tensor_copy(bias_row[:, g, :], ps[0:3 * HPG, 6 + g % 2, 0:LREL]).then_inc(bias_ev, 1)
            dve.wait_ge(bias_mm, 4)
            dve.tensor_copy(bs[:, :, :], ps[:, 7, 0:12].rearrange("p (g h) -> p g h", h=HPG)).then_inc(bias_ev, 1)
            dve.tensor_copy(bn[:, :, :], ps[0:NB, 7, 16:28].rearrange("p (g h) -> p g h", h=HPG)).then_inc(bias_ev, 1)

        z_done, az_done, ez_done, l1_done, lf_done, cum_done, nc_hi, nc_done = (S(n) for n in (
            "z_done", "az_done", "ez_done", "l1_done", "lf_done", "cum_done", "nc_hi", "nc_done"))
        vt_edges = S("vt_edges")
        ncum_zero = S("ncum_zero")

        def act_forget(act):
            act_split(act, "forget", 0, 0, 0, 1)
            act.wait_ge(h_ready, h_count[2, 2])
            for part, (s0, w) in enumerate(PARTS):
                src = product(act, "forget", 0, 0, part, 0, 1)
                act.activation(lf_z[:, s0:s0 + w], src[0:NHA, :], ACT.Identity,
                               bias=bf_c[:, 0:1]).then_inc(freed["act"], 1)
            act.wait_ge(az_done, 1)
            act.activation(lf_e[:, :], lf_a[:, :], ACT.Exp, scale=-1.0).then_inc(ez_done, 1)
            act.wait_ge(ez_done, 1)
            act.activation(lf_a[:, :], lf_e[:, :], ACT.Ln, bias=one_c[0:NHA, 0:1]).then_inc(l1_done, 1)
            act.wait_ge(cum_done, 1)
            act.wait_ge(ncum_zero, 1)
            act.activation(ncum[0:NHA, :], cum, ACT.Copy, scale=-1.0).then_inc(nc_hi, 1)

        def dve_forget(dve):
            dve_split(dve, "forget", 0, 0, 0, 1)
            dve.wait_ge(h_ready, h_count[2, 2])
            dve.memset(ncum[:, :].bitcast(F32), 0.0).then_inc(ncum_zero, 1)
            dve.memset(vt_hi[:, :, 1, :].bitcast(F32), 1.0).then_inc(vt_edges, 1)
            dve.memset(vt_lo[:, :, 1, :].bitcast(F32), 0.0).then_inc(vt_edges, 1)
            dve.wait_ge(freed["act"], PLAN.free_of["forget", 0, 0][1] + 3)
            dve.scalar_tensor_tensor(out=lf_a[:, :], in0=lf_z[:, :], scalar=-1.0, in1=lf_z[:, :],
                                     op0=ALU.mult, op1=ALU.max).then_inc(az_done, 1)
            dve.wait_ge(l1_done, 1)
            dve.scalar_tensor_tensor(out=lf_a[:, :], in0=lf_z[:, :], scalar=0.0, in1=lf_a[:, :],
                                     op0=ALU.min, op1=ALU.subtract).then_inc(lf_done, 1)
            dve.memset(cum_one, 1.0).then_inc(lf_done, 1)
            dve.wait_ge(lf_done, 2)
            dve.tensor_tensor_scan(cum, cum_one, lf_a[:, 0:SEQ], 0.0, ALU.mult, ALU.add).then_inc(cum_done, 1)
            dve.wait_ge(nc_hi, 1)
            dve.scalar_tensor_tensor(out=ncum[32:32 + NHA, :], in0=cum, scalar=-1.0,
                                     in1=ncum[0:NHA, :].bitcast(F32), op0=ALU.mult,
                                     op1=ALU.subtract).then_inc(nc_done, 1)

        k_out, v_out, kf_done, vf_done, qs_done, vt_mm, vt_hi_done, vt_lo_done = (S(n) for n in (
            "k_out", "v_out", "kf_done", "vf_done", "qs_done", "vt_mm", "vt_hi_done", "vt_lo_done"))
        qk_hi, tok_mm, tok_done, tok_out, combined = (S(n) for n in (
            "qk_hi", "tok_mm", "tok_done", "tok_out", "combined"))
        FIRST_A = dict(fox=0, dil=PAIRS_A)

        def grouped(ap, dil, s0, w):
            return ap.rearrange("p (r a) -> p a r", r=dil)[:, s0 // dil:(s0 + w) // dil, :]

        def in_tokens(ap, dil):
            return ap.rearrange("p (a r) -> p a r", r=dil)

        def act_qkv(act, ph, i, lo, hi, dil):
            A0 = FIRST_A[ph]
            plain = isinstance(i, int)
            a0 = A0 + (i if plain else lo)
            for j in range(3):
                act_split(act, ph, i, j, lo, hi)
                if j == 0 and a0 == PAIRS_A + 3:
                    act.wait_ge(combined, 1)
                if j == 1 and a0 > 0:
                    act.wait_ge(k_out, lin(lambda s: 16 * (A0 + s), i, lo, hi))
                    act.wait_ge(v_out, lin(lambda s: 16 * (A0 + s), i, lo, hi))
                    act.wait_ge(tok_mm, lin(lambda s: A0 + s, i, lo, hi))
                for part, (s0, w) in enumerate(PARTS):
                    src = product(act, ph, i, j, part, lo, hi)
                    pw = min(w, SEQ - s0)
                    if j == 0:
                        if part == 2:
                            act.activation(q_s[:, :], src[:, pw:w], ACT.Copy, scale=SCALE).then_inc(qs_done, 1)
                        act.activation(grouped(q_hi[:, :], dil, s0, pw), in_tokens(src[:, 0:pw], dil), ACT.Copy,
                                       scale=SCALE).then_inc(qk_hi, 1)
                    if j == 1:
                        act.activation(k_f[:, s0:s0 + w], src, ACT.Copy).then_inc(kf_done, 1)
                        act.activation(grouped(k_hi[:, :], dil, s0, pw), in_tokens(src[:, 0:pw], dil),
                                       ACT.Copy).then_inc(qk_hi, 1)
                    if j == 2:
                        act.activation(v_f[:, s0:s0 + w], src, ACT.Copy).then_inc(vf_done, 1)
                        act.activation(grouped(v_g[:, :], dil, s0, pw), in_tokens(src[:, 0:pw], dil),
                                       ACT.Copy).then_inc(freed["act"], 1)
            act.wait_ge(tok_mm, lin(lambda s: A0 + s + 1, i, lo, hi))
            if a0 > 0:
                act.wait_ge(tok_out, lin(lambda s: 16 * (A0 + s), i, lo, hi))
            act.activation(tok[:, :, :], ps[0:NB, 5, 0:3 * P].rearrange("p (c f) -> p c f", c=3),
                           ACT.Copy).then_inc(tok_done, 1)
            for n in range(2):
                act.wait_ge(vt_mm, lin(lambda s: 2 * (A0 + s) + n + 1, i, lo, hi))
                act.activation(vt_hi[:, 4 * n:4 * n + 4, 0:3:2, :], bank(6 + n).rearrange("p (n h d) -> p n h d", h=2, d=HD),
                               ACT.Copy).then_inc(vt_hi_done, 1)

        def dve_qkv(dve, ph, i, lo, hi, dil):
            A0 = FIRST_A[ph]
            for j in range(3):
                dve_split(dve, ph, i, j, lo, hi)
                for part, (s0, w) in enumerate(PARTS):
                    pw = min(w, SEQ - s0)
                    if j < 2:
                        src = product(dve, ph, i, j, part, lo, hi)
                        dve.wait_ge(qk_hi, lin(lambda s: 6 * (A0 + s) + 3 * j + part + 1, i, lo, hi))
                    if j == 0:
                        dve.scalar_tensor_tensor(out=grouped(q_lo[:, :], dil, s0, pw),
                                                 in0=in_tokens(src[:, 0:pw], dil), scalar=SCALE,
                                                 in1=grouped(q_hi[:, :].bitcast(F32), dil, s0, pw),
                                                 op0=ALU.mult, op1=ALU.subtract).then_inc(freed["dve"], 1)
                    if j == 1:
                        dve.tensor_tensor(grouped(k_lo[:, :], dil, s0, pw), in_tokens(src[:, 0:pw], dil),
                                          grouped(k_hi[:, :].bitcast(F32), dil, s0, pw),
                                          ALU.subtract).then_inc(freed["dve"], 1)
            if A0 == 0 and isinstance(i, int) and i == 0:
                dve_bias(dve)
            for n in range(2):
                dve.wait_ge(vt_hi_done, lin(lambda s: 2 * (A0 + s) + n + 1, i, lo, hi))
                dve.tensor_tensor(vt_lo[:, 4 * n:4 * n + 4, 0:3:2, :],
                                  bank(6 + n).rearrange("p (n h d) -> p n h d", h=2, d=HD),
                                  vt_hi[:, 4 * n:4 * n + 4, 0:3:2, :].bitcast(F32), ALU.subtract).then_inc(vt_lo_done, 1)

        def pe_qkv(pe, ph, i, lo, hi):
            A0 = FIRST_A[ph]
            for j in range(3):
                pe_block(pe, ph, i, j, lo, hi, h_hi, h_lo)
            if A0 == 0 and isinstance(i, int) and i == 0:
                pe_bias(pe)
            pe.wait_ge(freed["dve"], lin(lambda s: PLAN.free_of[ph, s, 1][1] + 3, i, lo, hi))
            pe.wait_ge(freed["act"], lin(lambda s: PLAN.free_of[ph, s, 2][1] + 3, i, lo, hi))
            for n, src in enumerate((q_s[:, :], k_f[:, SEQ:T], v_f[:, SEQ:T])):
                last = pe.transpose(ps[0:NB, 5, n * P:(n + 1) * P], src, ident[:, :])
            last.then_inc(tok_mm, 1)
            for n in range(NQ):
                last = pe.transpose(ps[:, 6 + n // 4, (n % 4) * P:(n % 4 + 1) * P], v_g[:, n * P:(n + 1) * P],
                                    ident[:, :])
                if n % 4 == 3:
                    last.then_inc(vt_mm, 1)
            pe.wait_ge(vt_lo_done, lin(lambda s: 2 * (A0 + s) + 2, i, lo, hi))
            pe.wait_ge(tok_done, lin(lambda s: A0 + s + 1, i, lo, hi))

        sc_done, mx_done, ex_done, rs_done, tr_done, pth_done, ptl_done, ov_done, oev_done, psel_done = (
            S("fox_" + n) for n in ("scores", "max", "exp", "rsum", "turned", "pt_hi", "pt_lo", "ov",
                                    "ov_read", "pair_sel"))
        TILES = [(hh, 2 * b + odd) for hh, b, _ in UNITS for odd in range(2)]
        TURNS = [(s, half) for s, (_, i) in enumerate(TILES) for half in range(1 + (i >= 4))]
        N_TILE, N_TURN, N_OV = len(TILES), len(TURNS), len(UNITS)

        def with_ones(v, j, hh):
            return v[:, j, hh:hh + 2, :].rearrange("p a d -> p (a d)")

        def turns_of(s):
            return [(n, half) for n, (s_, half) in enumerate(TURNS) if s_ == s]

        def pe_fox(pe, p, lo, hi):
            def scores(s):
                hh, i = TILES[s]
                rows, n = slice(HD * hh, HD * hh + HD), P * (i + 1)
                if s >= 2:
                    pe.wait_ge(ex_done, lin(lambda x: N_TILE * x + s - 1, p, lo, hi))
                for c0 in range(0, n, 512):
                    c1 = min(c0 + 512, n)
                    out = ps[:, 2 * (s % 2) + c0 // 512, 0:c1 - c0]
                    qs = slice(i * P, (i + 1) * P)
                    pe.matmul(out, q_hi[rows, qs], k_hi[rows, c0:c1], start=True, stop=False)
                    pe.matmul(out, q_hi[rows, qs], k_lo[rows, c0:c1], start=False, stop=False)
                    pe.matmul(out, q_lo[rows, qs], k_hi[rows, c0:c1], start=False, stop=False)
                    if c1 == n:
                        pe.matmul(out[:, c1 - c0 - P:c1 - c0], ident_b[:, :], causal_b[:, :],
                                  start=False, stop=False, skip_group_check=True)
                    last = pe.matmul(out, pair_sel[:, hh, :], ncum[:, c0:c1], start=False, stop=True)
                last.then_inc(sc_done, 1)

            def turn(s):
                hh, i = TILES[s]
                pe.wait_ge(ex_done, lin(lambda x: N_TILE * x + s + 1, p, lo, hi))
                for e, half in turns_of(s):
                    if e >= 2:
                        pe.wait_ge(ptl_done, lin(lambda x: N_TURN * x + e - 1, p, lo, hi))
                    for n in range(4 * half, min(4 * half + 4, i + 1)):
                        last = pe.transpose(ps[:, 4 + e % 2, (n % 4) * P:(n % 4 + 1) * P],
                                            prob[:, s % 2, n * P:(n + 1) * P], ident[:, :])
                    last.then_inc(tr_done, 1)

            def values(u):
                hh, b, at = UNITS[u]
                i = 2 * b + 1
                pe.wait_ge(ptl_done, lin(lambda x: N_TURN * x + turns_of(2 * u + 1)[-1][0] + 1, p, lo, hi))
                if u >= 2:
                    pe.wait_ge(oev_done, lin(lambda x: N_OV * x + u - 1, p, lo, hi))
                for j in range(i + 1):
                    c0 = P if j == i else 0
                    out = ps[:, 6 + u % 2, c0:256]
                    for n, (v, t) in enumerate(((vt_hi, pt_hi), (vt_hi, pt_lo), (vt_lo, pt_hi))):
                        last = pe.matmul(out, with_ones(v, j, hh), t[:, at + j, c0:256], start=(j == 0 and n == 0),
                                         stop=(j == i and n == 2), skip_group_check=True)
                last.then_inc(ov_done, 1)

            pe.wait_ge(vt_edges, 2)
            pe.wait_ge(psel_done, lin(lambda x: x + 1, p, lo, hi))
            pe.wait_ge(nc_done, 1)
            scores(0)
            for s in range(N_TILE):
                if s + 1 < N_TILE:
                    scores(s + 1)
                turn(s)
                if s and s % 2 == 0:
                    values(s // 2 - 1)
            values(N_OV - 1)
            pe.wait_ge(oev_done, lin(lambda x: N_OV * x + N_OV, p, lo, hi))

        def act_fox(act, p, lo, hi):
            def exp(s):
                n = P * (TILES[s][1] + 1)
                act.wait_ge(mx_done, lin(lambda x: N_TILE * x + s + 1, p, lo, hi))
                act.activation(prob[:, s % 2, 0:n], psf[:, 1024 * (s % 2):1024 * (s % 2) + n], ACT.Exp,
                               bias=nmax[:, s % 2:s % 2 + 1]).then_inc(ex_done, 1)

            sel = head_sel[:, 2 * p:2 * p + 2] if isinstance(p, int) else head_sel[:, bass.ds(2 * p, 2)]
            act.wait_ge(const_in, 112)
            act.activation(pair_sel[:, :, :], sel.unsqueeze(2).broadcast_to([P, 2, P]), ACT.Copy).then_inc(psel_done, 1)
            exp(0)
            for s in range(N_TILE):
                if s + 1 < N_TILE:
                    if s >= 1:
                        act.wait_ge(tr_done, lin(lambda x: N_TURN * x + turns_of(s - 1)[-1][0] + 1, p, lo, hi))
                    exp(s + 1)
                i, at = TILES[s][1], UNITS[s // 2][2]
                if s >= 4 and s % 2 == 0:
                    act.wait_ge(ov_done, lin(lambda x: N_OV * x + s // 2 - 1, p, lo, hi))
                for e, half in turns_of(s):
                    nb = min(4, i + 1 - 4 * half)
                    act.wait_ge(tr_done, lin(lambda x: N_TURN * x + e + 1, p, lo, hi))
                    act.activation(pt_hi[:, at + 4 * half:at + 4 * half + nb, (i % 2) * P:(i % 2 + 1) * P],
                                   bank(4 + e % 2, nb * P).rearrange("p (n c) -> p n c", c=P),
                                   ACT.Copy).then_inc(pth_done, 1)

        def dve_fox(dve, p, lo, hi):
            def biggest(s):
                n = P * (TILES[s][1] + 1)
                dve.wait_ge(sc_done, lin(lambda x: N_TILE * x + s + 1, p, lo, hi))
                dve.tensor_reduce(nmax[:, s % 2:s % 2 + 1], psf[:, 1024 * (s % 2):1024 * (s % 2) + n], AX.X,
                                  ALU.max, negate=True).then_inc(mx_done, 1)

            def out(u):
                hh, b, _ = UNITS[u]
                rows, others = slice(HD * hh, HD * hh + HD), slice(HD - HD * hh, P - HD * hh)
                dve.wait_ge(ov_done, lin(lambda x: N_OV * x + u + 1, p, lo, hi))
                dve.reciprocal(rsum[rows, :], ps[others, 6 + u % 2, 0:256]).then_inc(rs_done, 1)
                dve.wait_ge(rs_done, lin(lambda x: N_OV * x + u + 1, p, lo, hi))
                dst = o_st[rows, p, 256 * b:256 * (b + 1)] if isinstance(p, int) else \
                    o_st[rows, bass.ds(p, 1), 256 * b:256 * (b + 1)].rearrange("p a c -> p (a c)")
                dve.tensor_tensor(dst, ps[rows, 6 + u % 2, 0:256], rsum[rows, :], ALU.mult).then_inc(oev_done, 1)

            biggest(0)
            for s in range(N_TILE):
                if s + 1 < N_TILE:
                    biggest(s + 1)
                i, at = TILES[s][1], UNITS[s // 2][2]
                for e, half in turns_of(s):
                    nb = min(4, i + 1 - 4 * half)
                    sl = (slice(None), slice(at + 4 * half, at + 4 * half + nb), slice((i % 2) * P, (i % 2 + 1) * P))
                    dve.wait_ge(pth_done, lin(lambda x: N_TURN * x + e + 1, p, lo, hi))
                    dve.tensor_tensor(pt_lo[sl], bank(4 + e % 2, nb * P).rearrange("p (n c) -> p n c", c=P),
                                      pt_hi[sl].bitcast(F32), ALU.subtract).then_inc(ptl_done, 1)
                if s and s % 2:
                    if s >= 3:
                        out(s // 2 - 1)
            out(N_OV - 1)

        d_sc, d_mt, d_mx, d_ex, d_tr, d_pth, d_ptl, d_ov, d_oev, bias_in = (S("dil_" + n) for n in (
            "scores", "biased", "max", "exp", "turned", "pt_hi", "pt_lo", "ov", "ov_read", "bias"))

        def has_prev(g, n):
            per = SEQ // DIL[g] // P
            return per > 0 and n % per != 0

        def pe_dil(pe, d, g):
            def scores(s):
                hh, n = s // NQ, s % NQ
                rows = slice(HD * hh, HD * hh + HD)
                if s >= 4:
                    pe.wait_ge(d_mt, 16 * d + s - 3)
                k0, c0 = ((n - 1) * P, 0) if has_prev(g, n) else (n * P, P)
                out = ps[:, s % 4, c0:256]
                for m, (a, b) in enumerate(((q_hi, k_hi), (q_hi, k_lo), (q_lo, k_hi))):
                    last = pe.matmul(out, a[rows, n * P:(n + 1) * P], b[rows, k0:(n + 1) * P],
                                     start=(m == 0), stop=(m == 2))
                last.then_inc(d_sc, 1)

            def turn(s):
                n = s % NQ
                pe.wait_ge(d_ex, 16 * d + s + 1)
                if s >= 2:
                    pe.wait_ge(d_ptl, 16 * d + s - 1)
                for c0 in ((0, P) if has_prev(g, n) else (P,)):
                    last = pe.transpose(ps[:, 4 + s % 2, c0:c0 + P], prob_b[:, s % 4, c0:c0 + P], ident[:, :])
                last.then_inc(d_tr, 1)

            def values(hh):
                pe.wait_ge(d_ptl, 16 * d + NQ * (hh + 1))
                if hh:
                    pe.wait_ge(d_oev, 2 * d + hh)
                begun = set()
                for j in range(NQ):
                    end = j + 1 + (j + 1 < NQ and has_prev(g, j + 1))
                    for b0, b1 in ([(j, end)] if j // 4 == (end - 1) // 4 else [(j, j + 1), (j + 1, end)]):
                        out = ps[:, 6 + b0 // 4, (b0 % 4) * P:(b0 % 4) * P + (b1 - b0) * P]
                        cs = slice((b0 - j) * P, (b1 - j) * P)
                        for v, t in ((vt_hi, pt_hi), (vt_hi, pt_lo), (vt_lo, pt_hi)):
                            last = pe.matmul(out, with_ones(v, j, hh), t[:, j, cs], start=(b0 // 4 not in begun),
                                             stop=True, skip_group_check=True)
                            begun.add(b0 // 4)
                last.then_inc(d_ov, 1)

            for s in range(3):
                scores(s)
            for s in range(16):
                if s + 3 < 16:
                    scores(s + 3)
                turn(s)
                if s % NQ == NQ - 1:
                    values(s // NQ)
            pe.wait_ge(d_oev, 2 * d + 2)

        def act_dil(act, d, g):
            def exp(s):
                hh, n = s // NQ, s % NQ
                c0 = 0 if has_prev(g, n) else P
                act.wait_ge(d_mx, 16 * d + s + 1)
                if s >= 4:
                    act.wait_ge(d_tr, 16 * d + s - 3)
                act.activation(prob_b[:, s % 4, c0:256], score_b[:, s % 4, c0:256], ACT.Exp,
                               bias=nmx[:, g, hh, n:n + 1], accum_out=den[:, g, hh, n:n + 1]).then_inc(d_ex, 1)

            def out(hh):
                rows = slice(HD * hh, HD * hh + HD)
                act.wait_ge(d_ov, 2 * d + hh + 1)
                act.activation(o_g[rows, g, :], psf[rows, 6 * 512:8 * 512], ACT.Copy).then_inc(d_oev, 1)

            ptf = pt_hi[:, :, :].rearrange("p n c -> p (n c)")
            exp(0)
            for s in range(16):
                if s + 1 < 16:
                    exp(s + 1)
                n = s % NQ
                if s == NQ:
                    out(0)
                w = 256 if has_prev(g, n) else P
                act.wait_ge(d_tr, 16 * d + s + 1)
                act.activation(ptf[:, n * 256 + P - w:n * 256 + P], ps[:, 4 + s % 2, 256 - w:256],
                               ACT.Copy).then_inc(d_pth, 1)
            out(1)

        def dve_dil(dve, d, g):
            def biased(s):
                hh, n = s // NQ, s % NQ
                c0 = 0 if has_prev(g, n) else P
                if s == 0:
                    dve.wait_ge(S(f"bias_dma{d % 2}"), 32 * (d // 2 + 1))
                    if g == 2:
                        dve.wait_ge(bias_in, d // 3 + 1)
                dve.wait_ge(d_sc, 16 * d + s + 1)
                if s >= 4:
                    dve.wait_ge(d_ex, 16 * d + s - 3)
                dve.tensor_tensor_reduce(score_b[:, s % 4, c0:256], ps[:, s % 4, c0:256],
                                         bias_t[:, d % 2, hh, c0:256], 1.0, -3.0e38, ALU.add, ALU.max,
                                         mx[:, g, hh, n:n + 1]).then_inc(d_mt, 1)
                dve.wait_ge(d_mt, 16 * d + s + 1)
                dve.tensor_scalar(nmx[:, g, hh, n:n + 1], mx[:, g, hh, n:n + 1], -1.0, None,
                                  ALU.mult).then_inc(d_mx, 1)

            lof = pt_lo[:, :, :].rearrange("p n c -> p (n c)")
            hif = pt_hi[:, :, :].rearrange("p n c -> p (n c)").bitcast(F32)
            biased(0)
            biased(1)
            for s in range(16):
                if s + 2 < 16:
                    biased(s + 2)
                n = s % NQ
                w = 256 if has_prev(g, n) else P
                sl = slice(n * 256 + P - w, n * 256 + P)
                dve.wait_ge(d_pth, 16 * d + s + 1)
                dve.tensor_tensor(lof[:, sl], ps[:, 4 + s % 2, 256 - w:256], hif[:, sl],
                                  ALU.subtract).then_inc(d_ptl, 1)

        wide_set, wide_mm, m_ev, w_sub, w_exp, cb_step = (S("cb_" + n) for n in (
            "wide", "spread", "max_ev", "sub", "exp", "step"))

        def pe_combine(pe, pair):
            for kind in range(2):
                for g in range(3):
                    pe.wait_ge(wide_set, 6 * pair + 3 * kind + g + 1)
                    if kind:
                        pe.wait_ge(m_ev, 3 * pair + g + 1)
                    for n in range(NQ):
                        last = pe.matmul(ps[:, 2 * g + n // 4, (n % 4) * P:(n % 4 + 1) * P],
                                         wide[:, n, :, :].rearrange("p h d -> p (h d)"), ident[:, :],
                                         start=True, stop=True)
                    last.then_inc(wide_mm, 1)
            pe.wait_ge(combined, pair + 1)

        def group_view(g, ap):
            return ap.rearrange("p (r a) -> p a r", r=DIL[g])

        def act_combine(act, pair):
            for g in range(3):
                act.wait_ge(wide_mm, 6 * pair + g + 1)
                act.activation(in_tokens(wg[:, g, :], DIL[g]), group_view(g, psf[:, 1024 * g:1024 * (g + 1)]),
                               ACT.Copy).then_inc(m_ev, 1)
            act.wait_ge(w_sub, pair + 1)
            act.activation(wg[:, :, :], wg[:, :, :], ACT.Exp).then_inc(w_exp, 1)

        def dve_combine(dve, pair):
            cnt = [13 * pair]

            def link(ins):
                cnt[0] += 1
                ins.then_inc(cb_step, 1)
                dve.wait_ge(cb_step, cnt[0])

            dve.wait_ge(d_ex, 16 * 3 * (pair + 1))
            for kind, src in enumerate((mx, den)):
                for g in range(3):
                    if kind + g:
                        dve.wait_ge(wide_mm, 6 * pair + 3 * kind + g)
                    dve.tensor_copy(wide[:, :, :, :], src[:, g, :, :].rearrange("p h n -> p n h").unsqueeze(3)
                                    .broadcast_to([P, NQ, 2, HD])).then_inc(wide_set, 1)
                if kind == 0:
                    dve.wait_ge(m_ev, 3 * pair + 3)
                    dve.wait_ge(k_out, 16 * (PAIRS_A + 3 * pair + 3))
                    dve.wait_ge(v_out, 16 * (PAIRS_A + 3 * pair + 3))
                    link(dve.tensor_tensor(mxall, wg[:, 0, :], wg[:, 1, :], ALU.max))
                    link(dve.tensor_tensor(mxall, mxall, wg[:, 2, :], ALU.max))
                    dve.tensor_tensor(wg[:, :, :], wg[:, :, :], mxall.unsqueeze(1).broadcast_to([P, 3, SEQ]),
                                      ALU.subtract).then_inc(w_sub, 1)
                    dve.wait_ge(w_sub, pair + 1)
            dve.wait_ge(w_exp, pair + 1)
            for g in range(3):
                dve.wait_ge(wide_mm, 6 * pair + 4 + g)
                dst = mxall if g else tsum
                link(dve.tensor_tensor(in_tokens(dst, DIL[g]), in_tokens(wg[:, g, :], DIL[g]),
                                       group_view(g, psf[:, 1024 * g:1024 * (g + 1)]), ALU.mult))
                if g:
                    link(dve.tensor_tensor(tsum, tsum, mxall, ALU.add))
            link(dve.reciprocal(tsum, tsum))
            link(dve.tensor_tensor(wg[:, :, :], wg[:, :, :], tsum.unsqueeze(1).broadcast_to([P, 3, SEQ]), ALU.mult))
            dve.wait_ge(d_oev, 2 * 3 * (pair + 1))
            for g in range(3):
                link(dve.tensor_tensor(in_tokens(wg[:, g, :], DIL[g]), in_tokens(wg[:, g, :], DIL[g]),
                                       group_view(g, o_g[:, g, :]), ALU.mult))
            link(dve.tensor_tensor(wg[:, 0, :], wg[:, 0, :], wg[:, 1, :], ALU.add))
            dve.tensor_tensor(o_st[:, PAIRS_A + pair, 0:SEQ], wg[:, 0, :], wg[:, 2, :], ALU.add)\
                .then_inc(combined, 1)

        kc_in = [S("kc_in0"), S("kc_in1")]
        kc_used, kc_zero, s_in, s_dot, s_step, s_rows, s_mm, s_ev, p_ready, v_mul, v_mm, s_out = (S("smp_" + n) for n in (
            "kc_used", "kc_zero", "in", "dot", "step", "rows", "mm", "ev", "p_ready", "v_mul", "v_mm", "out"))
        lf_out = S("lf_out")
        A_LAST = PAIRS_A + 3 * PAIRS_B

        def pool_cache(pool, kv):
            def load(b, slot):
                if kv and b >= 2:
                    pool.wait_ge(v_mm, b - 1)
                elif kv or b >= 2:
                    pool.wait_ge(kc_used, NB * kv + b - 1)
                if isinstance(b, int):
                    bsl = lambda t: t[b:b + 1]
                else:
                    bsl = lambda t: t[bass.ds(b, 1)]
                src = A["cache_a_v"] if kv else A["cache_a_k"]
                for pg in range(NPAGE):
                    page = pool.value_load(pages[0:1, bass.ds(b * NPAGE + pg, 1)] if not isinstance(b, int) else
                                           pages[0:1, b * NPAGE + pg:b * NPAGE + pg + 1],
                                           min_val=0, max_val=A["cache_a_k"].shape[0] - 1)
                    pool.dma_start(kc_a[:, slot, pg, :], src[bass.ds(page, 1)].rearrange("a p c -> (a p) c")
                                   ).then_inc(kc_in[slot], 16)
                    if not kv:
                        dst = lfp[:, pg, b, :] if isinstance(b, int) else \
                            lfp[:, pg, bass.ds(b, 1), :].rearrange("p a c -> p (a c)")
                        pool.dma_start(dst, A["cache_a_logf"][bass.ds(page, 1)].rearrange("a p c -> (a p) c")
                                       ).then_inc(kc_in[slot], 16)
                for g, (name, n) in enumerate(zip(("b1", "b2", "b3"), SAMPLE_KEYS)):
                    cache = A["cache_" + name]
                    step = cache.shape[1] // n
                    one = bsl(cache).rearrange("a (n s) c -> (a n) s c", s=step)[:, 0, kv * 256:(kv + 1) * 256]
                    pool.dma_start(kc_b[0:n, slot, g, :], one).then_inc(kc_in[slot], 16)
                if not kv:
                    pool.dma_start(qb[:, slot, :], bsl(qkv_s)[:, 0, :].broadcast_to([P, WA + WB])
                                   ).then_inc(kc_in[slot], 16)
            for b in range(NB):
                load(b, b % 2)

        def pool_samples(pool):
            pool.wait_ge(tok_out, 16 * A_LAST)
            pool.wait_ge(lf_out, 16)
            pool.wait_ge(combined, PAIRS_B)
            pool.wait_ge(tok_done, A_LAST)
            pool.dma_start(kn[:, :], qkv_s[:, 1, :]).then_inc(s_in, 16)
            pool.dma_start(vn[:, :], qkv_s[:, 2, :]).then_inc(s_in, 16)
            pool.dma_start(lf_new[:, :], A["lf_t"][:, SEQ:T].rearrange("h b -> b h").unsqueeze(2),
                           allow_slow_non_contiguous=True).then_inc(s_in, 16)
            pool.dma_start(upto[:, :], A["upto"]).then_inc(s_in, 16)
            pool.dma_start(own_a[:, :], A["own_a"]).then_inc(s_in, 16)
            pool.dma_start(own_b[:, :], A["own_b"]).then_inc(s_in, 16)
            pool.dma_start(head_a[:, :], A["head_a"]).then_inc(s_in, 16)
            pool.dma_start(head_b[:, :], A["head_b"]).then_inc(s_in, 16)
            pool.memset(kc_b[:, :, :, :], 0.0).then_inc(kc_zero, 1)
            pool.memset(p_a[:, :, :], 0.0).then_inc(kc_zero, 1)
            pool.memset(p_b[:, :, :], 0.0).then_inc(kc_zero, 1)
            pool.wait_ge(kc_zero, 3)
            pool_cache(pool, 0)
            pool_cache(pool, 1)

        K_IN, V_IN = 16 * (2 * NPAGE + 3 + 1), 16 * (NPAGE + 3)

        def dve_gates(dve):
            cnt = [0]

            def dot(b, slot, i):
                dve.wait_ge(kc_in[slot], i * K_IN + K_IN)
                s3 = (lambda t, n: t[:, :, b, :]) if isinstance(b, int) else \
                    (lambda t, n: t[:, :, bass.ds(b, 1), :].rearrange("p g a h -> p g (a h)"))
                s2 = (lambda t: t[:, b, :]) if isinstance(b, int) else \
                    (lambda t: t[:, bass.ds(b, 1), :].rearrange("p a h -> p (a h)"))
                dve.tensor_tensor(prod[:, 0:NPAGE * WA].rearrange("p (g c) -> p g c", c=WA), kc_a[:, slot, :, :],
                                  qb[:, slot, 0:WA].unsqueeze(1).broadcast_to([P, NPAGE, WA]), ALU.mult)
                dve.tensor_tensor(prod[:, NPAGE * WA:NPAGE * WA + WB],
                                  kc_b[:, slot, :, :].rearrange("p g c -> p (g c)"), qb[:, slot, WA:WA + WB], ALU.mult)
                dve.tensor_tensor(prn[:, :], kn[:, :], qb[0:NB, slot, :], ALU.mult).then_inc(s_dot, 1)
                dve.wait_ge(s_dot, lin(lambda s: 2 * s + (slot + 1), i, 1, NB // 2))
                dve.tensor_reduce(s3(s_a, 0), prod[:, 0:NPAGE * WA].rearrange("p (g h d) -> p g h d", g=NPAGE, d=HD),
                                  AX.X, ALU.add)
                dve.tensor_reduce(s3(s_b, 0), prod[:, NPAGE * WA:].rearrange("p (g h d) -> p g h d", g=3, d=HD),
                                  AX.X, ALU.add)
                dve.tensor_reduce(s2(sn_a), prn[:, 0:WA].rearrange("p (h d) -> p h d", d=HD), AX.X, ALU.add)
                dve.tensor_reduce(s3(sn_b, 0), prn[:, WA:].rearrange("p (g h d) -> p g h d", g=3, d=HD),
                                  AX.X, ALU.add).then_inc(kc_used, 1)
                dve.wait_ge(kc_used, lin(lambda s: 2 * s + (slot + 1), i, 1, NB // 2))

            def link(ins):
                cnt[0] += 1
                ins.then_inc(s_step, 1)
                dve.wait_ge(s_step, cnt[0])

            for n in range(ROWS + 1):
                dve_split(dve, "gates", 0, n, 0, 1)
                if n == 1:
                    dve.wait_ge(s_in, 128)
                for b in DOTS.get(n, ()):
                    dot(b, b % 2, b // 2)
            link(dve.tensor_tensor(s_b[:, :, :, :], s_b[:, :, :, :],
                                   bs[:, :, :].unsqueeze(2).broadcast_to([P, 3, NB, HPG]), ALU.add))
            dve.tensor_tensor(sn_b[:, :, :, :], sn_b[:, :, :, :],
                              bn[:, :, :].unsqueeze(2).broadcast_to([NB, 3, NB, HPG]), ALU.add).then_inc(s_rows, 1)
            dve_split(dve, "gates", 0, ROWS + 1, 0, 1)
            dve.wait_ge(s_ev, 1)
            dve.wait_ge(s_mm, 1)
            link(dve.tensor_tensor(cols[:, 0:1], crow[:, 255:256], lf_new[:, :], ALU.add))
            link(dve.tensor_scalar(crow[:, :], crow[:, :], cols[:, 0:1], -1.0, ALU.subtract, ALU.mult))
            link(dve.tensor_tensor(row_a[:, 0:256], row_a[:, 0:256], crow[:, :], ALU.add))
            link(dve.tensor_tensor(row_a[:, 256:264], row_a[:, 256:264], own_a[:, :], ALU.add))
            link(dve.tensor_tensor(row_b[:, 384:408].rearrange("p (g b) -> p g b", g=3),
                                   row_b[:, 384:408].rearrange("p (g b) -> p g b", g=3),
                                   own_b[:, :].unsqueeze(1).broadcast_to([32, 3, NB]), ALU.add))
            link(dve.tensor_reduce(cols[:, 1:2], row_a[:, :], AX.X, ALU.max, negate=True))
            dve.tensor_reduce(cols[0:32, 2:3], row_b[:, :], AX.X, ALU.max, negate=True).then_inc(s_rows, 1)
            dve.wait_ge(s_ev, 3)
            link(dve.reciprocal(cols[:, 5:6], cols[:, 3:4]))
            link(dve.reciprocal(cols[0:32, 6:7], cols[0:32, 4:5]))
            dve.tensor_scalar(row_a[:, :], row_a[:, :], cols[:, 5:6], None, ALU.mult)
            dve.tensor_scalar(row_b[:, :], row_b[:, :], cols[0:32, 6:7], None, ALU.mult).then_inc(s_rows, 1)

            for n in range(ROWS + 2, 2 * KD):
                dve_split(dve, "gates", 0, n, 0, 1)
                if n == VALUES_END:
                    dve.wait_ge(v_mm, NB)
                    dve.tensor_tensor(masked[:, 0:WA].rearrange("p (h d) -> p h d", d=HD),
                                      ps[0:64, 7, 0:WA].rearrange("p (h d) -> p h d", d=HD),
                                      head_a[:, :].unsqueeze(2).broadcast_to([64, NHA, HD]), ALU.mult)
                    link(dve.tensor_tensor(masked[0:32, WA:].rearrange("p (h d) -> p h d", d=HD),
                                           ps[0:32, 6, 0:256].rearrange("p (h d) -> p h d", d=HD),
                                           head_b[:, :].unsqueeze(2).broadcast_to([32, HPG, HD]), ALU.mult))
                    dve.tensor_reduce(o_rows[:, 0, :], masked[:, 0:WA].rearrange("p (h d) -> p d h", d=HD),
                                      AX.X, ALU.add)
                    dve.tensor_reduce(o_rows[0:32, 1, :], masked[0:32, WA:].rearrange("p (h d) -> p d h", d=HD),
                                      AX.X, ALU.add).then_inc(o_rows_done, 1)

        DOTS = {1: (0,), 2: (1, 2), 3: (3,), 4: (4, 5), 5: (6,), 6: (7,)}
        ROWS = 8
        VALUES = {10: (0, 1), 11: (2, 3), 12: (4,), 13: (5, 6), 14: (7,)}
        VALUES_END = 14
        o_rows_done = S("smp_o_rows")

        def flat(t):
            return t.rearrange("p b h -> p (b h)")

        def pe_rows(pe):
            pe.wait_ge(s_rows, 1)
            for pg in range(NPAGE):
                pe.transpose(ps[0:64, 6, 256 + pg * P:256 + (pg + 1) * P], flat(s_a[:, pg, :, :]), ident[:, :])
            pe.transpose(ps[0:64, 7, 408:416], flat(sn_a[:, :, :]), ident[0:NB, 0:NB])
            for g in range(3):
                pe.transpose(ps[0:32, 7, g * P:(g + 1) * P], flat(s_b[:, g, :, :]), ident[:, :])
                pe.transpose(ps[0:32, 7, 384 + g * NB:384 + (g + 1) * NB], flat(sn_b[:, g, :, :]),
                             ident[0:NB, 0:NB])
            pe.matmul(ps[0:64, 6, 0:P], flat(lfp[:, 0, :, :]), upto[:, :], start=True, stop=True)
            pe.matmul(ps[0:64, 6, P:2 * P], flat(lfp[:, 0, :, :]), ones[:, :], start=True, stop=False)
            pe.matmul(ps[0:64, 6, P:2 * P], flat(lfp[:, 1, :, :]), upto[:, :], start=False,
                      stop=True).then_inc(s_mm, 1)

        def pe_columns(pe):
            pe.wait_ge(s_rows, 3)
            i64, i32 = ident[0:64, 0:64], ident[0:32, 0:32]
            for pg in range(NPAGE):
                pe.transpose(ps[:, 6, pg * 64:(pg + 1) * 64], row_a[:, pg * P:(pg + 1) * P], i64)
            pe.transpose(ps[0:NB, 6, 256:320], row_a[:, 256:264], i64)
            for g in range(3):
                pe.transpose(ps[:, 6, P + g * 32:P + (g + 1) * 32], row_b[:, g * P:(g + 1) * P], i32)
                last = pe.transpose(ps[0:NB, 6, 320 + g * 32:352 + g * 32],
                                    row_b[:, 384 + g * NB:384 + (g + 1) * NB], i32)
            last.then_inc(s_mm, 1)

        def pe_values(pe, b):
            if b == 0:
                pe.wait_ge(p_ready, 1)
                pe.matmul(ps[0:64, 7, 0:WA], flat(pn_a[:, :, :]), vn[:, 0:WA], start=True, stop=False)
                for g in range(3):
                    pe.matmul(ps[0:32, 6, 0:256], flat(pn_b[:, g, :, :]), vn[:, WA + g * 256:WA + (g + 1) * 256],
                              start=(g == 0), stop=False)
            pe.wait_ge(kc_in[b % 2], NB // 2 * K_IN + (b // 2 + 1) * V_IN)
            end = b == NB - 1
            for pg in range(NPAGE):
                pe.matmul(ps[0:64, 7, 0:WA], p_a[:, pg, b * 64:(b + 1) * 64], kc_a[:, b % 2, pg, :],
                          start=False, stop=(end and pg == NPAGE - 1))
            for g in range(3):
                last = pe.matmul(ps[0:32, 6, 0:256], p_b[:, g, b * 32:(b + 1) * 32], kc_b[:, b % 2, g, :],
                                 start=False, stop=(end and g == 2))
            last.then_inc(v_mm, 1)

        def pe_gates(pe):
            for n in range(2 * KD):
                pe_block(pe, "gates", 0, n, 0, 1, h_hi, h_lo)
                if n == ROWS:
                    pe_rows(pe)
                if n == ROWS + 1:
                    pe_columns(pe)
                for b in VALUES.get(n, ()):
                    pe_values(pe, b)
            pe.wait_ge(o_rows_done, 1)
            pe.transpose(ps[0:HD, 6, 0:64], o_rows[:, 0, :], ident[0:64, 0:64])
            pe.transpose(ps[0:HD, 6, 64:96], o_rows[0:32, 1, :], ident[0:32, 0:32]).then_inc(s_mm, 1)

        def act_rows(act):
            act.wait_ge(s_mm, 1)
            act.activation(row_a[:, 0:256], ps[0:64, 6, 256:512], ACT.Copy)
            act.activation(row_a[:, 256:264], ps[0:64, 7, 408:416], ACT.Copy)
            act.activation(crow[:, :], ps[0:64, 6, 0:256], ACT.Copy)
            act.activation(row_b[:, :], ps[0:32, 7, 0:408], ACT.Copy).then_inc(s_ev, 1)
            act.wait_ge(s_rows, 2)
            act.activation(row_a[:, :], row_a[:, :], ACT.Exp, bias=cols[:, 1:2],
                           accum_out=cols[:, 3:4]).then_inc(s_ev, 1)
            act.activation(row_b[:, :], row_b[:, :], ACT.Exp, bias=cols[0:32, 2:3],
                           accum_out=cols[0:32, 4:5]).then_inc(s_ev, 1)

        def act_columns(act):
            act.wait_ge(s_mm, 2)
            act.wait_ge(kc_zero, 3)
            act.activation(p_a[:, :, :].rearrange("p g (b c) -> p g b c", c=72)[:, :, :, 0:NHA],
                           ps[:, 6, 0:P].rearrange("p (g b h) -> p g b h", g=2, h=NHA), ACT.Copy)
            act.activation(p_b[:, :, :].rearrange("p g (b c) -> p g b c", c=36)[:, :, :, 0:HPG],
                           ps[:, 6, P:P + 96].rearrange("p (g b h) -> p g b h", g=3, h=HPG), ACT.Copy)
            act.activation(pn_a[:, :, :], ps[0:NB, 6, 256:320].rearrange("p (b h) -> p b h", h=NHA), ACT.Copy)
            act.activation(pn_b[:, :, :, :], ps[0:NB, 6, 320:416].rearrange("p (g b h) -> p g b h", g=3, h=HPG),
                           ACT.Copy).then_inc(p_ready, 1)

        z_done = S("mg_z")
        g_out = [S(f"gate_out{n}") for n in range(GATE_SLOTS)]
        g_in = [S(f"gate_in{n}") for n in range(2)]

        def act_gates(act):
            act.wait_ge(combined, PAIRS_B)
            for n in range(2 * KD):
                act_split(act, "gates", 0, n, 0, 1)
                if n == ROWS + 1:
                    act_rows(act)
                if n == ROWS + 2:
                    act_columns(act)
                if n >= GATE_SLOTS:
                    act.wait_ge(g_out[n % GATE_SLOTS], 16 * (n // GATE_SLOTS))
                for part, (s0, w) in enumerate(PARTS):
                    act.activation(gate_st[:, n % GATE_SLOTS, s0:s0 + w], product(act, "gates", 0, n, part, 0, 1),
                                   ACT.Sigmoid).then_inc(freed["act"], 1)
                act.wait_ge(freed["act"], PLAN.free_of["gates", 0, n][1] + 3)
                act.dma_start(gates_s[n], gate_st[:, n % GATE_SLOTS, :]).then_inc(g_out[n % GATE_SLOTS], 16)
            act.wait_ge(s_mm, 3)
            for hh in range(2):
                rows = slice(HD * hh, HD * hh + HD)
                for c0, n, h, t0 in ((0, 64, NHA, 0), (64, 32, HPG, PAIRS_A)):
                    last = act.activation(o_st[rows, t0:t0 + h // 2, SEQ:T],
                                          ps[0:HD, 6, c0:c0 + n].rearrange("d (b t h) -> d t b h", t=h // 2, h=2)
                                          [:, :, :, hh], ACT.Copy)
            last.then_inc(s_out, 1)

        o_hi_done, o_lo_done = S("mg_o_hi"), S("mg_o_lo")
        z_hi_done, z_lo_done = S("mg_z_hi"), S("mg_z_lo")
        z_hi, z_lo = h_hi, h_lo

        def pe_merge(pe):
            for i in range(PROJ_ITERS):
                for j in range(8):
                    a, b = (o_hi[:, PAIRS_A:, :], o_lo[:, PAIRS_A:, :]) if j % 2 else (o_hi, o_lo)
                    pe_block(pe, "proj", i, j, i, i + 1, a, b,
                             None if i or j else lambda part: pe.wait_ge(o_lo_done, part + 1))
            for j in range(KD):
                pe_block(pe, "out", 0, j, 0, 1, z_hi, z_lo,
                         None if j else lambda part: pe.wait_ge(z_lo_done, 3 * (KD - 1) + part + 1))

        PROJ_SPLITS = {0: 0, 4: 1, 7: 2}

        def pool_gates(pool):
            for out in g_out:
                pool.wait_ge(out, 16 * 2 * KD // GATE_SLOTS)
            pool.wait_ge(s_out, 1)
            for m in range(KD):
                if m >= 2:
                    pool.wait_ge(z_done, 3 * (m - 1))
                pool.dma_start(gate_in[:, m % 2, :, :],
                               gates_s.rearrange("(a m) p t -> m p a t", a=2)[m]).then_inc(g_in[m % 2], 16)

        def act_merge(act):
            for i in range(PROJ_ITERS):
                for j in range(8):
                    if j in PROJ_SPLITS:
                        act_split(act, "proj", i, PROJ_SPLITS[j], i, i + 1)
                    if j % 2:
                        m = 4 * i + j // 2
                        for part, (s0, w) in enumerate(PARTS):
                            act.wait_ge(z_done, 3 * m + part + 1)
                            act.activation(z_hi[:, m, s0:s0 + w], z_f[:, m % 2, s0:s0 + w],
                                           ACT.Copy).then_inc(z_hi_done, 1)
            for j in range(KD):
                act_split(act, "out", 0, j, 0, 1)
                act_post_square(act, 3, j)

        def dve_merge(dve):
            for i in range(PROJ_ITERS):
                for j in range(8):
                    if j in PROJ_SPLITS:
                        dve_split(dve, "proj", i, PROJ_SPLITS[j], i, i + 1)
                    m = 4 * i + j // 2
                    free = PLAN.free_of["proj", i, j][1]
                    if j % 2 == 0:
                        dve.wait_ge(g_in[m % 2], 16 * (m // 2 + 1))
                        if m >= 2:
                            dve.wait_ge(z_lo_done, 3 * (m - 1))
                        for part, (s0, w) in enumerate(PARTS):
                            dve.tensor_tensor(z_f[:, m % 2, s0:s0 + w], product(dve, "proj", i, j, part, i, i + 1),
                                              gate_in[:, m % 2, 0, s0:s0 + w], ALU.mult).then_inc(freed["dve"], 1)
                        continue
                    for part, (s0, w) in enumerate(PARTS):
                        g = gate_in[:, m % 2, 1, s0:s0 + w]
                        dve.tensor_tensor(g, product(dve, "proj", i, j, part, i, i + 1), g,
                                          ALU.mult).then_inc(freed["dve"], 1)
                    for part, (s0, w) in enumerate(PARTS):
                        z = z_f[:, m % 2, s0:s0 + w]
                        dve.wait_ge(freed["dve"], free + part + 1)
                        dve.tensor_tensor(z, z, gate_in[:, m % 2, 1, s0:s0 + w], ALU.add).then_inc(z_done, 1)
                    for part, (s0, w) in enumerate(PARTS):
                        dve.wait_ge(z_hi_done, 3 * m + part + 1)
                        dve.tensor_tensor(z_lo[:, m, s0:s0 + w], z_f[:, m % 2, s0:s0 + w],
                                          z_hi[:, m, s0:s0 + w].bitcast(F32), ALU.subtract).then_inc(z_lo_done, 1)
            for j in range(KD):
                dve_split(dve, "out", 0, j, 0, 1)
                for part, (s0, w) in enumerate(PARTS):
                    dve.tensor_copy(acc[:, j, s0:s0 + w], product(dve, "out", 0, j, part, 0, 1)
                                    ).then_inc(freed["dve"], 1)
                if j:
                    dve_post_add(dve, 3, j - 1)
            dve_post_add(dve, 3, KD - 1)

        block = ctx.enter_context(nc.Block())

        @block.sync
        def _(sp):
            for n in range(RING):
                sp.dma_start(w_raw[:, n, :], A["w_chunks"][n]).then_inc(w_loaded[n], 16)
            with sp.Fori(1, PLAN.chunks // RING) as i:
                for n in range(RING):
                    sp.wait_ge(w_lo_done, RING * i + (n - RING + 1))
                    sp.dma_start(w_raw[:, n, :], A["w_chunks"][bass.ds(RING * i + n, 1)]
                                 .rearrange("a p c -> (a p) c")).then_inc(w_loaded[n], 16)
            for n in range(PLAN.chunks // RING * RING, PLAN.chunks):
                sp.wait_ge(w_lo_done, n - RING + 1)
                sp.dma_start(w_raw[:, n % RING, :], A["w_chunks"][n]).then_inc(w_loaded[n % RING], 16)

        @block.gpsimd
        def _(pool):
            pool.memset(ones[:, :], 1.0).then_inc(S("ones_set"), 1)
            pool.memset(eps_c[:, :], EPS).then_inc(S("ones_set"), 1)
            pool.memset(one_c[:, :], 1.0).then_inc(S("ones_set"), 1)
            pool.wait_ge(S("ones_set"), 3)
            pool.memset(rb[N_BUCKETS:N_BUCKETS + 1, :], 1.0).then_inc(S("rb_one"), 1)
            for dst, name in ((ident, "ident"), (causal_f, "causal"), (pages, "page_table"), (bf_c, "b_f"),
                              (head_sel, "head_sel")):
                pool.dma_start(dst[:, :], A[name]).then_inc(const_in, 16)
            pool.dma_start(gains[:, :, :], A["gains"].rearrange("p (n k) -> p n k", n=6)).then_inc(const_in, 16)
            pool.dma_start(rb[0:N_BUCKETS, :], A["rel_bias"]).then_inc(const_in, 16)
            pool_norms(pool, 0)
            pool_norms(pool, 1)
            pool.wait_ge(x_done, x_count[1, 2])
            pool.dma_start(x_spill, x_res[:, :, :]).then_inc(S("x_spilled"), 16)
            pool.wait_ge(h_ready, h_count[2, 2])
            for dst, name in ((sel_p, "sel_prompt"), (sel_s, "sel_sample")):
                pool.dma_start(dst[:, :, :].rearrange("p g y -> p (g y)"), A[name]).then_inc(sel_in, 16)
            pool.dma_start(sel_n[:, :], A["sel_new"]).then_inc(sel_in, 16)
            pool.wait_ge(bias_ev, 3)
            for g in range(3):
                hs = slice(g * HPG, (g + 1) * HPG)
                pool.dma_start(bias_rows[hs], bias_row[hs, g, :].unsqueeze(1).broadcast_to([HPG, P, LREL])
                               ).then_inc(bias_out, 16)
            pool.wait_ge(lf_done, 1)
            pool.dma_start(A["lf_t"], lf_a[:, :]).then_inc(lf_out, 16)
            pool.wait_ge(S("x_spilled"), 16)

            def out_qkv(a, col, k_dst, v_dst):
                pool.wait_ge(kf_done, 3 * a + 3)
                pool.dma_start(k_dst, k_f[:, :]).then_inc(k_out, 16)
                pool.wait_ge(vf_done, 3 * a + 3)
                pool.dma_start(v_dst, v_f[:, :]).then_inc(v_out, 16)
                pool.wait_ge(tok_done, a + 1)
                pool.dma_start(qkv_s[:, :, col:col + P] if isinstance(col, int) else
                               qkv_s[:, :, bass.ds(col, P)], tok[:, :, :]).then_inc(tok_out, 16)

            for p in range(PAIRS_A):
                out_qkv(p, p * P, A["ka_t"][p * P:(p + 1) * P, :], A["va_t"][p * P:(p + 1) * P, :])
            for a in range(PAIRS_A, A_LAST):
                d = a - PAIRS_A
                pair, g = d // 3, d % 3
                if d >= 2:
                    pool.wait_ge(d_mt, 16 * (d - 1))
                if d == 0:
                    pool.wait_ge(bias_out, 48)
                if d == 0:
                    pool.wait_ge(oev_done, N_OV * PAIRS_A)
                for hh in range(2):
                    src = bass.AP(bias_rows_t, (g * HPG + 2 * pair + hh) * P * LREL + 127, [[LREL - 1, P], [1, 256]])
                    pool.dma_start(bias_t[:, d % 2, hh, :], src).then_inc(S(f"bias_dma{d % 2}"), 16)
                if g == 2:
                    pool.wait_ge(S(f"bias_dma{d % 2}"), 32 * (d // 2 + 1))
                    pool.memset(bias_t[HD:P, d % 2, :, P:P + HD], NEG).then_inc(bias_in, 1)
                col = g * 256 + pair * P
                out_qkv(a, WA + col, A["kb_t"][col:col + P, :], A["vb_t"][col:col + P, :])
            for n, (name, keep) in enumerate((("b1", 127), ("b2", 256), ("b3", 256))):
                c = A["cache_" + name]
                pool.dma_start(A["buf_" + name], c[:, c.shape[1] - keep:, :]).then_inc(S("buf_out"), 16)
            pool_samples(pool)
            pool_gates(pool)
            pool.wait_ge(mm_done, 3 * PLAN.block_of["proj", PROJ_ITERS - 1, 7] + 3)
            pool.wait_ge(z_lo_done, 3 * KD)
            pool.dma_start(x_res[:, :, :], x_spill).then_inc(x_back, 16)
            pool_norms(pool, 2)
            for part, (s0, w) in enumerate(PARTS):
                pool.wait_ge(x_done, x_count[5, part])
                pool.dma_start(A["y_t"].rearrange("(k p) t -> p k t", p=P)[:, :, s0:s0 + w], x_res[:, :, s0:s0 + w]
                               ).then_inc(S("y_out"), 16)
            pool.wait_ge(S("y_out"), 48)
            pool.wait_ge(S("buf_out"), 48)
            pool.wait_ge(lf_out, 16)
            pool.wait_ge(k_out, 16 * A_LAST)
            pool.wait_ge(v_out, 16 * A_LAST)
            pool.wait_ge(tok_out, 16 * A_LAST)
            pool.wait_ge(bias_out, 48)

        @block.scalar
        def _(act):
            for part, (s0, w) in enumerate(PARTS):
                act.dma_start(x_res[:, :, s0:s0 + w], A["x_t"].rearrange("(k p) t -> p k t", p=P)[:, :, s0:s0 + w]
                              ).then_inc(x_in[part], 16)
            act.wait_ge(S("ones_set"), 3)
            first_splits(act, act_split)
            act_norms(act, 0)
            steps(act, FFN_ITERS, lambda i, lo, hi, first: act_ffn(act, "ffn1", i, lo, hi), last_apart=True)
            act_norms(act, 1)
            act_forget(act)
            act.wait_ge(S("x_spilled"), 16)

            def fox(i, lo, hi, first):
                act_qkv(act, "fox", i, lo, hi, 1)
                act_fox(act, i, lo, hi)
            steps(act, PAIRS_A, fox)
            for d in range(3 * PAIRS_B):
                act_qkv(act, "dil", d, d, d + 1, DIL[d % 3])
                act_dil(act, d, d % 3)
                if d % 3 == 2:
                    act_combine(act, d // 3)
            act_gates(act)
            for out in g_out:
                act.wait_ge(out, 16 * 2 * KD // GATE_SLOTS)
            for s0, w in PARTS:
                if s0 + w > SEQ:
                    act.wait_ge(s_out, 1)
                act.activation(o_hi[:, :, s0:s0 + w], o_st[:, :, s0:s0 + w], ACT.Copy).then_inc(o_hi_done, 1)
            act_merge(act)
            act_norms(act, 2)
            steps(act, FFN_ITERS, lambda i, lo, hi, first: act_ffn(act, "ffn2", i, lo, hi), last_apart=True)
            act_norms(act, 3)

        @block.vector
        def _(dve):
            dve.wait_ge(const_in, 112)
            dve.tensor_copy(ident_b[:, :], ident[:, :]).then_inc(S("bf_set"), 1)
            dve.tensor_copy(causal_b[:, :], causal_f[:, :]).then_inc(S("bf_set"), 1)
            dve.tensor_scalar(gains[:, 1, :], gains[:, 1, :], 0.5, None, ALU.mult).then_inc(S("bf_set"), 1)
            dve.tensor_scalar(gains[:, 5, :], gains[:, 5, :], 0.5, None, ALU.mult).then_inc(S("bf_set"), 1)
            dve.wait_ge(S("bf_set"), 4)
            first_splits(dve, dve_split)
            dve_norms(dve, 0)
            steps(dve, FFN_ITERS, lambda i, lo, hi, first: dve_ffn(dve, "ffn1", i, lo, hi, first), last_apart=True)
            dve_norms(dve, 1)
            dve_forget(dve)

            def fox(i, lo, hi, first):
                dve_qkv(dve, "fox", i, lo, hi, 1)
                dve_fox(dve, i, lo, hi)
            steps(dve, PAIRS_A, fox)
            for d in range(3 * PAIRS_B):
                dve_qkv(dve, "dil", d, d, d + 1, DIL[d % 3])
                dve_dil(dve, d, d % 3)
                if d % 3 == 2:
                    dve_combine(dve, d // 3)
            dve_gates(dve)
            for part, (s0, w) in enumerate(PARTS):
                dve.wait_ge(o_hi_done, part + 1)
                dve.tensor_tensor(o_lo[:, :, s0:s0 + w], o_st[:, :, s0:s0 + w],
                                  o_hi[:, :, s0:s0 + w].bitcast(F32), ALU.subtract).then_inc(o_lo_done, 1)
            dve_merge(dve)
            dve_norms(dve, 2)
            steps(dve, FFN_ITERS, lambda i, lo, hi, first: dve_ffn(dve, "ffn2", i, lo, hi, first), last_apart=True)
            dve_norms(dve, 3)

        @block.tensor
        def _(pe):
            pe_norms(pe, 0)
            steps(pe, FFN_ITERS, lambda i, lo, hi, first: pe_ffn(pe, "ffn1", i, lo, hi), last_apart=True)
            pe_norms(pe, 1)
            pe.wait_ge(S("bf_set"), 4)
            pe_block(pe, "forget", 0, 0, 0, 1, h_hi, h_lo,
                     lambda part: pe.wait_ge(h_ready, h_count[2, part]))

            def fox(i, lo, hi, first):
                pe_qkv(pe, "fox", i, lo, hi)
                pe_fox(pe, i, lo, hi)
            steps(pe, PAIRS_A, fox)
            for d in range(3 * PAIRS_B):
                pe_qkv(pe, "dil", d, d, d + 1)
                pe_dil(pe, d, d % 3)
                if d % 3 == 2:
                    pe_combine(pe, d // 3)
            pe_gates(pe)
            pe_merge(pe)
            pe_norms(pe, 2)
            steps(pe, FFN_ITERS, lambda i, lo, hi, first: pe_ffn(pe, "ffn2", i, lo, hi), last_apart=True)
            pe_norms(pe, 3)


def lay_out_weights(w):
    out = np.zeros((PLAN.chunks, P, CH), np.float32)

    def put(n, block):
        k = block.shape[0] // P
        out[n, :, :k * block.shape[1]] = block.reshape(k, P, -1).transpose(1, 0, 2).reshape(P, -1)

    for ph, pre in (("ffn1", "ffn1_"), ("ffn2", "ffn2_")):
        for i in range(FFN_ITERS):
            c = FIRST_CHUNK[ph] + CHUNKS[ph] * i
            for f in range(2):
                cols = slice((2 * i + f) * P, (2 * i + f + 1) * P)
                put(c + 2 * f, w[pre + "w_gate"][:, cols])
                put(c + 2 * f + 1, w[pre + "w_up"][:, cols])
            down = w[pre + "w_down"][2 * i * P:(2 * i + 2) * P]
            put(c + 4, down[:, 0:512])
            put(c + 5, down[:, 512:1024])
    w_in = w["w_in"]
    put(FIRST_CHUNK["forget"], w_in[:, COL_FA:COL_FA + P])
    for p in range(PAIRS_A):
        for n, col in enumerate((COL_QA, COL_KA, COL_VA)):
            put(FIRST_CHUNK["fox"] + 3 * p + n, w_in[:, col + p * P:col + (p + 1) * P])
    for d in range(3 * PAIRS_B):
        for n, col in enumerate((COL_QB, COL_KB, COL_VB)):
            at = col + (d % 3) * 256 + (d // 3) * P
            put(FIRST_CHUNK["dil"] + 3 * d + n, w_in[:, at:at + P])
    for n in range(2 * KD):
        put(FIRST_CHUNK["gates"] + n, w_in[:, COL_GA + n * P:COL_GA + (n + 1) * P])
    for i in range(PROJ_ITERS):
        c = FIRST_CHUNK["proj"] + 3 * i
        for n in range(2):
            put(c + n, w["w_proj_a"][:, (4 * i + 2 * n) * P:(4 * i + 2 * n + 2) * P])
        put(c + 2, w["w_proj_b"][:, 4 * i * P:(4 * i + 4) * P])
    for n in range(KD):
        put(FIRST_CHUNK["out"] + n, w["w_out"][:, n * P:(n + 1) * P])
    return out


OUTS = {"y_t": (D, T), "ka_t": (WA, T), "va_t": (WA, T), "lf_t": (NHA, T), "kb_t": (WB, T), "vb_t": (WB, T),
        "buf_b1": (NB, 127, 512), "buf_b2": (NB, 256, 512), "buf_b3": (NB, 256, 512)}


def kernel(**inputs):
    import concourse.bacc as bacc
    from concourse.bass_utils import run_bass_kernel_spmd

    x = {k: np.asarray(v) for k, v in inputs.items()}
    w = {k: x[k][0] for k in x if k.endswith(("w_gate", "w_up", "w_down", "w_out", "w_proj_a", "w_proj_b"))
         or k == "w_in"}
    arrays = dict(shape_constants())
    arrays["x_t"] = np.concatenate([x["x_prompt"][0].T, x["x_sample"][:, 0].T], axis=1)
    gains = [x[n][0] for n in ("ffn1_pre_g", "ffn1_post_g", "mix_pre_g", "mix_post_g", "ffn2_pre_g", "ffn2_post_g")]
    arrays["gains"] = np.stack([g.reshape(KD, P).T for g in gains], axis=1).reshape(P, -1)
    arrays["w_chunks"] = lay_out_weights(w)
    arrays["b_f"] = x["b_f"].reshape(NHA, 1)
    arrays["rel_bias"] = x["rel_bias"]
    arrays["page_table"] = x["page_table"].reshape(1, -1)
    arrays["cache_a_k"] = x["cache_a_k"][0].reshape(-1, PAGE, WA)
    arrays["cache_a_v"] = x["cache_a_v"][0].reshape(-1, PAGE, WA)
    arrays["cache_a_logf"] = x["cache_a_logf"][0]
    for g in (1, 2, 3):
        arrays[f"cache_b{g}"] = x[f"cache_b{g}_kv"][0].reshape(NB, -1, 512)
    nc = bacc.Bacc("TRN2", target_bir_lowering=False, num_devices=1, dynamic_dma_scratch_size=4096)
    A = {}
    for name, a in arrays.items():
        arrays[name] = a = np.ascontiguousarray(a)
        A[name] = nc.dram_tensor(name, a.shape, mybir.dt.from_np(a.dtype), kind="ExternalInput").ap()
    for name, shape in OUTS.items():
        A[name] = nc.dram_tensor(name, shape, F32, kind="ExternalOutput").ap()
    build(nc, A)
    r = run_bass_kernel_spmd(nc, [arrays], core_ids=[0]).results[0]

    def tokens(a, heads):
        a = np.asarray(a).T
        return a[:SEQ].reshape(1, 1, SEQ, heads, -1), a[SEQ:].reshape(1, NB, 1, heads, -1)

    y = np.asarray(r["y_t"]).T
    ka, ka_s = tokens(r["ka_t"], NHA)
    va, va_s = tokens(r["va_t"], NHA)
    lf, lf_s = tokens(r["lf_t"], NHA)
    kb, kb_s = tokens(r["kb_t"], 3 * HPG)
    vb, vb_s = tokens(r["vb_t"], 3 * HPG)
    prompt, sample = [], []
    for g, window in enumerate((128, 512, 2048)):
        hs = slice(g * HPG, (g + 1) * HPG)
        keep = min(window, SEQ)
        prompt.append(np.stack([kb[:, :, SEQ - keep:, hs], vb[:, :, SEQ - keep:, hs]], axis=3))
        old = np.asarray(r[f"buf_b{g + 1}"]).reshape(1, NB, -1, 2, HPG, HD)
        new = np.stack([kb_s[:, :, :, hs], vb_s[:, :, :, hs]], axis=3)
        sample.append(np.concatenate([old, new], axis=2))
    return (y[:SEQ][None], y[SEQ:][:, None], ka, va, lf[..., 0], *prompt, ka_s, va_s, lf_s[..., 0], *sample)
```

```python
from contextlib import ExitStack

import numpy as np
import concourse.bass as bass
from concourse import mybir

F32, F32R, BF16, I32 = mybir.dt.float32, mybir.dt.float32r, mybir.dt.bfloat16, mybir.dt.int32
ALU, ACT, AX = mybir.AluOpType, mybir.ActivationFunctionType, mybir.AxisListType

P = 128
D = 1024
KD = D // P
SEQ, NB = 1024, 8
T = SEQ + NB
PARTS = ((0, 352), (352, 352), (704, 328))
DFF = 2816
HD = 64
NHA, WA = 8, 512
DIL = (1, 4, 16)
HPG = 4
WB = 768
PAIRS_A, PAIRS_B = NHA // 2, HPG // 2
COL_QA, COL_KA, COL_VA, COL_FA = 0, 512, 1024, 1536
COL_QB = 1544
COL_KB, COL_VB = COL_QB + WB, COL_QB + 2 * WB
COL_GA = COL_QB + 3 * WB
COL_GB = COL_GA + D
NQ = SEQ // P
PAGE, NPAGE = 128, 2
CH = 1024
RING = 3
FFN_ITERS = DFF // P // 2
PROJ_ITERS = KD // 4
SCALE = HD ** -0.5
EPS = 1e-6
NEG = -1e30
LREL = 384
N_BUCKETS, MAX_DISTANCE = 32, 2048
GATE_SLOTS = 3
UNITS = [(0, 3, 0), (1, 0, 8), (0, 2, 0), (1, 1, 6), (1, 2, 0), (0, 1, 6), (0, 0, 0), (1, 3, 2)]
PT_SLOTS = 10
SAMPLE_KEYS = (128, 64, 16)

PHASES = ("ffn1", "forget", "fox", "dil", "gates", "proj", "out", "ffn2")
ITERS = dict(ffn1=FFN_ITERS, forget=1, fox=PAIRS_A, dil=PAIRS_B * 3, gates=1, proj=PROJ_ITERS, out=1, ffn2=FFN_ITERS)
CHUNKS = dict(ffn1=6, forget=1, fox=3, dil=3, gates=2 * KD, proj=3, out=KD, ffn2=6)
FFN_BLOCKS = [(0, 0, 128, 8, "act"), (1, 0, 128, 8, "u"), (2, 0, 128, 8, "act"), (3, 0, 128, 8, "u")] + \
             [(4 + m // 4, 128 * (m % 4), 512, 2, "dve") for m in range(8)]
QKV_BLOCKS = [(0, 0, 128, 8, "dve"), (1, 0, 128, 8, "dve"), (2, 0, 128, 8, "act")]
PROJ_BLOCKS = [(m // 2, 128 * (m % 2), 256, 4, "dve") if branch == 0 else (2, 128 * m, 512, 2, "dve")
               for m in range(4) for branch in range(2)]
BLOCKS = dict(ffn1=FFN_BLOCKS, ffn2=FFN_BLOCKS, forget=[(0, 0, 128, 8, "act")], fox=QKV_BLOCKS, dil=QKV_BLOCKS,
              gates=[(n, 0, 128, 8, "act") for n in range(2 * KD)], proj=PROJ_BLOCKS,
              out=[(n, 0, 128, 8, "dve") for n in range(KD)])


class Counts:

    def __init__(self, chunks, chunk_of, block_of, free_of, before, last_block):
        self.chunks, self.chunk_of, self.block_of = chunks, chunk_of, block_of
        self.free_of, self.before, self.last_block = free_of, before, last_block


def plan():
    chunk = block = 0
    freed = dict(act=0, dve=0, u=0)
    chunk_of, block_of, free_of, before, last_block = {}, {}, {}, {}, {}
    user = [None, None]
    for ph in PHASES:
        for i in range(ITERS[ph]):
            for j, (c, _, _, _, who) in enumerate(BLOCKS[ph]):
                key = (ph, i, j)
                chunk_of[key] = chunk + c
                last_block[chunk + c] = block
                block_of[key] = block
                free_of[key] = (who, freed[who])
                before[key] = user[j % 2]
                user[j % 2] = key
                freed[who] += 3
                block += 1
            chunk += CHUNKS[ph]
    return Counts(chunk, chunk_of, block_of, free_of, before, last_block)


PLAN = plan()
FIRST_CHUNK = {}
for _ph in PHASES:
    FIRST_CHUNK[_ph] = PLAN.chunk_of[_ph, 0, 0]


def lin(f, i, lo, hi):
    if isinstance(i, int):
        return f(i)
    a, d = f(lo), (f(lo + 1) - f(lo) if hi > lo + 1 else 0)
    assert all(f(x) == a + d * (x - lo) for x in range(lo, hi))
    return (i * d + (a - d * lo)) if d else a


def t5_buckets(dist):
    dist = np.asarray(dist)
    exact = N_BUCKETS // 2
    large = exact + (np.log(np.maximum(dist, 1) / exact) / np.log(MAX_DISTANCE / exact)
                     * (N_BUCKETS - exact)).astype(np.int32)
    return np.where(dist < exact, dist, np.minimum(large, N_BUCKETS - 1)).astype(np.int32)


def shape_constants():
    c = {}
    sel = np.zeros((P, NHA), np.float32)
    for h in range(NHA):
        sel[h, h] = sel[32 + h, h] = 1.0
    c["head_sel"] = sel
    c["ident"] = np.eye(P, dtype=np.float32)
    q, k = np.arange(P)[:, None], np.arange(P)[None, :]
    c["causal"] = np.where(k <= q, 0.0, NEG).astype(np.float32)
    c["upto"] = (q <= k).astype(np.float32)
    prompt = np.zeros((N_BUCKETS + 1, 3, LREL), np.float32)
    sample = np.zeros((N_BUCKETS + 1, 3, P), np.float32)
    for g, dil in enumerate(DIL):
        most = min(128, SEQ // dil - 1)
        for y in range(LREL):
            d = 255 - y
            if 0 <= d <= most:
                prompt[t5_buckets(d * dil), g, y] = 1.0
            else:
                prompt[N_BUCKETS, g, y] = NEG
        for p in range(P):
            if p < SAMPLE_KEYS[g]:
                sample[t5_buckets((SAMPLE_KEYS[g] - p) * dil), g, p] = 1.0
            else:
                sample[N_BUCKETS, g, p] = NEG
    new = np.zeros((N_BUCKETS + 1, NB), np.float32)
    new[t5_buckets(0)] = 1.0
    c["sel_prompt"], c["sel_sample"], c["sel_new"] = prompt.reshape(33, -1), sample.reshape(33, -1), new
    own = np.where(np.arange(NB)[:, None] == np.arange(NB)[None, :], 0.0, NEG).astype(np.float32)
    c["own_a"] = np.repeat(own, NHA, axis=0)
    c["own_b"] = np.repeat(own, HPG, axis=0)
    c["head_a"] = np.tile(np.eye(NHA, dtype=np.float32), (NB, 1))
    c["head_b"] = np.tile(np.eye(HPG, dtype=np.float32), (NB, 1))
    return c


def build(nc, A):
    ctx = ExitStack()
    with ctx:
        class Place:

            def __init__(self, at, end):
                self.at, self.end = at, end

            def __call__(self, name, shape, dt):
                n = int(np.prod(shape[1:])) * (2 if dt == BF16 else 4)
                t = nc.alloc_sbuf_tensor_at(name, shape, dt, offset=self.at)
                self.at += -(-n // 32) * 32
                assert self.at <= self.end, (name, self.at, self.end)
                return t

        base = -(-nc.sbuf_base // 32) * 32
        ring = Place(base, base + 3 * RING * 4 * CH)
        w_raw = ring("w_raw", [P, RING, CH], F32)
        w_hi = ring("w_hi", [P, RING, CH], F32R)
        w_lo = ring("w_lo", [P, RING, CH], F32R)
        hidden = Place(ring.end, ring.end + 2 * 4 * KD * T)
        h_hi = hidden("h_hi", [P, KD, T], F32R)
        h_lo = hidden("h_lo", [P, KD, T], F32R)
        R0 = hidden.end
        R1, R2, R3, R4, R5 = R0 + 33024, R0 + 57792, R0 + 66048, R0 + 90816, R0 + 115584
        x_res = Place(R0, R1)("x_res", [P, KD, T], F32)
        acc = Place(R1, R3)("acc", [P, KD, T], F32)
        pu = Place(R3, R4)
        u_hi, u_lo = pu("u_hi", [P, 2, T], F32R), pu("u_lo", [P, 2, T], F32R)
        sg2 = pu("sg2", [P, 2, T], F32)
        gate_f, u_f = sg2[:, 0, :], sg2[:, 1, :]
        PW = PARTS[0][1]
        pn = Place(R4, R5)
        pn2 = Place(R3, R4)
        norm_buf = [pn2("norm_buf0", [P, KD, PW], F32), pn("norm_buf1", [P, KD, PW], F32),
                    pn2("norm_buf2", [P, KD, PW], F32)]
        sq_sum = pn("sq_sum", [P, T], F32)
        sq_tile = Place(R4, R5)("sq_tile", [P, 2, T], F32)
        root, rinv = pn("root", [P, 3, PW], F32), pn("rinv", [P, 3, PW], F32)
        o_hi, z_f = Place(R0, R2)("o_hi", [P, 6, T], F32R), Place(R0 + 24768, R1)("z_f", [P, 2, T], F32)
        gate_in = Place(R3, R4)("gate_in", [P, 2, 2, T], F32)
        o_lo = Place(R4, R5)("o_lo", [P, 6, T], F32R)
        t1 = Place(R0, R1)
        q_hi, q_lo = t1("q_hi", [P, SEQ], F32R), t1("q_lo", [P, SEQ], F32R)
        k_hi, k_lo = t1("k_hi", [P, SEQ], F32R), t1("k_lo", [P, SEQ], F32R)
        prob = t1("prob", [P, 2, SEQ], F32)
        v_g, k_f = t1("v_g", [P, SEQ], F32), t1("k_f", [P, T], F32)
        prob_b = prob[:, :, :].rearrange("p a (s c) -> p (a s) c", c=256)
        o_st = Place(R1, R2)("o_st", [P, 6, T], F32)
        t2 = Place(R2, R5)
        pt_hi, pt_lo = t2("pt_hi", [P, PT_SLOTS, 256], F32R), t2("pt_lo", [P, PT_SLOTS, 256], F32R)
        vt_hi, vt_lo = t2("vt_hi", [P, NQ, 3, HD], F32R), t2("vt_lo", [P, NQ, 3, HD], F32R)
        v_f = t2("v_f", [P, T], F32)
        score_b = v_g[:, :].rearrange("p (s c) -> p s c", c=256)
        q_s = t2("q_s", [P, NB], F32)
        R2b = t2.at
        ncum = t2("neg_cum", [P, SEQ], F32R)
        pair_sel = t2("pair_sel", [P, 2, P], F32R)
        lf_at = t2.at
        lf_z, lf_e, lf_a = (t2(n, [NHA, T], F32) for n in ("lf_z", "lf_e", "lf_a"))
        bias_row = Place(lf_at, R5)("bias_row", [3 * HPG, 3, LREL], F32)
        cum, cum_one = lf_z[:, 0:SEQ], lf_e[:, 0:SEQ]
        t3 = Place(R2b, R5)
        o_g = t3("o_g", [P, 3, SEQ], F32)
        bias_t = t3("bias_t", [P, 2, 2, 256], F32)
        wide = t3("wide", [P, NQ, 2, HD], F32)
        wg = Place(R0 + 4 * 4 * SEQ, R1)("wg", [P, 3, SEQ], F32)
        mxall, tsum = k_f[:, 0:SEQ], v_f[:, 0:SEQ]
        t5 = Place(R2, R5)
        kc_a, kc_b = t5("kc_a", [P, 2, NPAGE, WA], F32), t5("kc_b", [P, 2, 3, 256], F32)
        qb = t5("qb", [P, 2, WA + WB], F32)
        prod = t5("prod", [P, NPAGE * WA + WB], F32)
        kn, vn = t5("kn", [NB, WA + WB], F32), t5("vn", [NB, WA + WB], F32)
        qn = t5("qn", [NB, WA + WB], F32)
        lfp = t5("lfp", [P, NPAGE, NB, NHA], F32)
        s_a, s_b = t5("s_a", [P, NPAGE, NB, NHA], F32), t5("s_b", [P, 3, NB, HPG], F32)
        sn_a, sn_b = t5("sn_a", [NB, NB, NHA], F32), t5("sn_b", [NB, 3, NB, HPG], F32)
        p_a, p_b = t5("p_a", [P, NPAGE, NB * 72], F32), t5("p_b", [P, 3, NB * 36], F32)
        t5b = Place(R0, R1)
        gate_st = t5b("gate_st", [P, GATE_SLOTS, T], F32)
        upto = t5b("upto_c", [P, P], F32)
        row_a, row_b = t5b("row_a", [64, 264], F32), t5b("row_b", [32, 408], F32)
        crow = t5b("crow", [64, 256], F32)
        cols = t5b("cols", [64, 8], F32)
        head_a, head_b = t5b("head_a_c", [64, NHA], F32), t5b("head_b_c", [32, HPG], F32)
        pn_a, pn_b = t5b("pn_a", [NB, NB, NHA], F32), t5b("pn_b", [NB, 3, NB, HPG], F32)
        o_rows = t5b("o_rows", [64, 2, HD], F32)
        masked = t5b("masked", [64, WA + 256], F32)
        s_own = t5b("s_own", [NB, NHA + 3 * HPG], F32)
        lf_new = t5b("lf_new", [64, 1], F32)
        own_a, own_b = t5b("own_a_c", [64, NB], F32), t5b("own_b_c", [32, NB], F32)
        pc = Place(R5, nc.sbuf_usable_end)
        ident, ones = pc("ident_c", [P, P], F32), pc("ones", [P, P], F32)
        causal_f = pc("causal_c", [P, P], F32)
        ident_b, causal_b = pc("ident_b", [P, P], BF16), pc("causal_b", [P, P], BF16)
        head_sel = pc("head_sel_c", [P, NHA], F32)
        gains = pc("gains_c", [P, 6, KD], F32)
        eps_c, one_c, bf_c = pc("eps_c", [P, 1], F32), pc("one_c", [P, 1], F32), pc("b_f_c", [NHA, 1], F32)
        rb = pc("rel_bias_c", [N_BUCKETS + 1, 3 * HPG], F32)
        bs, bn = pc("bias_sample", [P, 3, HPG], F32), pc("bias_new", [NB, 3, HPG], F32)
        pages = pc("pages_c", [1, NB * NPAGE], I32)
        nmax, rsum = pc("nmax", [P, 2], F32), pc("rsum", [P, 256], F32)
        tok = pc("tok", [NB, 3, P], F32)
        mx, nmx, den = (pc(n, [P, 3, 2, NQ], F32) for n in ("mx", "nmx", "den"))
        t6 = Place(R2, R2b)
        sel_p, sel_s, sel_n = t6("sel_prompt_c", [33, 3, LREL], F32), t6("sel_sample_c", [33, 3, P], F32), \
            t6("sel_new_c", [33, NB], F32)

        ps = ctx.enter_context(nc.psum_tensor("ps", [P, 8, 512], F32))
        psf = ps[:, :, :].rearrange("p b c -> p (b c)")

        def bank(n, w=512):
            return ps[:, n, 0:w]

        x_spill = nc.dram_tensor("x_spill", [P, KD, T], F32).ap()
        gates_s = nc.dram_tensor("gates_s", [2 * KD, P, T], F32).ap()
        bias_rows_t = nc.dram_tensor("bias_rows", [3 * HPG, P, LREL], F32)
        bias_rows = bias_rows_t.ap()
        qkv_s = nc.dram_tensor("qkv_s", [NB, 3, WA + WB], F32).ap()

        sem = {}

        def S(name):
            if name not in sem:
                sem[name] = ctx.enter_context(nc.semaphore(name))
            return sem[name]

        w_loaded = [S(f"w_loaded{n}") for n in range(RING)]
        w_hi_done, w_lo_done, mm_done = S("w_hi_done"), S("w_lo_done"), S("mm_done")
        u_f_done = S("u_f_done")
        freed = dict(act=S("banks_freed_by_act"), dve=S("banks_freed_by_dve"), u=u_f_done)
        const_in, x_in = S("const_in"), [S(f"x_in{part}") for part in range(3)]

        def chunk_no(ph, c):
            return lambda s: FIRST_CHUNK[ph] + s * CHUNKS[ph] + c

        def act_split(act, ph, i, c, lo, hi):
            f = chunk_no(ph, c + 2)
            i0 = i if isinstance(i, int) else lo
            slot = f(i0) % RING
            if isinstance(i, int) and f(i) >= PLAN.chunks:
                return
            act.wait_ge(w_loaded[slot], lin(lambda s: 16 * (f(s) // RING + 1), i, lo, hi))
            if f(i0) >= RING:
                act.wait_ge(mm_done, lin(lambda s: 3 * PLAN.last_block[f(s) - RING] + 3, i, lo, hi))
            act.activation(w_hi[:, slot, :], w_raw[:, slot, :], ACT.Copy).then_inc(w_hi_done, 1)

        def dve_split(dve, ph, i, c, lo, hi):
            f = chunk_no(ph, c + 2)
            slot = f(i if isinstance(i, int) else lo) % RING
            if isinstance(i, int) and f(i) >= PLAN.chunks:
                return
            dve.wait_ge(w_hi_done, lin(lambda s: f(s) + 1, i, lo, hi))
            dve.tensor_tensor(w_lo[:, slot, :], w_raw[:, slot, :], w_hi[:, slot, :].bitcast(F32),
                              ALU.subtract).then_inc(w_lo_done, 1)

        def first_splits(eng, split):
            for c in (-2, -1):
                split(eng, "ffn1", 0, c, 0, 1)

        def pe_block(pe, ph, i, j, lo, hi, rhs_hi, rhs_lo, rhs_wait=None, lo_wait=None,
                     between=None):
            c, off, width, k_tiles, _ = BLOCKS[ph][j]
            i0 = i if isinstance(i, int) else lo
            slot = PLAN.chunk_of[ph, i0, j] % RING
            hi_w = w_hi[:, slot, 0:k_tiles * width].rearrange("p (k c) -> p k c", c=width)
            lo_w = w_lo[:, slot, 0:k_tiles * width].rearrange("p (k c) -> p k c", c=width)
            pe.wait_ge(w_lo_done, lin(lambda s: PLAN.chunk_of[ph, s, j] + 1, i, lo, hi))
            for part, (s0, w) in enumerate(PARTS):
                if PLAN.before[ph, i0, j] is not None:
                    who = PLAN.free_of[PLAN.before[ph, i0, j]][0]
                    pe.wait_ge(freed[who], lin(lambda s: PLAN.free_of[PLAN.before[ph, s, j]][1] + part + 1,
                                               i, lo, hi))
                if rhs_wait:
                    rhs_wait(part)
                out = bank(3 * (j % 2) + part, w)
                passes = [(k, a, b) for k in range(k_tiles)
                          for a, b in ((hi_w, rhs_hi), (hi_w, rhs_lo), (lo_w, rhs_hi))]
                if lo_wait:
                    passes.sort(key=lambda one: one[2] is rhs_lo)
                for n, (k, a, b) in enumerate(passes):
                    if lo_wait and n == 2 * k_tiles:
                        lo_wait(part)
                    last = pe.matmul(out, a[:, k, off:off + P], b[:, k, s0:s0 + w],
                                     start=(n == 0), stop=(n == 3 * k_tiles - 1))
                last.then_inc(mm_done, 1)
                if between:
                    between(part)

        def product(eng, ph, i, j, part, lo, hi):
            eng.wait_ge(mm_done, lin(lambda s: 3 * PLAN.block_of[ph, s, j] + part + 1, i, lo, hi))
            return bank(3 * (j % 2) + part, PARTS[part][1])

        GROUPS = [[(0, 0), (0, 1), (0, 2)],
                  [(1, 0), (1, 1), (1, 2), (2, 0), (2, 1), (2, 2)],
                  [(3, 0), (3, 1), (3, 2), (4, 0), (4, 1), (4, 2)],
                  [(5, 0), (5, 1), (5, 2)]]
        EVENTS = [e for g in GROUPS for e in g]
        EV = {e: n for n, e in enumerate(EVENTS)}
        post_sq, post_sum = S("post_squares"), S("post_square_sums")
        x_count = {e: n + 1 for n, e in enumerate(e for e in EVENTS if e[0] % 2)}
        h_count = {e: n + 1 for n, e in enumerate(e for e in EVENTS if e[0] % 2 == 0)}
        squares, sums, roots, normed_f, h_hi_done, x_done, h_ready, recips, x_back = (S(n) for n in (
            "squares", "sums", "roots", "normed_f", "h_hi_done", "x_done", "h_ready", "recips", "x_back"))
        post_normed = S("post_normed")
        AFTER = {1: "ffn1", 3: "out", 5: "ffn2"}

        HALF = KD // 2
        x_done_pool = S("x_done_pool")

        def wait_x(eng, e):
            eng.wait_ge(x_done, x_count[e])
            eng.wait_ge(x_done_pool, x_count[e])

        def wait_over(eng, e):
            if e[0] % 2:
                wait_x(eng, e)
            else:
                eng.wait_ge(h_ready, h_count[e])

        def wait_h(pe, t):
            return (lambda part: pe.wait_ge(h_hi_done, h_count[t, part]),
                    lambda part: pe.wait_ge(h_ready, h_count[t, part]))

        def act_square(act, e):
            t, part = e
            s0, w = PARTS[part]
            n = EV[e]
            if t == 0:
                act.wait_ge(x_in[part], 16)
            else:
                wait_x(act, (t - 1, part))
            if n >= 3:
                wait_over(act, EVENTS[n - 3])
            act.activation(norm_buf[n % 3][:, :, 0:w], x_res[:, :, s0:s0 + w],
                           ACT.Square).then_inc(squares, 1)

        def act_post_square(act, t, m):
            ph = AFTER[t]
            last = ITERS[ph] - 1, len(BLOCKS[ph]) - KD + m
            if m >= 3:
                act.wait_ge(post_sum, 3 * ((KD - 1) * (t // 2) + m - 2))
            for part, (s0, w) in enumerate(PARTS):
                act.wait_ge(freed["dve"], PLAN.free_of[ph, last[0], last[1]][1] + part + 1)
                dst = sq_tile[:, m % 2, s0:s0 + w] if m else sq_sum[:, s0:s0 + w]
                act.activation(dst, acc[:, m, s0:s0 + w], ACT.Square).then_inc(post_sq, 1)

        def dve_post_add(dve, t, m):
            for part, (s0, w) in enumerate(PARTS):
                done = 3 * ((KD - 1) * (t // 2) + m - 1) + part + 1
                dve.wait_ge(post_sq, 3 * (KD * (t // 2) + m) + part + 1)
                if m > 1:
                    dve.wait_ge(post_sum, done - 3)
                if m:
                    dve.tensor_tensor(sq_sum[:, s0:s0 + w], sq_sum[:, s0:s0 + w], sq_tile[:, m % 2, s0:s0 + w],
                                      ALU.add).then_inc(post_sum, 1)

        def act_root(act, e):
            n, w = EV[e], PARTS[e[1]][1]
            act.wait_ge(sums, n + 1)
            if n >= 3:
                act.wait_ge(recips, n - 2)
            act.activation(root[:, n % 3, 0:w], bank(6 + n % 2, w), ACT.Sqrt, bias=eps_c[:, 0:1],
                           scale=1.0 / D).then_inc(roots, 1)

        def act_high(act, e):
            s0, w = PARTS[e[1]]
            act.wait_ge(normed_f, h_count[e])
            act.activation(h_hi[:, :, s0:s0 + w], norm_buf[EV[e] % 3][:, :, 0:w], ACT.Copy).then_inc(h_hi_done, 1)

        def act_norms(act, group):
            post = [e for e in GROUPS[group] if e[0] % 2]
            pre = [e for e in GROUPS[group] if e[0] % 2 == 0]
            for part in range(3):
                if post:
                    act_root(act, post[part])
                if pre and part < (2 if post else 3):
                    if not post or part:
                        act_square(act, pre[part - 1 if post else part])
            if pre and post:
                act_square(act, pre[1])
            for part, e in enumerate(pre):
                act_root(act, e)
                if post and part == 0:
                    act_square(act, pre[2])
                if part:
                    act_high(act, pre[part - 1])
            if pre:
                act_high(act, pre[2])

        def pe_norms(pe, group):
            for e in GROUPS[group]:
                n, w = EV[e], PARTS[e[1]][1]
                if n == 0:
                    pe.wait_ge(S("ones_set"), 3)
                if e[0] % 2:
                    pe.wait_ge(post_sum, 3 * ((KD - 1) * (e[0] // 2 + 1) - 1) + e[1] + 1)
                else:
                    pe.wait_ge(squares, h_count[e])
                if n >= 2:
                    pe.wait_ge(roots, n - 1)
                s0 = PARTS[e[1]][0]
                terms = [sq_sum[:, s0:s0 + w]] if e[0] % 2 else [norm_buf[n % 3][:, k, 0:w] for k in range(KD)]
                for k, term in enumerate(terms):
                    last = pe.matmul(bank(6 + n % 2, w), ones[:, :], term, start=(k == 0), stop=(k == len(terms) - 1))
                last.then_inc(sums, 1)

        def dve_norms(dve, group):
            for e in GROUPS[group]:
                t, part = e
                s0, w = PARTS[part]
                n = EV[e]
                buf = norm_buf[n % 3]
                src = acc if t % 2 else x_res
                dve.wait_ge(roots, n + 1)
                dve.reciprocal(rinv[:, n % 3, 0:w], root[:, n % 3, 0:w]).then_inc(recips, 1)
                dve.wait_ge(recips, n + 1)
                if n >= 3:
                    wait_over(dve, EVENTS[n - 3])
                for k in range(KD):
                    last = dve.scalar_tensor_tensor(out=buf[:, k, 0:w], in0=src[:, k, s0:s0 + w],
                                                    scalar=gains[:, t, k:k + 1], in1=rinv[:, n % 3, 0:w],
                                                    op0=ALU.mult, op1=ALU.mult)
                if t % 2:
                    last.then_inc(post_normed, 1)
                    dve.wait_ge(post_normed, x_count[e])
                    if t == 3:
                        dve.wait_ge(x_back, 16)
                    x = x_res[:, 0:HALF, s0:s0 + w]
                    dve.tensor_tensor(x, x, buf[:, 0:HALF, 0:w], ALU.add).then_inc(x_done, 1)
                else:
                    last.then_inc(normed_f, 1)

        def pool_norms(pool, group):
            for n, (t, part) in enumerate(GROUPS[group]):
                e, (s0, w) = (t, part), PARTS[part]
                buf = norm_buf[EV[e] % 3]
                if n:
                    b = GROUPS[group][n - 1]
                    pool.wait_ge(x_done_pool if b[0] % 2 else h_ready, (x_count if b[0] % 2 else h_count)[b])
                elif group == 0:
                    pool.wait_ge(S("rb_one"), 1)
                if t % 2:
                    pool.wait_ge(post_normed, x_count[e])
                    if t == 3:
                        pool.wait_ge(x_back, 16)
                    x = x_res[:, HALF:, s0:s0 + w]
                    pool.tensor_tensor(x, x, buf[:, HALF:, 0:w], ALU.add).then_inc(x_done_pool, 1)
                else:
                    pool.wait_ge(h_hi_done, h_count[e])
                    pool.tensor_tensor(h_lo[:, :, s0:s0 + w], buf[:, :, 0:w],
                                       h_hi[:, :, s0:s0 + w].bitcast(F32), ALU.subtract).then_inc(h_ready, 1)

        u_hi_done, u_lo_done = S("u_hi_done"), S("u_lo_done")
        U_STEP = dict(ffn1=0, ffn2=FFN_ITERS)

        def u_parts(ph, f, part):
            return lambda s: 3 * (2 * (U_STEP[ph] + s) + f) + part + 1

        def pe_down(pe, ph, i, lo, hi, j0):
            for j in range(j0, j0 + 8):
                pe_block(pe, ph, i, j, lo, hi, u_hi, u_lo,
                         (lambda part: pe.wait_ge(u_lo_done, lin(u_parts(ph, 1, part), i, lo, hi)))
                         if j == j0 else None)

        def post_of(ph, i):
            for t, name in AFTER.items():
                if name == ph and isinstance(i, int) and i == ITERS[ph] - 1:
                    return t
            return None

        def dve_down(dve, ph, i, lo, hi, first, j0, ms):
            for m in ms:
                for part, (s0, w) in enumerate(PARTS):
                    src = product(dve, ph, i, j0 + m, part, lo, hi)
                    dst = acc[:, m, s0:s0 + w]
                    if first:
                        dve.tensor_copy(dst, src).then_inc(freed["dve"], 1)
                    else:
                        dve.tensor_tensor(dst, dst, src, ALU.add).then_inc(freed["dve"], 1)
                t = post_of(ph, i)
                if t is not None and m:
                    dve_post_add(dve, t, m - 1)
                if t is not None and m == KD - 1:
                    dve_post_add(dve, t, m)

        def pe_ffn(pe, ph, i, lo, hi):
            first = isinstance(i, int) and i == 0
            norm = 0 if ph == "ffn1" else 4
            for j in range(4):
                pe_block(pe, ph, i, j, lo, hi, h_hi, h_lo,
                         *(wait_h(pe, norm) if first and j == 0 else ()))
            pe_down(pe, ph, i, lo, hi, 4)

        def act_ffn(act, ph, i, lo, hi):
            t = post_of(ph, i)
            if isinstance(i, int) and i == 0:
                act.wait_ge(h_ready, h_count[0 if ph == "ffn1" else 4, 2])
            for j in range(6):
                act_split(act, ph, i, j, lo, hi)
                f = j // 2
                if j in (0, 2):
                    for part, (s0, w) in enumerate(PARTS):
                        src = product(act, ph, i, j, part, lo, hi)
                        if ph != "ffn1" or f or not isinstance(i, int) or i:
                            act.wait_ge(u_f_done, lin(lambda s: u_parts(ph, f, part)(s) - 3, i, lo, hi))
                        act.activation(gate_f[:, s0:s0 + w], src, ACT.Silu).then_inc(freed["act"], 1)
                if j in (1, 3):
                    for part, (s0, w) in enumerate(PARTS):
                        act.wait_ge(u_f_done, lin(u_parts(ph, f, part), i, lo, hi))
                        act.activation(u_hi[:, f, s0:s0 + w], u_f[:, s0:s0 + w], ACT.Copy).then_inc(u_hi_done, 1)
                if t is not None and j >= 4:
                    for m in range(4 * (j - 4), 4 * (j - 3)):
                        act_post_square(act, t, m)

        def dve_ffn(dve, ph, i, lo, hi, first):
            for j in range(6):
                dve_split(dve, ph, i, j, lo, hi)
                f = j // 2
                if j in (1, 3):
                    for part, (s0, w) in enumerate(PARTS):
                        src = product(dve, ph, i, j, part, lo, hi)
                        dve.wait_ge(freed["act"], lin(lambda s: PLAN.free_of[ph, s, j - 1][1] + part + 1, i, lo, hi))
                        if ph != "ffn1" or f or not isinstance(i, int) or i:
                            dve.wait_ge(u_lo_done, lin(lambda s: u_parts(ph, f, part)(s) - 3, i, lo, hi))
                        dve.tensor_tensor(u_f[:, s0:s0 + w], src, gate_f[:, s0:s0 + w],
                                          ALU.mult).then_inc(u_f_done, 1)
                    for part, (s0, w) in enumerate(PARTS):
                        dve.wait_ge(u_hi_done, lin(u_parts(ph, f, part), i, lo, hi))
                        dve.tensor_tensor(u_lo[:, f, s0:s0 + w], u_f[:, s0:s0 + w],
                                          u_hi[:, f, s0:s0 + w].bitcast(F32), ALU.subtract).then_inc(u_lo_done, 1)
                if j >= 4:
                    dve_down(dve, ph, i, lo, hi, first, 4, range(4 * (j - 4), 4 * (j - 3)))

        def steps(eng, n, body, last_apart=False):
            body(0, 0, 1, True)
            end = n - 1 if last_apart else n
            with eng.Fori(1, end) as i:
                body(i, 1, end, False)
            if last_apart:
                body(n - 1, n - 1, n, False)

        bias_mm, bias_ev, bias_out = S("bias_mm"), S("bias_ev"), S("bias_out")
        sel_in = S("sel_in")

        def pe_bias(pe):
            pe.wait_ge(sel_in, 48)
            pe.wait_ge(S("rb_one"), 1)
            pe.wait_ge(const_in, 112)
            for g in range(3):
                if g == 2:
                    pe.wait_ge(bias_ev, 1)
                pe.matmul(ps[0:3 * HPG, 6 + g % 2, 0:LREL], rb[:, :], sel_p[:, g, :],
                          start=True, stop=True).then_inc(bias_mm, 1)
            pe.wait_ge(bias_ev, 2)
            for g in range(3):
                pe.matmul(ps[:, 7, g * HPG:(g + 1) * HPG], sel_s[:, g, :], rb[:, g * HPG:(g + 1) * HPG],
                          start=True, stop=True)
            pe.matmul(ps[0:NB, 7, 16:28], sel_n[:, :], rb[:, :], start=True, stop=True).then_inc(bias_mm, 1)
            pe.wait_ge(bias_ev, 5)

        def dve_bias(dve):
            for g in range(3):
                dve.wait_ge(bias_mm, g + 1)
                dve.tensor_copy(bias_row[:, g, :], ps[0:3 * HPG, 6 + g % 2, 0:LREL]).then_inc(bias_ev, 1)
            dve.wait_ge(bias_mm, 4)
            dve.tensor_copy(bs[:, :, :], ps[:, 7, 0:12].rearrange("p (g h) -> p g h", h=HPG)).then_inc(bias_ev, 1)
            dve.tensor_copy(bn[:, :, :], ps[0:NB, 7, 16:28].rearrange("p (g h) -> p g h", h=HPG)).then_inc(bias_ev, 1)

        z_done, az_done, ez_done, l1_done, lf_done, cum_done, nc_hi, nc_done = (S(n) for n in (
            "z_done", "az_done", "ez_done", "l1_done", "lf_done", "cum_done", "nc_hi", "nc_done"))
        vt_edges = S("vt_edges")
        ncum_zero = S("ncum_zero")

        def act_forget(act):
            act_split(act, "forget", 0, 0, 0, 1)
            act.wait_ge(h_ready, h_count[2, 2])
            for part, (s0, w) in enumerate(PARTS):
                src = product(act, "forget", 0, 0, part, 0, 1)
                act.activation(lf_z[:, s0:s0 + w], src[0:NHA, :], ACT.Identity,
                               bias=bf_c[:, 0:1]).then_inc(freed["act"], 1)
            act.wait_ge(az_done, 1)
            act.activation(lf_e[:, :], lf_a[:, :], ACT.Exp, scale=-1.0).then_inc(ez_done, 1)
            act.wait_ge(ez_done, 1)
            act.activation(lf_a[:, :], lf_e[:, :], ACT.Ln, bias=one_c[0:NHA, 0:1]).then_inc(l1_done, 1)
            act.wait_ge(cum_done, 1)
            act.wait_ge(ncum_zero, 1)
            act.activation(ncum[0:NHA, :], cum, ACT.Copy, scale=-1.0).then_inc(nc_hi, 1)

        def dve_forget(dve):
            dve_split(dve, "forget", 0, 0, 0, 1)
            dve.wait_ge(h_ready, h_count[2, 2])
            dve.memset(ncum[:, :].bitcast(F32), 0.0).then_inc(ncum_zero, 1)
            dve.memset(vt_hi[:, :, 1, :].bitcast(F32), 1.0).then_inc(vt_edges, 1)
            dve.memset(vt_lo[:, :, 1, :].bitcast(F32), 0.0).then_inc(vt_edges, 1)
            dve.wait_ge(freed["act"], PLAN.free_of["forget", 0, 0][1] + 3)
            dve.scalar_tensor_tensor(out=lf_a[:, :], in0=lf_z[:, :], scalar=-1.0, in1=lf_z[:, :],
                                     op0=ALU.mult, op1=ALU.max).then_inc(az_done, 1)
            dve.wait_ge(l1_done, 1)
            dve.scalar_tensor_tensor(out=lf_a[:, :], in0=lf_z[:, :], scalar=0.0, in1=lf_a[:, :],
                                     op0=ALU.min, op1=ALU.subtract).then_inc(lf_done, 1)
            dve.memset(cum_one, 1.0).then_inc(lf_done, 1)
            dve.wait_ge(lf_done, 2)
            dve.tensor_tensor_scan(cum, cum_one, lf_a[:, 0:SEQ], 0.0, ALU.mult, ALU.add).then_inc(cum_done, 1)
            dve.wait_ge(nc_hi, 1)
            dve.scalar_tensor_tensor(out=ncum[32:32 + NHA, :], in0=cum, scalar=-1.0,
                                     in1=ncum[0:NHA, :].bitcast(F32), op0=ALU.mult,
                                     op1=ALU.subtract).then_inc(nc_done, 1)

        k_out, v_out, kf_done, vf_done, qs_done, vt_mm, vt_hi_done, vt_lo_done = (S(n) for n in (
            "k_out", "v_out", "kf_done", "vf_done", "qs_done", "vt_mm", "vt_hi_done", "vt_lo_done"))
        qk_hi, tok_mm, tok_done, tok_out, combined = (S(n) for n in (
            "qk_hi", "tok_mm", "tok_done", "tok_out", "combined"))
        FIRST_A = dict(fox=0, dil=PAIRS_A)

        def grouped(ap, dil, s0, w):
            return ap.rearrange("p (r a) -> p a r", r=dil)[:, s0 // dil:(s0 + w) // dil, :]

        def in_tokens(ap, dil):
            return ap.rearrange("p (a r) -> p a r", r=dil)

        def act_qkv(act, ph, i, lo, hi, dil):
            A0 = FIRST_A[ph]
            plain = isinstance(i, int)
            a0 = A0 + (i if plain else lo)
            for j in range(3):
                act_split(act, ph, i, j, lo, hi)
                if j == 1 and a0 == PAIRS_A + 3:
                    act.wait_ge(combined, 1)
                if j == 1 and a0 > 0:
                    act.wait_ge(k_out, lin(lambda s: 16 * (A0 + s), i, lo, hi))
                    act.wait_ge(v_out, lin(lambda s: 16 * (A0 + s), i, lo, hi))
                    act.wait_ge(tok_mm, lin(lambda s: A0 + s, i, lo, hi))
                for part, (s0, w) in enumerate(PARTS):
                    src = product(act, ph, i, j, part, lo, hi)
                    pw = min(w, SEQ - s0)
                    if j == 0:
                        if part == 2:
                            act.activation(q_s[:, :], src[:, pw:w], ACT.Copy, scale=SCALE).then_inc(qs_done, 1)
                        act.activation(grouped(q_hi[:, :], dil, s0, pw), in_tokens(src[:, 0:pw], dil), ACT.Copy,
                                       scale=SCALE).then_inc(qk_hi, 1)
                    if j == 1:
                        act.activation(k_f[:, s0:s0 + w], src, ACT.Copy).then_inc(kf_done, 1)
                        act.activation(grouped(k_hi[:, :], dil, s0, pw), in_tokens(src[:, 0:pw], dil),
                                       ACT.Copy).then_inc(qk_hi, 1)
                    if j == 2:
                        act.activation(v_f[:, s0:s0 + w], src, ACT.Copy).then_inc(vf_done, 1)
                        act.activation(grouped(v_g[:, :], dil, s0, pw), in_tokens(src[:, 0:pw], dil),
                                       ACT.Copy).then_inc(freed["act"], 1)
                if j == 0 and ph == "dil" and i and i % 3 == 0:
                    act_weights(act, i // 3 - 1)
            act.wait_ge(tok_mm, lin(lambda s: A0 + s + 1, i, lo, hi))
            if a0 > 0:
                act.wait_ge(tok_out, lin(lambda s: 16 * (A0 + s), i, lo, hi))
            act.activation(tok[:, :, :], ps[0:NB, 5, 0:3 * P].rearrange("p (c f) -> p c f", c=3),
                           ACT.Copy).then_inc(tok_done, 1)
            for n in range(2):
                act.wait_ge(vt_mm, lin(lambda s: 2 * (A0 + s) + n + 1, i, lo, hi))
                act.activation(vt_hi[:, 4 * n:4 * n + 4, 0:3:2, :],
                               bank(6 + n).rearrange("p (n h d) -> p n h d", h=2, d=HD),
                               ACT.Copy).then_inc(vt_hi_done, 1)

        def dve_qkv(dve, ph, i, lo, hi, dil):
            A0 = FIRST_A[ph]
            for j in range(3):
                dve_split(dve, ph, i, j, lo, hi)
                for part, (s0, w) in enumerate(PARTS):
                    pw = min(w, SEQ - s0)
                    if j < 2:
                        src = product(dve, ph, i, j, part, lo, hi)
                        dve.wait_ge(qk_hi, lin(lambda s: 6 * (A0 + s) + 3 * j + part + 1, i, lo, hi))
                    if j == 0:
                        dve.scalar_tensor_tensor(out=grouped(q_lo[:, :], dil, s0, pw),
                                                 in0=in_tokens(src[:, 0:pw], dil), scalar=SCALE,
                                                 in1=grouped(q_hi[:, :].bitcast(F32), dil, s0, pw),
                                                 op0=ALU.mult, op1=ALU.subtract).then_inc(freed["dve"], 1)
                    if j == 1:
                        dve.tensor_tensor(grouped(k_lo[:, :], dil, s0, pw), in_tokens(src[:, 0:pw], dil),
                                          grouped(k_hi[:, :].bitcast(F32), dil, s0, pw),
                                          ALU.subtract).then_inc(freed["dve"], 1)
                if j == 0 and ph == "dil" and i and i % 3 == 0:
                    dve_weights(dve, i // 3 - 1)
            if A0 == 0 and isinstance(i, int) and i == 0:
                dve_bias(dve)
            for n in range(2):
                dve.wait_ge(vt_hi_done, lin(lambda s: 2 * (A0 + s) + n + 1, i, lo, hi))
                dve.tensor_tensor(vt_lo[:, 4 * n:4 * n + 4, 0:3:2, :],
                                  bank(6 + n).rearrange("p (n h d) -> p n h d", h=2, d=HD),
                                  vt_hi[:, 4 * n:4 * n + 4, 0:3:2, :].bitcast(F32), ALU.subtract).then_inc(vt_lo_done, 1)

        def pe_qkv(pe, ph, i, lo, hi):
            A0 = FIRST_A[ph]
            for j in range(3):
                pe_block(pe, ph, i, j, lo, hi, h_hi, h_lo,
                         between=(lambda part: pe_combine(pe, i // 3 - 1, 3 * j + part))
                         if ph == "dil" and i and i % 3 == 0 and j < 2 else None)
            if A0 == 0 and isinstance(i, int) and i == 0:
                pe_bias(pe)
            pe.wait_ge(freed["dve"], lin(lambda s: PLAN.free_of[ph, s, 1][1] + 3, i, lo, hi))
            pe.wait_ge(freed["act"], lin(lambda s: PLAN.free_of[ph, s, 2][1] + 3, i, lo, hi))
            for n, src in enumerate((q_s[:, :], k_f[:, SEQ:T], v_f[:, SEQ:T])):
                last = pe.transpose(ps[0:NB, 5, n * P:(n + 1) * P], src, ident[:, :])
            last.then_inc(tok_mm, 1)
            if ph == "fox" and (not isinstance(i, int) or i):
                pe.wait_ge(oev_done, lin(lambda s: N_OV * s, i, lo, hi))
            if ph == "dil" and i == 0:
                pe.wait_ge(oev_done, N_OV * PAIRS_A)
            if ph == "dil" and i:
                pe.wait_ge(d_oev, 4 * i)
                if i % 3 == 0:
                    pe.wait_ge(den_read, i)
            for n in range(NQ):
                last = pe.transpose(ps[:, 6 + n // 4, (n % 4) * P:(n % 4 + 1) * P], v_g[:, n * P:(n + 1) * P],
                                    ident[:, :])
                if n % 4 == 3:
                    last.then_inc(vt_mm, 1)
            pe.wait_ge(vt_lo_done, lin(lambda s: 2 * (A0 + s) + 2, i, lo, hi))
            pe.wait_ge(tok_done, lin(lambda s: A0 + s + 1, i, lo, hi))

        sc_done, mx_done, ex_done, rs_done, tr_done, pth_done, ptl_done, ov_done, oev_done, psel_done = (
            S("fox_" + n) for n in ("scores", "max", "exp", "rsum", "turned", "pt_hi", "pt_lo", "ov",
                                    "ov_read", "pair_sel"))
        TILES = [(hh, 2 * b + odd) for hh, b, _ in UNITS for odd in range(2)]
        TURNS = [(s, half) for s, (_, i) in enumerate(TILES) for half in range(1 + (i >= 4))]
        N_TILE, N_TURN, N_OV = len(TILES), len(TURNS), len(UNITS)

        def with_ones(v, j, hh):
            return v[:, j, hh:hh + 2, :].rearrange("p a d -> p (a d)")

        def turns_of(s):
            return [(n, half) for n, (s_, half) in enumerate(TURNS) if s_ == s]

        def pe_fox(pe, p, lo, hi):
            def scores(s):
                hh, i = TILES[s]
                rows, n = slice(HD * hh, HD * hh + HD), P * (i + 1)
                if s >= 2:
                    pe.wait_ge(ex_done, lin(lambda x: N_TILE * x + s - 1, p, lo, hi))
                for c0 in range(0, n, 512):
                    c1 = min(c0 + 512, n)
                    out = ps[:, 2 * (s % 2) + c0 // 512, 0:c1 - c0]
                    qs = slice(i * P, (i + 1) * P)
                    pe.matmul(out, q_hi[rows, qs], k_hi[rows, c0:c1], start=True, stop=False)
                    pe.matmul(out, q_hi[rows, qs], k_lo[rows, c0:c1], start=False, stop=False)
                    pe.matmul(out, q_lo[rows, qs], k_hi[rows, c0:c1], start=False, stop=False)
                    if c1 == n:
                        pe.matmul(out[:, c1 - c0 - P:c1 - c0], ident_b[:, :], causal_b[:, :],
                                  start=False, stop=False, skip_group_check=True)
                    last = pe.matmul(out, pair_sel[:, hh, :], ncum[:, c0:c1], start=False, stop=True)
                last.then_inc(sc_done, 1)

            def turn(s):
                hh, i = TILES[s]
                pe.wait_ge(ex_done, lin(lambda x: N_TILE * x + s + 1, p, lo, hi))
                for e, half in turns_of(s):
                    if e >= 2:
                        pe.wait_ge(ptl_done, lin(lambda x: N_TURN * x + e - 1, p, lo, hi))
                    for n in range(4 * half, min(4 * half + 4, i + 1)):
                        last = pe.transpose(ps[:, 4 + e % 2, (n % 4) * P:(n % 4 + 1) * P],
                                            prob[:, s % 2, n * P:(n + 1) * P], ident[:, :])
                    last.then_inc(tr_done, 1)

            def values(u):
                hh, b, at = UNITS[u]
                i = 2 * b + 1
                pe.wait_ge(ptl_done, lin(lambda x: N_TURN * x + turns_of(2 * u + 1)[-1][0] + 1, p, lo, hi))
                if u >= 2:
                    pe.wait_ge(oev_done, lin(lambda x: N_OV * x + u - 1, p, lo, hi))
                for j in range(i + 1):
                    c0 = P if j == i else 0
                    out = ps[:, 6 + u % 2, c0:256]
                    for n, (v, t) in enumerate(((vt_hi, pt_hi), (vt_hi, pt_lo), (vt_lo, pt_hi))):
                        last = pe.matmul(out, with_ones(v, j, hh), t[:, at + j, c0:256], start=(j == 0 and n == 0),
                                         stop=(j == i and n == 2), skip_group_check=True)
                last.then_inc(ov_done, 1)

            pe.wait_ge(vt_edges, 2)
            pe.wait_ge(psel_done, lin(lambda x: x + 1, p, lo, hi))
            pe.wait_ge(nc_done, 1)
            scores(0)
            for s in range(N_TILE):
                if s + 1 < N_TILE:
                    scores(s + 1)
                turn(s)
                if s and s % 2 == 0:
                    values(s // 2 - 1)
            values(N_OV - 1)

        def act_fox(act, p, lo, hi):
            def exp(s):
                n = P * (TILES[s][1] + 1)
                act.wait_ge(mx_done, lin(lambda x: N_TILE * x + s + 1, p, lo, hi))
                act.activation(prob[:, s % 2, 0:n], psf[:, 1024 * (s % 2):1024 * (s % 2) + n], ACT.Exp,
                               bias=nmax[:, s % 2:s % 2 + 1]).then_inc(ex_done, 1)

            sel = head_sel[:, 2 * p:2 * p + 2] if isinstance(p, int) else head_sel[:, bass.ds(2 * p, 2)]
            act.wait_ge(const_in, 112)
            act.activation(pair_sel[:, :, :], sel.unsqueeze(2).broadcast_to([P, 2, P]), ACT.Copy).then_inc(psel_done, 1)
            exp(0)
            for s in range(N_TILE):
                i, at = TILES[s][1], UNITS[s // 2][2]
                if s >= 4 and s % 2 == 0:
                    act.wait_ge(ov_done, lin(lambda x: N_OV * x + s // 2 - 1, p, lo, hi))
                for e, half in turns_of(s):
                    nb = min(4, i + 1 - 4 * half)
                    act.wait_ge(tr_done, lin(lambda x: N_TURN * x + e + 1, p, lo, hi))
                    act.activation(pt_hi[:, at + 4 * half:at + 4 * half + nb, (i % 2) * P:(i % 2 + 1) * P],
                                   bank(4 + e % 2, nb * P).rearrange("p (n c) -> p n c", c=P),
                                   ACT.Copy).then_inc(pth_done, 1)
                if s + 1 < N_TILE:
                    exp(s + 1)

        def dve_fox(dve, p, lo, hi):
            def biggest(s):
                n = P * (TILES[s][1] + 1)
                dve.wait_ge(sc_done, lin(lambda x: N_TILE * x + s + 1, p, lo, hi))
                dve.tensor_reduce(nmax[:, s % 2:s % 2 + 1], psf[:, 1024 * (s % 2):1024 * (s % 2) + n], AX.X,
                                  ALU.max, negate=True).then_inc(mx_done, 1)

            def out(u):
                hh, b, _ = UNITS[u]
                rows, others = slice(HD * hh, HD * hh + HD), slice(HD - HD * hh, P - HD * hh)
                dve.wait_ge(ov_done, lin(lambda x: N_OV * x + u + 1, p, lo, hi))
                if u or not isinstance(p, int) or p:
                    dve.wait_ge(oev_done, lin(lambda x: N_OV * x + u, p, lo, hi))
                dve.reciprocal(rsum[rows, :], ps[others, 6 + u % 2, 0:256]).then_inc(rs_done, 1)
                dve.wait_ge(rs_done, lin(lambda x: N_OV * x + u + 1, p, lo, hi))
                dst = o_st[rows, p, 256 * b:256 * (b + 1)] if isinstance(p, int) else \
                    o_st[rows, bass.ds(p, 1), 256 * b:256 * (b + 1)].rearrange("p a c -> p (a c)")
                dve.tensor_tensor(dst, ps[rows, 6 + u % 2, 0:256], rsum[rows, :], ALU.mult).then_inc(oev_done, 1)

            biggest(0)
            for s in range(N_TILE):
                if s + 1 < N_TILE:
                    biggest(s + 1)
                i, at = TILES[s][1], UNITS[s // 2][2]
                for e, half in turns_of(s):
                    nb = min(4, i + 1 - 4 * half)
                    sl = (slice(None), slice(at + 4 * half, at + 4 * half + nb), slice((i % 2) * P, (i % 2 + 1) * P))
                    dve.wait_ge(pth_done, lin(lambda x: N_TURN * x + e + 1, p, lo, hi))
                    dve.tensor_tensor(pt_lo[sl], bank(4 + e % 2, nb * P).rearrange("p (n c) -> p n c", c=P),
                                      pt_hi[sl].bitcast(F32), ALU.subtract).then_inc(ptl_done, 1)
                if s >= 4 and s % 2 == 0:
                    out(s // 2 - 2)
            out(N_OV - 2)
            out(N_OV - 1)

        d_sc, d_mt, d_mx, d_ex, d_tr, d_pth, d_ptl, d_val, d_oev, bias_in = (S("dil_" + n) for n in (
            "scores", "biased", "max", "exp", "turned", "pt_hi", "pt_lo", "value", "ov_read", "bias"))

        def has_prev(g, n):
            per = SEQ // DIL[g] // P
            return per > 0 and n % per != 0

        def pe_dil(pe, d, g):
            def scores(s):
                hh, n = s // NQ, s % NQ
                rows = slice(HD * hh, HD * hh + HD)
                if s >= 4:
                    pe.wait_ge(d_mt, 16 * d + s - 3)
                k0, c0 = ((n - 1) * P, 0) if has_prev(g, n) else (n * P, P)
                out = ps[:, s % 4, c0:256]
                for m, (a, b) in enumerate(((q_hi, k_hi), (q_hi, k_lo), (q_lo, k_hi))):
                    last = pe.matmul(out, a[rows, n * P:(n + 1) * P], b[rows, k0:(n + 1) * P],
                                     start=(m == 0), stop=(m == 2))
                last.then_inc(d_sc, 1)

            def turn(s):
                n = s % NQ
                pe.wait_ge(d_ex, 16 * d + s + 1)
                if s >= 2:
                    pe.wait_ge(d_ptl, 16 * d + s - 1)
                for c0 in ((0, P) if has_prev(g, n) else (P,)):
                    last = pe.transpose(ps[:, 4 + s % 2, c0:c0 + P], prob_b[:, s % 4, c0:c0 + P], ident[:, :])
                last.then_inc(d_tr, 1)

            def value(hh, j):
                pe.wait_ge(d_ptl, 16 * d + NQ * hh + min(j + 2, NQ))
                if hh and j in (0, 3):
                    pe.wait_ge(d_oev, 4 * d + 1 + (j == 3))
                end = j + 1 + (j + 1 < NQ and has_prev(g, j + 1))
                for b0, b1 in ([(j, end)] if j // 4 == (end - 1) // 4 else [(j, j + 1), (j + 1, end)]):
                    out = ps[:, 6 + b0 // 4, (b0 % 4) * P:(b0 % 4) * P + (b1 - b0) * P]
                    cs = slice((b0 - j) * P, (b1 - j) * P)
                    for v, t in ((vt_hi, pt_hi), (vt_hi, pt_lo), (vt_lo, pt_hi)):
                        last = pe.matmul(out, with_ones(v, j, hh), t[:, j, cs], start=((hh, b0 // 4) not in begun),
                                         stop=True, skip_group_check=True)
                        begun.add((hh, b0 // 4))
                last.then_inc(d_val, 1)

            begun = set()
            for s in range(3):
                scores(s)
            for s in range(16):
                turn(s)
                if s + 3 < 16:
                    scores(s + 3)
                if s >= 2:
                    value((s - 2) // NQ, (s - 2) % NQ)
            value(1, NQ - 2)
            value(1, NQ - 1)

        def act_dil(act, d, g):
            def exp(s):
                hh, n = s // NQ, s % NQ
                c0 = 0 if has_prev(g, n) else P
                act.wait_ge(d_mx, 16 * d + s + 1)
                if s >= 4:
                    act.wait_ge(d_tr, 16 * d + s - 3)
                act.activation(prob_b[:, s % 4, c0:256], score_b[:, s % 4, c0:256], ACT.Exp,
                               bias=nmx[:, g, hh, n:n + 1], accum_out=den[:, g, hh, n:n + 1]).then_inc(d_ex, 1)

            def out(hh, half):
                rows, cs = slice(HD * hh, HD * hh + HD), slice(512 * half, 512 * half + 512)
                act.wait_ge(d_val, 16 * d + NQ * hh + 4 * half + 4)
                act.activation(o_g[rows, g, cs], ps[rows, 6 + half, :], ACT.Copy).then_inc(d_oev, 1)

            ptf = pt_hi[:, :, :].rearrange("p n c -> p (n c)")
            exp(0)
            exp(1)
            for s in range(16):
                n = s % NQ
                w = 256 if has_prev(g, n) else P
                if s >= NQ:
                    act.wait_ge(d_val, 16 * d + n + 1)
                act.wait_ge(d_tr, 16 * d + s + 1)
                act.activation(ptf[:, n * 256 + P - w:n * 256 + P], ps[:, 4 + s % 2, 256 - w:256],
                               ACT.Copy).then_inc(d_pth, 1)
                if s + 2 < 16:
                    exp(s + 2)
                if s in OUT_AT:
                    out(*OUT_AT[s])
            out(1, 0)
            out(1, 1)

        OUT_AT = {7: (0, 0), 11: (0, 1)}

        def dve_dil(dve, d, g):
            def biased(s):
                hh, n = s // NQ, s % NQ
                c0 = 0 if has_prev(g, n) else P
                if s == 0:
                    dve.wait_ge(S(f"bias_dma{d % 2}"), 32 * (d // 2 + 1))
                    if g == 2:
                        dve.wait_ge(bias_in, d // 3 + 1)
                dve.wait_ge(d_sc, 16 * d + s + 1)
                if s >= 4:
                    dve.wait_ge(d_ex, 16 * d + s - 3)
                dve.tensor_tensor_reduce(score_b[:, s % 4, c0:256], ps[:, s % 4, c0:256],
                                         bias_t[:, d % 2, hh, c0:256], 1.0, -3.0e38, ALU.add, ALU.max,
                                         mx[:, g, hh, n:n + 1]).then_inc(d_mt, 1)
                dve.wait_ge(d_mt, 16 * d + s + 1)
                dve.tensor_scalar(nmx[:, g, hh, n:n + 1], mx[:, g, hh, n:n + 1], -1.0, None,
                                  ALU.mult).then_inc(d_mx, 1)

            lof = pt_lo[:, :, :].rearrange("p n c -> p (n c)")
            hif = pt_hi[:, :, :].rearrange("p n c -> p (n c)").bitcast(F32)
            biased(0)
            biased(1)
            for s in range(16):
                if s + 2 < 16:
                    biased(s + 2)
                n = s % NQ
                w = 256 if has_prev(g, n) else P
                sl = slice(n * 256 + P - w, n * 256 + P)
                dve.wait_ge(d_pth, 16 * d + s + 1)
                dve.tensor_tensor(lof[:, sl], ps[:, 4 + s % 2, 256 - w:256], hif[:, sl],
                                  ALU.subtract).then_inc(d_ptl, 1)

        wide_set, wide_mm, m_ev, w_sub, w_exp, cb_step = (S("cb_" + n) for n in (
            "wide", "spread", "max_ev", "sub", "exp", "step"))

        den_read = S("cb_den_read")

        def pe_combine(pe, pair, step):
            kind, g = step // 3, step % 3
            pe.wait_ge(wide_set, 6 * pair + step + 1)
            if step == 0:
                pe.wait_ge(d_oev, 4 * 3 * (pair + 1))
            elif step <= 3:
                pe.wait_ge(m_ev, 3 * pair + step)
            else:
                pe.wait_ge(den_read, 3 * pair + g)
            for n in range(NQ):
                last = pe.matmul(ps[:, 6 + n // 4, (n % 4) * P:(n % 4 + 1) * P],
                                 wide[:, n, :, :].rearrange("p h d -> p (h d)"), ident[:, :], start=True, stop=True)
            last.then_inc(wide_mm, 1)

        def group_view(g, ap):
            return ap.rearrange("p (r a) -> p a r", r=DIL[g])

        def act_maxima(act, pair):
            for g in range(3):
                act.wait_ge(wide_mm, 6 * pair + g + 1)
                act.activation(in_tokens(wg[:, g, :], DIL[g]), group_view(g, psf[:, 6 * 512:8 * 512]),
                               ACT.Copy).then_inc(m_ev, 1)

        def act_weights(act, pair):
            act.wait_ge(w_sub, pair + 1)
            act.activation(wg[:, :, :], wg[:, :, :], ACT.Exp).then_inc(w_exp, 1)

        cb_count = [0]

        def cb_link(dve, ins):
            cb_count[0] += 1
            ins.then_inc(cb_step, 1)
            dve.wait_ge(cb_step, cb_count[0])

        def dve_widen(dve, pair, step):
            src = (mx, den)[step // 3]
            if step:
                dve.wait_ge(wide_mm, 6 * pair + step)
            dve.tensor_copy(wide[:, :, :, :], src[:, step % 3, :, :].rearrange("p h n -> p n h").unsqueeze(3)
                            .broadcast_to([P, NQ, 2, HD])).then_inc(wide_set, 1)

        def dve_maxima(dve, pair):
            dve.wait_ge(d_ex, 16 * 3 * (pair + 1))
            for step in range(4):
                dve_widen(dve, pair, step)
            dve.wait_ge(m_ev, 3 * pair + 3)
            dve.wait_ge(k_out, 16 * (PAIRS_A + 3 * pair + 3))
            dve.wait_ge(v_out, 16 * (PAIRS_A + 3 * pair + 3))
            cb_link(dve, dve.tensor_tensor(mxall, wg[:, 0, :], wg[:, 1, :], ALU.max))
            cb_link(dve, dve.tensor_tensor(mxall, mxall, wg[:, 2, :], ALU.max))
            dve.tensor_tensor(wg[:, :, :], wg[:, :, :], mxall.unsqueeze(1).broadcast_to([P, 3, SEQ]),
                              ALU.subtract).then_inc(w_sub, 1)
            dve.wait_ge(w_sub, pair + 1)

        def dve_weights(dve, pair):
            dve.wait_ge(w_exp, pair + 1)
            for g in range(3):
                if g < 2:
                    dve_widen(dve, pair, 4 + g)
                dve.wait_ge(wide_mm, 6 * pair + 4 + g)
                dst = mxall if g else tsum
                dve.tensor_tensor(in_tokens(dst, DIL[g]), in_tokens(wg[:, g, :], DIL[g]),
                                  group_view(g, psf[:, 6 * 512:8 * 512]), ALU.mult).then_inc(den_read, 1)
                dve.wait_ge(den_read, 3 * pair + g + 1)
                if g:
                    cb_link(dve, dve.tensor_tensor(tsum, tsum, mxall, ALU.add))
            cb_link(dve, dve.reciprocal(tsum, tsum))
            dve.wait_ge(num_done, 5 * (pair + 1))
            dve.tensor_tensor(o_st[:, PAIRS_A + pair, 0:SEQ], o_g[:, 0, :], tsum, ALU.mult).then_inc(combined, 1)

        num_done = S("cb_numerator")

        def pool_weights(pool, pair):
            pool.wait_ge(w_exp, pair + 1)
            pool.wait_ge(d_oev, 4 * 3 * (pair + 1))
            for n in range(5):
                if n:
                    pool.wait_ge(num_done, 5 * pair + n)
                g = n if n < 3 else n - 2
                if n < 3:
                    pool.tensor_tensor(group_view(g, o_g[:, g, :]), group_view(g, o_g[:, g, :]),
                                       in_tokens(wg[:, g, :], DIL[g]), ALU.mult).then_inc(num_done, 1)
                else:
                    pool.tensor_tensor(in_tokens(o_g[:, 0, :], DIL[g]), in_tokens(o_g[:, 0, :], DIL[g]),
                                       group_view(g, o_g[:, g, :]), ALU.add).then_inc(num_done, 1)

        kc_in = [S("kc_in0"), S("kc_in1")]
        kc_used, kc_zero, s_in, s_dot, s_step, s_rows, s_mm, s_ev, p_ready, v_mm, s_out = (S("smp_" + n) for n in (
            "kc_used", "kc_zero", "in", "dot", "step", "rows", "mm", "ev", "p_ready", "v_mm", "out"))
        lf_out = S("lf_out")
        A_LAST = PAIRS_A + 3 * PAIRS_B

        def pool_cache(pool, kv):
            def load(b, slot):
                if kv and b >= 2:
                    pool.wait_ge(v_mm, b - 1)
                elif kv or b >= 2:
                    pool.wait_ge(kc_used, NB * kv + b - 1)
                if isinstance(b, int):
                    bsl = lambda t: t[b:b + 1]
                else:
                    bsl = lambda t: t[bass.ds(b, 1)]
                src = A["cache_a_v"] if kv else A["cache_a_k"]
                for pg in range(NPAGE):
                    page = pool.value_load(pages[0:1, bass.ds(b * NPAGE + pg, 1)] if not isinstance(b, int) else
                                           pages[0:1, b * NPAGE + pg:b * NPAGE + pg + 1],
                                           min_val=0, max_val=A["cache_a_k"].shape[0] - 1)
                    pool.dma_start(kc_a[:, slot, pg, :], src[bass.ds(page, 1)].rearrange("a p c -> (a p) c")
                                   ).then_inc(kc_in[slot], 16)
                    if not kv:
                        dst = lfp[:, pg, b, :] if isinstance(b, int) else \
                            lfp[:, pg, bass.ds(b, 1), :].rearrange("p a c -> p (a c)")
                        pool.dma_start(dst, A["cache_a_logf"][bass.ds(page, 1)].rearrange("a p c -> (a p) c")
                                       ).then_inc(kc_in[slot], 16)
                for g, (name, n) in enumerate(zip(("b1", "b2", "b3"), SAMPLE_KEYS)):
                    cache = A["cache_" + name]
                    step = cache.shape[1] // n
                    one = bsl(cache).rearrange("a (n s) c -> (a n) s c", s=step)[:, 0, kv * 256:(kv + 1) * 256]
                    pool.dma_start(kc_b[0:n, slot, g, :], one).then_inc(kc_in[slot], 16)
                if not kv:
                    pool.dma_start(qb[:, slot, :], bsl(qkv_s)[:, 0, :].broadcast_to([P, WA + WB])
                                   ).then_inc(kc_in[slot], 16)
            for b in range(NB):
                load(b, b % 2)

        def pool_samples(pool):
            pool.wait_ge(tok_out, 16 * A_LAST)
            pool.wait_ge(lf_out, 16)
            pool.wait_ge(combined, PAIRS_B)
            pool.wait_ge(tok_done, A_LAST)
            pool.dma_start(kn[:, :], qkv_s[:, 1, :]).then_inc(s_in, 16)
            pool.dma_start(qn[:, :], qkv_s[:, 0, :]).then_inc(s_in, 16)
            pool.dma_start(vn[:, :], qkv_s[:, 2, :]).then_inc(s_in, 16)
            pool.dma_start(lf_new[:, :], A["lf_t"][:, SEQ:T].rearrange("h b -> b h").unsqueeze(2),
                           allow_slow_non_contiguous=True).then_inc(s_in, 16)
            pool.dma_start(upto[:, :], A["upto"]).then_inc(s_in, 16)
            pool.dma_start(own_a[:, :], A["own_a"]).then_inc(s_in, 16)
            pool.dma_start(own_b[:, :], A["own_b"]).then_inc(s_in, 16)
            pool.dma_start(head_a[:, :], A["head_a"]).then_inc(s_in, 16)
            pool.dma_start(head_b[:, :], A["head_b"]).then_inc(s_in, 16)
            pool.memset(kc_b[:, :, :, :], 0.0).then_inc(kc_zero, 1)
            pool.memset(p_a[:, :, :], 0.0).then_inc(kc_zero, 1)
            pool.memset(p_b[:, :, :], 0.0).then_inc(kc_zero, 1)
            pool.wait_ge(kc_zero, 3)
            pool_cache(pool, 0)
            pool_cache(pool, 1)

        K_IN, V_IN = 16 * (2 * NPAGE + 3 + 1), 16 * (NPAGE + 3)

        def dve_gates(dve):
            cnt = [0]

            def dot(b, slot, i):
                dve.wait_ge(kc_in[slot], i * K_IN + K_IN)
                s3 = (lambda t, n: t[:, :, b, :]) if isinstance(b, int) else \
                    (lambda t, n: t[:, :, bass.ds(b, 1), :].rearrange("p g a h -> p g (a h)"))
                dve.tensor_tensor(prod[:, 0:NPAGE * WA].rearrange("p (g c) -> p g c", c=WA), kc_a[:, slot, :, :],
                                  qb[:, slot, 0:WA].unsqueeze(1).broadcast_to([P, NPAGE, WA]), ALU.mult)
                dve.tensor_tensor(prod[:, NPAGE * WA:NPAGE * WA + WB],
                                  kc_b[:, slot, :, :].rearrange("p g c -> p (g c)"), qb[:, slot, WA:WA + WB],
                                  ALU.mult).then_inc(s_dot, 1)
                dve.wait_ge(s_dot, lin(lambda s: 2 * s + (slot + 1), i, 1, NB // 2))
                dve.tensor_reduce(s3(s_a, 0), prod[:, 0:NPAGE * WA].rearrange("p (g h d) -> p g h d", g=NPAGE, d=HD),
                                  AX.X, ALU.add)
                dve.tensor_reduce(s3(s_b, 0), prod[:, NPAGE * WA:].rearrange("p (g h d) -> p g h d", g=3, d=HD),
                                  AX.X, ALU.add).then_inc(kc_used, 1)
                dve.wait_ge(kc_used, lin(lambda s: 2 * s + (slot + 1), i, 1, NB // 2))

            def link(ins):
                cnt[0] += 1
                ins.then_inc(s_step, 1)
                dve.wait_ge(s_step, cnt[0])

            for n in range(ROWS + 1):
                dve_split(dve, "gates", 0, n, 0, 1)
                if n == 0:
                    dve_weights(dve, PAIRS_B - 1)
                if n == 2:
                    dve.wait_ge(s_in, 144)
                    link(dve.tensor_tensor(qn[:, :], kn[:, :], qn[:, :], ALU.mult))
                    link(dve.tensor_reduce(s_own[:, :], qn[:, :].rearrange("p (h d) -> p h d", d=HD), AX.X, ALU.add))
                    dve.tensor_copy(sn_a[:, :, :], s_own[:, 0:NHA].unsqueeze(1).broadcast_to([NB, NB, NHA]))
                    for g in range(3):
                        own = s_own[:, NHA + g * HPG:NHA + (g + 1) * HPG]
                        last = dve.tensor_tensor(sn_b[:, g, :, :], own.unsqueeze(1).broadcast_to([NB, NB, HPG]),
                                                 bn[:, g, :].unsqueeze(1).broadcast_to([NB, NB, HPG]), ALU.add)
                    last.then_inc(s_new, 1)
                for b in DOTS.get(n, ()):
                    dot(b, b % 2, b // 2)
            dve.tensor_tensor(s_b[:, :, :, :], s_b[:, :, :, :],
                              bs[:, :, :].unsqueeze(2).broadcast_to([P, 3, NB, HPG]), ALU.add).then_inc(s_rows, 1)
            dve_split(dve, "gates", 0, ROWS + 1, 0, 1)
            dve.wait_ge(s_ev, 1)
            dve.wait_ge(s_mm, 1)
            link(dve.tensor_tensor(cols[:, 0:1], crow[:, 255:256], lf_new[:, :], ALU.add))
            link(dve.tensor_scalar(crow[:, :], crow[:, :], cols[:, 0:1], -1.0, ALU.subtract, ALU.mult))
            link(dve.tensor_tensor(row_a[:, 0:256], row_a[:, 0:256], crow[:, :], ALU.add))
            link(dve.tensor_tensor(row_a[:, 256:264], row_a[:, 256:264], own_a[:, :], ALU.add))
            link(dve.tensor_tensor(row_b[:, 384:408].rearrange("p (g b) -> p g b", g=3),
                                   row_b[:, 384:408].rearrange("p (g b) -> p g b", g=3),
                                   own_b[:, :].unsqueeze(1).broadcast_to([32, 3, NB]), ALU.add))
            link(dve.tensor_reduce(cols[:, 1:2], row_a[:, :], AX.X, ALU.max, negate=True))
            dve.tensor_reduce(cols[0:32, 2:3], row_b[:, :], AX.X, ALU.max, negate=True).then_inc(s_rows, 1)
            dve.wait_ge(s_ev, 3)
            link(dve.reciprocal(cols[:, 5:6], cols[:, 3:4]))
            link(dve.reciprocal(cols[0:32, 6:7], cols[0:32, 4:5]))
            dve.tensor_scalar(row_a[:, :], row_a[:, :], cols[:, 5:6], None, ALU.mult)
            dve.tensor_scalar(row_b[:, :], row_b[:, :], cols[0:32, 6:7], None, ALU.mult).then_inc(s_rows, 1)

            for n in range(ROWS + 2, 2 * KD):
                dve_split(dve, "gates", 0, n, 0, 1)
                if n == VALUES_END:
                    dve.wait_ge(v_mm, NB)
                    dve.tensor_tensor(masked[:, 0:WA].rearrange("p (h d) -> p h d", d=HD),
                                      ps[0:64, 7, 0:WA].rearrange("p (h d) -> p h d", d=HD),
                                      head_a[:, :].unsqueeze(2).broadcast_to([64, NHA, HD]), ALU.mult)
                    link(dve.tensor_tensor(masked[0:32, WA:].rearrange("p (h d) -> p h d", d=HD),
                                           ps[0:32, 6, 0:256].rearrange("p (h d) -> p h d", d=HD),
                                           head_b[:, :].unsqueeze(2).broadcast_to([32, HPG, HD]), ALU.mult))
                    dve.tensor_reduce(o_rows[:, 0, :], masked[:, 0:WA].rearrange("p (h d) -> p d h", d=HD),
                                      AX.X, ALU.add)
                    dve.tensor_reduce(o_rows[0:32, 1, :], masked[0:32, WA:].rearrange("p (h d) -> p d h", d=HD),
                                      AX.X, ALU.add).then_inc(o_rows_done, 1)

        DOTS = {3: (0,), 4: (1,), 5: (2, 3), 6: (4,), 7: (5,), 8: (6,), 9: (7,)}
        ROWS = 10
        VALUES = {12: (0, 1), 13: (2, 3), 14: (4, 5), 15: (6, 7)}
        VALUES_END = 15
        s_new = S("smp_new")
        o_rows_done = S("smp_o_rows")

        def flat(t):
            return t.rearrange("p b h -> p (b h)")

        def pe_rows(pe):
            pe.wait_ge(s_new, 1)
            pe.wait_ge(den_read, 3 * PAIRS_B)
            pe.wait_ge(s_rows, 1)
            for pg in range(NPAGE):
                pe.transpose(ps[0:64, 6, 256 + pg * P:256 + (pg + 1) * P], flat(s_a[:, pg, :, :]), ident[:, :])
            pe.transpose(ps[0:64, 7, 408:416], flat(sn_a[:, :, :]), ident[0:NB, 0:NB])
            for g in range(3):
                pe.transpose(ps[0:32, 7, g * P:(g + 1) * P], flat(s_b[:, g, :, :]), ident[:, :])
                pe.transpose(ps[0:32, 7, 384 + g * NB:384 + (g + 1) * NB], flat(sn_b[:, g, :, :]),
                             ident[0:NB, 0:NB])
            pe.matmul(ps[0:64, 6, 0:P], flat(lfp[:, 0, :, :]), upto[:, :], start=True, stop=True)
            pe.matmul(ps[0:64, 6, P:2 * P], flat(lfp[:, 0, :, :]), ones[:, :], start=True, stop=False)
            pe.matmul(ps[0:64, 6, P:2 * P], flat(lfp[:, 1, :, :]), upto[:, :], start=False,
                      stop=True).then_inc(s_mm, 1)

        def pe_columns(pe):
            pe.wait_ge(s_rows, 3)
            i64, i32 = ident[0:64, 0:64], ident[0:32, 0:32]
            for pg in range(NPAGE):
                pe.transpose(ps[:, 6, pg * 64:(pg + 1) * 64], row_a[:, pg * P:(pg + 1) * P], i64)
            pe.transpose(ps[0:NB, 6, 256:320], row_a[:, 256:264], i64)
            for g in range(3):
                pe.transpose(ps[:, 6, P + g * 32:P + (g + 1) * 32], row_b[:, g * P:(g + 1) * P], i32)
                last = pe.transpose(ps[0:NB, 6, 320 + g * 32:352 + g * 32],
                                    row_b[:, 384 + g * NB:384 + (g + 1) * NB], i32)
            last.then_inc(s_mm, 1)

        def pe_values(pe, b):
            if b == 0:
                pe.wait_ge(p_ready, 1)
                pe.matmul(ps[0:64, 7, 0:WA], flat(pn_a[:, :, :]), vn[:, 0:WA], start=True, stop=False)
                for g in range(3):
                    pe.matmul(ps[0:32, 6, 0:256], flat(pn_b[:, g, :, :]), vn[:, WA + g * 256:WA + (g + 1) * 256],
                              start=(g == 0), stop=False)
            pe.wait_ge(kc_in[b % 2], NB // 2 * K_IN + (b // 2 + 1) * V_IN)
            end = b == NB - 1
            for pg in range(NPAGE):
                pe.matmul(ps[0:64, 7, 0:WA], p_a[:, pg, b * 64:(b + 1) * 64], kc_a[:, b % 2, pg, :],
                          start=False, stop=(end and pg == NPAGE - 1))
            for g in range(3):
                last = pe.matmul(ps[0:32, 6, 0:256], p_b[:, g, b * 32:(b + 1) * 32], kc_b[:, b % 2, g, :],
                                 start=False, stop=(end and g == 2))
            last.then_inc(v_mm, 1)

        def pe_gates(pe):
            for n in range(2 * KD):
                pe_block(pe, "gates", 0, n, 0, 1, h_hi, h_lo,
                         between=(lambda part: pe_combine(pe, PAIRS_B - 1, 3 * n + part)) if n < 2 else None)
                if n == ROWS:
                    pe_rows(pe)
                if n == ROWS + 1:
                    pe_columns(pe)
                for b in VALUES.get(n, ()):
                    pe_values(pe, b)
            pe.wait_ge(o_rows_done, 1)
            pe.transpose(ps[0:HD, 6, 0:64], o_rows[:, 0, :], ident[0:64, 0:64])
            pe.transpose(ps[0:HD, 6, 64:96], o_rows[0:32, 1, :], ident[0:32, 0:32]).then_inc(s_mm, 1)

        def act_rows(act):
            act.wait_ge(s_mm, 1)
            act.activation(row_a[:, 0:256], ps[0:64, 6, 256:512], ACT.Copy)
            act.activation(row_a[:, 256:264], ps[0:64, 7, 408:416], ACT.Copy)
            act.activation(crow[:, :], ps[0:64, 6, 0:256], ACT.Copy)
            act.activation(row_b[:, :], ps[0:32, 7, 0:408], ACT.Copy).then_inc(s_ev, 1)
            act.wait_ge(s_rows, 2)
            act.activation(row_a[:, :], row_a[:, :], ACT.Exp, bias=cols[:, 1:2],
                           accum_out=cols[:, 3:4]).then_inc(s_ev, 1)
            act.activation(row_b[:, :], row_b[:, :], ACT.Exp, bias=cols[0:32, 2:3],
                           accum_out=cols[0:32, 4:5]).then_inc(s_ev, 1)

        def act_columns(act):
            act.wait_ge(s_mm, 2)
            act.wait_ge(kc_zero, 3)
            act.activation(p_a[:, :, :].rearrange("p g (b c) -> p g b c", c=72)[:, :, :, 0:NHA],
                           ps[:, 6, 0:P].rearrange("p (g b h) -> p g b h", g=2, h=NHA), ACT.Copy)
            act.activation(p_b[:, :, :].rearrange("p g (b c) -> p g b c", c=36)[:, :, :, 0:HPG],
                           ps[:, 6, P:P + 96].rearrange("p (g b h) -> p g b h", g=3, h=HPG), ACT.Copy)
            act.activation(pn_a[:, :, :], ps[0:NB, 6, 256:320].rearrange("p (b h) -> p b h", h=NHA), ACT.Copy)
            act.activation(pn_b[:, :, :, :], ps[0:NB, 6, 320:416].rearrange("p (g b h) -> p g b h", g=3, h=HPG),
                           ACT.Copy).then_inc(p_ready, 1)

        z_done = S("mg_z")
        g_out = [S(f"gate_out{n}") for n in range(GATE_SLOTS)]
        g_in = [S(f"gate_in{n}") for n in range(2)]

        def act_gates(act):
            for n in range(2 * KD):
                act_split(act, "gates", 0, n, 0, 1)
                if n == ROWS + 1:
                    act_rows(act)
                if n == ROWS + 2:
                    act_columns(act)
                if n >= GATE_SLOTS:
                    act.wait_ge(g_out[n % GATE_SLOTS], 16 * (n // GATE_SLOTS))
                for part, (s0, w) in enumerate(PARTS):
                    act.activation(gate_st[:, n % GATE_SLOTS, s0:s0 + w], product(act, "gates", 0, n, part, 0, 1),
                                   ACT.Sigmoid).then_inc(freed["act"], 1)
                act.wait_ge(freed["act"], PLAN.free_of["gates", 0, n][1] + 3)
                act.dma_start(gates_s[n], gate_st[:, n % GATE_SLOTS, :]).then_inc(g_out[n % GATE_SLOTS], 16)
                if n == 0:
                    act_weights(act, PAIRS_B - 1)
            act.wait_ge(s_mm, 3)
            for hh in range(2):
                rows = slice(HD * hh, HD * hh + HD)
                for c0, n, h, t0 in ((0, 64, NHA, 0), (64, 32, HPG, PAIRS_A)):
                    last = act.activation(o_st[rows, t0:t0 + h // 2, SEQ:T],
                                          ps[0:HD, 6, c0:c0 + n].rearrange("d (b t h) -> d t b h", t=h // 2, h=2)
                                          [:, :, :, hh], ACT.Copy)
            last.then_inc(s_out, 1)

        o_hi_done, o_lo_done = S("mg_o_hi"), S("mg_o_lo")
        z_hi_done, z_lo_done = S("mg_z_hi"), S("mg_z_lo")
        z_hi, z_lo = h_hi, h_lo

        def pe_merge(pe):
            for i in range(PROJ_ITERS):
                for j in range(8):
                    a, b = (o_hi[:, PAIRS_A:, :], o_lo[:, PAIRS_A:, :]) if j % 2 else (o_hi, o_lo)
                    pe_block(pe, "proj", i, j, i, i + 1, a, b,
                             *(() if i or j else (lambda part: pe.wait_ge(o_hi_done, part + 1),
                                                  lambda part: pe.wait_ge(o_lo_done, part + 1))))
            for j in range(KD):
                pe_block(pe, "out", 0, j, 0, 1, z_hi, z_lo,
                         None if j else lambda part: pe.wait_ge(z_lo_done, 3 * (KD - 1) + part + 1))

        PROJ_SPLITS = {0: 0, 4: 1, 7: 2}

        def pool_gates(pool):
            for slot, out in enumerate(g_out):
                pool.wait_ge(out, 16 * len(range(slot, 2 * KD, GATE_SLOTS)))
            pool.wait_ge(s_out, 1)
            for m in range(KD):
                if m >= 2:
                    pool.wait_ge(z_done, 3 * (m - 1))
                pool.dma_start(gate_in[:, m % 2, :, :],
                               gates_s.rearrange("(a m) p t -> m p a t", a=2)[m]).then_inc(g_in[m % 2], 16)

        def act_merge(act):
            for i in range(PROJ_ITERS):
                for j in range(8):
                    if j in PROJ_SPLITS:
                        act_split(act, "proj", i, PROJ_SPLITS[j], i, i + 1)
                    if j % 2:
                        m = 4 * i + j // 2
                        for part, (s0, w) in enumerate(PARTS):
                            act.wait_ge(z_done, 3 * m + part + 1)
                            act.activation(z_hi[:, m, s0:s0 + w], z_f[:, m % 2, s0:s0 + w],
                                           ACT.Copy).then_inc(z_hi_done, 1)
            for j in range(KD):
                act_split(act, "out", 0, j, 0, 1)
                act_post_square(act, 3, j)

        def dve_merge(dve):
            for i in range(PROJ_ITERS):
                for j in range(8):
                    if j in PROJ_SPLITS:
                        dve_split(dve, "proj", i, PROJ_SPLITS[j], i, i + 1)
                    m = 4 * i + j // 2
                    free = PLAN.free_of["proj", i, j][1]
                    if j % 2 == 0:
                        dve.wait_ge(g_in[m % 2], 16 * (m // 2 + 1))
                        if m >= 2:
                            dve.wait_ge(z_lo_done, 3 * (m - 1))
                        for part, (s0, w) in enumerate(PARTS):
                            dve.tensor_tensor(z_f[:, m % 2, s0:s0 + w], product(dve, "proj", i, j, part, i, i + 1),
                                              gate_in[:, m % 2, 0, s0:s0 + w], ALU.mult).then_inc(freed["dve"], 1)
                        continue
                    for part, (s0, w) in enumerate(PARTS):
                        g = gate_in[:, m % 2, 1, s0:s0 + w]
                        dve.tensor_tensor(g, product(dve, "proj", i, j, part, i, i + 1), g,
                                          ALU.mult).then_inc(freed["dve"], 1)
                    for part, (s0, w) in enumerate(PARTS):
                        z = z_f[:, m % 2, s0:s0 + w]
                        dve.wait_ge(freed["dve"], free + part + 1)
                        dve.tensor_tensor(z, z, gate_in[:, m % 2, 1, s0:s0 + w], ALU.add).then_inc(z_done, 1)
                    for part, (s0, w) in enumerate(PARTS):
                        dve.wait_ge(z_hi_done, 3 * m + part + 1)
                        dve.tensor_tensor(z_lo[:, m, s0:s0 + w], z_f[:, m % 2, s0:s0 + w],
                                          z_hi[:, m, s0:s0 + w].bitcast(F32), ALU.subtract).then_inc(z_lo_done, 1)
            for j in range(KD):
                dve_split(dve, "out", 0, j, 0, 1)
                for part, (s0, w) in enumerate(PARTS):
                    dve.tensor_copy(acc[:, j, s0:s0 + w], product(dve, "out", 0, j, part, 0, 1)
                                    ).then_inc(freed["dve"], 1)
                if j:
                    dve_post_add(dve, 3, j - 1)
            dve_post_add(dve, 3, KD - 1)

        block = ctx.enter_context(nc.Block())

        @block.sync
        def _(sp):
            for n in range(RING):
                sp.dma_start(w_raw[:, n, :], A["w_chunks"][n]).then_inc(w_loaded[n], 16)
            with sp.Fori(1, PLAN.chunks // RING) as i:
                for n in range(RING):
                    sp.wait_ge(w_lo_done, RING * i + (n - RING + 1))
                    sp.dma_start(w_raw[:, n, :], A["w_chunks"][bass.ds(RING * i + n, 1)]
                                 .rearrange("a p c -> (a p) c")).then_inc(w_loaded[n], 16)
            for n in range(PLAN.chunks // RING * RING, PLAN.chunks):
                sp.wait_ge(w_lo_done, n - RING + 1)
                sp.dma_start(w_raw[:, n % RING, :], A["w_chunks"][n]).then_inc(w_loaded[n % RING], 16)
            for part, (s0, w) in enumerate(PARTS):
                wait_x(sp, (5, part))
                sp.dma_start(A["y_t"].rearrange("(k p) t -> p k t", p=P)[:, :, s0:s0 + w], x_res[:, :, s0:s0 + w]
                             ).then_inc(S("y_out"), 16)
            sp.wait_ge(S("y_out"), 48)

        @block.gpsimd
        def _(pool):
            pool.memset(ones[:, :], 1.0).then_inc(S("ones_set"), 1)
            pool.memset(eps_c[:, :], EPS).then_inc(S("ones_set"), 1)
            pool.memset(one_c[:, :], 1.0).then_inc(S("ones_set"), 1)
            pool.wait_ge(S("ones_set"), 3)
            pool.memset(rb[N_BUCKETS:N_BUCKETS + 1, :], 1.0).then_inc(S("rb_one"), 1)
            for dst, name in ((ident, "ident"), (causal_f, "causal"), (pages, "page_table"), (bf_c, "b_f"),
                              (head_sel, "head_sel")):
                pool.dma_start(dst[:, :], A[name]).then_inc(const_in, 16)
            pool.dma_start(gains[:, :, :], A["gains"].rearrange("p (n k) -> p n k", n=6)).then_inc(const_in, 16)
            pool.dma_start(rb[0:N_BUCKETS, :], A["rel_bias"]).then_inc(const_in, 16)
            pool_norms(pool, 0)
            pool_norms(pool, 1)
            wait_x(pool, (1, 2))
            pool.dma_start(x_spill, x_res[:, :, :]).then_inc(S("x_spilled"), 16)
            pool.wait_ge(h_ready, h_count[2, 2])
            for dst, name in ((sel_p, "sel_prompt"), (sel_s, "sel_sample")):
                pool.dma_start(dst[:, :, :].rearrange("p g y -> p (g y)"), A[name]).then_inc(sel_in, 16)
            pool.dma_start(sel_n[:, :], A["sel_new"]).then_inc(sel_in, 16)
            pool.wait_ge(bias_ev, 3)
            for g in range(3):
                hs = slice(g * HPG, (g + 1) * HPG)
                pool.dma_start(bias_rows[hs], bias_row[hs, g, :].unsqueeze(1).broadcast_to([HPG, P, LREL])
                               ).then_inc(bias_out, 16)
            pool.wait_ge(lf_done, 1)
            pool.dma_start(A["lf_t"], lf_a[:, :]).then_inc(lf_out, 16)
            pool.wait_ge(S("x_spilled"), 16)

            def out_qkv(a, col, k_dst, v_dst):
                pool.wait_ge(kf_done, 3 * a + 3)
                pool.dma_start(k_dst, k_f[:, :]).then_inc(k_out, 16)
                pool.wait_ge(vf_done, 3 * a + 3)
                pool.dma_start(v_dst, v_f[:, :]).then_inc(v_out, 16)
                pool.wait_ge(tok_done, a + 1)
                pool.dma_start(qkv_s[:, :, col:col + P] if isinstance(col, int) else
                               qkv_s[:, :, bass.ds(col, P)], tok[:, :, :]).then_inc(tok_out, 16)

            for p in range(PAIRS_A):
                out_qkv(p, p * P, A["ka_t"][p * P:(p + 1) * P, :], A["va_t"][p * P:(p + 1) * P, :])
            for a in range(PAIRS_A, A_LAST):
                d = a - PAIRS_A
                pair, g = d // 3, d % 3
                if d >= 2:
                    pool.wait_ge(d_mt, 16 * (d - 1))
                if d == 0:
                    pool.wait_ge(bias_out, 48)
                if d == 0:
                    pool.wait_ge(oev_done, N_OV * PAIRS_A)
                for hh in range(2):
                    src = bass.AP(bias_rows_t, (g * HPG + 2 * pair + hh) * P * LREL + 127, [[LREL - 1, P], [1, 256]])
                    pool.dma_start(bias_t[:, d % 2, hh, :], src).then_inc(S(f"bias_dma{d % 2}"), 16)
                if g == 2:
                    pool.wait_ge(S(f"bias_dma{d % 2}"), 32 * (d // 2 + 1))
                    pool.memset(bias_t[HD:P, d % 2, :, P:P + HD], NEG).then_inc(bias_in, 1)
                if d and g == 0:
                    pool_weights(pool, pair - 1)
                col = g * 256 + pair * P
                out_qkv(a, WA + col, A["kb_t"][col:col + P, :], A["vb_t"][col:col + P, :])
            for n, (name, keep) in enumerate((("b1", 127), ("b2", 256), ("b3", 256))):
                c = A["cache_" + name]
                pool.dma_start(A["buf_" + name], c[:, c.shape[1] - keep:, :]).then_inc(S("buf_out"), 16)
            pool_weights(pool, PAIRS_B - 1)
            pool_samples(pool)
            pool_gates(pool)
            pool.wait_ge(mm_done, 3 * PLAN.block_of["proj", PROJ_ITERS - 1, 7] + 3)
            pool.wait_ge(z_lo_done, 3 * KD)
            pool.dma_start(x_res[:, :, :], x_spill).then_inc(x_back, 16)
            pool_norms(pool, 2)
            pool_norms(pool, 3)
            pool.wait_ge(S("buf_out"), 48)
            pool.wait_ge(lf_out, 16)
            pool.wait_ge(k_out, 16 * A_LAST)
            pool.wait_ge(v_out, 16 * A_LAST)
            pool.wait_ge(tok_out, 16 * A_LAST)
            pool.wait_ge(bias_out, 48)

        @block.scalar
        def _(act):
            for part, (s0, w) in enumerate(PARTS):
                act.dma_start(x_res[:, :, s0:s0 + w], A["x_t"].rearrange("(k p) t -> p k t", p=P)[:, :, s0:s0 + w]
                              ).then_inc(x_in[part], 16)
            act.wait_ge(S("ones_set"), 3)
            first_splits(act, act_split)
            act_norms(act, 0)
            steps(act, FFN_ITERS, lambda i, lo, hi, first: act_ffn(act, "ffn1", i, lo, hi), last_apart=True)
            act_norms(act, 1)
            act_forget(act)
            act.wait_ge(S("x_spilled"), 16)

            def fox(i, lo, hi, first):
                act_qkv(act, "fox", i, lo, hi, 1)
                act_fox(act, i, lo, hi)
            steps(act, PAIRS_A, fox)
            for d in range(3 * PAIRS_B):
                act_qkv(act, "dil", d, d, d + 1, DIL[d % 3])
                act_dil(act, d, d % 3)
                if d % 3 == 2:
                    act_maxima(act, d // 3)
            act_gates(act)
            for slot, out in enumerate(g_out):
                act.wait_ge(out, 16 * len(range(slot, 2 * KD, GATE_SLOTS)))
            for s0, w in PARTS:
                if s0 + w > SEQ:
                    act.wait_ge(s_out, 1)
                act.activation(o_hi[:, :, s0:s0 + w], o_st[:, :, s0:s0 + w], ACT.Copy).then_inc(o_hi_done, 1)
            act_merge(act)
            act_norms(act, 2)
            steps(act, FFN_ITERS, lambda i, lo, hi, first: act_ffn(act, "ffn2", i, lo, hi), last_apart=True)
            act_norms(act, 3)

        @block.vector
        def _(dve):
            dve.wait_ge(const_in, 112)
            dve.tensor_copy(ident_b[:, :], ident[:, :]).then_inc(S("bf_set"), 1)
            dve.tensor_copy(causal_b[:, :], causal_f[:, :]).then_inc(S("bf_set"), 1)
            dve.tensor_scalar(gains[:, 1, :], gains[:, 1, :], 0.5, None, ALU.mult).then_inc(S("bf_set"), 1)
            dve.tensor_scalar(gains[:, 5, :], gains[:, 5, :], 0.5, None, ALU.mult).then_inc(S("bf_set"), 1)
            dve.wait_ge(S("bf_set"), 4)
            first_splits(dve, dve_split)
            dve_norms(dve, 0)
            steps(dve, FFN_ITERS, lambda i, lo, hi, first: dve_ffn(dve, "ffn1", i, lo, hi, first), last_apart=True)
            dve_norms(dve, 1)
            dve_forget(dve)

            def fox(i, lo, hi, first):
                dve_qkv(dve, "fox", i, lo, hi, 1)
                dve_fox(dve, i, lo, hi)
            steps(dve, PAIRS_A, fox)
            for d in range(3 * PAIRS_B):
                dve_qkv(dve, "dil", d, d, d + 1, DIL[d % 3])
                dve_dil(dve, d, d % 3)
                if d % 3 == 2:
                    dve_maxima(dve, d // 3)
            dve_gates(dve)
            for part, (s0, w) in enumerate(PARTS):
                dve.wait_ge(o_hi_done, part + 1)
                dve.tensor_tensor(o_lo[:, :, s0:s0 + w], o_st[:, :, s0:s0 + w],
                                  o_hi[:, :, s0:s0 + w].bitcast(F32), ALU.subtract).then_inc(o_lo_done, 1)
            dve_merge(dve)
            dve_norms(dve, 2)
            steps(dve, FFN_ITERS, lambda i, lo, hi, first: dve_ffn(dve, "ffn2", i, lo, hi, first), last_apart=True)
            dve_norms(dve, 3)

        @block.tensor
        def _(pe):
            pe_norms(pe, 0)
            steps(pe, FFN_ITERS, lambda i, lo, hi, first: pe_ffn(pe, "ffn1", i, lo, hi), last_apart=True)
            pe_norms(pe, 1)
            pe.wait_ge(S("bf_set"), 4)
            pe_block(pe, "forget", 0, 0, 0, 1, h_hi, h_lo,
                     *wait_h(pe, 2))

            def fox(i, lo, hi, first):
                pe_qkv(pe, "fox", i, lo, hi)
                pe_fox(pe, i, lo, hi)
            steps(pe, PAIRS_A, fox)
            for d in range(3 * PAIRS_B):
                pe_qkv(pe, "dil", d, d, d + 1)
                pe_dil(pe, d, d % 3)
            pe_gates(pe)
            pe_merge(pe)
            pe_norms(pe, 2)
            steps(pe, FFN_ITERS, lambda i, lo, hi, first: pe_ffn(pe, "ffn2", i, lo, hi), last_apart=True)
            pe_norms(pe, 3)


def lay_out_weights(w):
    out = np.zeros((PLAN.chunks, P, CH), np.float32)

    def put(n, block):
        k = block.shape[0] // P
        out[n, :, :k * block.shape[1]] = block.reshape(k, P, -1).transpose(1, 0, 2).reshape(P, -1)

    for ph, pre in (("ffn1", "ffn1_"), ("ffn2", "ffn2_")):
        for i in range(FFN_ITERS):
            c = FIRST_CHUNK[ph] + CHUNKS[ph] * i
            for f in range(2):
                cols = slice((2 * i + f) * P, (2 * i + f + 1) * P)
                put(c + 2 * f, w[pre + "w_gate"][:, cols])
                put(c + 2 * f + 1, w[pre + "w_up"][:, cols])
            down = w[pre + "w_down"][2 * i * P:(2 * i + 2) * P]
            put(c + 4, down[:, 0:512])
            put(c + 5, down[:, 512:1024])
    w_in = w["w_in"]
    put(FIRST_CHUNK["forget"], w_in[:, COL_FA:COL_FA + P])
    for p in range(PAIRS_A):
        for n, col in enumerate((COL_QA, COL_KA, COL_VA)):
            put(FIRST_CHUNK["fox"] + 3 * p + n, w_in[:, col + p * P:col + (p + 1) * P])
    for d in range(3 * PAIRS_B):
        for n, col in enumerate((COL_QB, COL_KB, COL_VB)):
            at = col + (d % 3) * 256 + (d // 3) * P
            put(FIRST_CHUNK["dil"] + 3 * d + n, w_in[:, at:at + P])
    for n in range(2 * KD):
        put(FIRST_CHUNK["gates"] + n, w_in[:, COL_GA + n * P:COL_GA + (n + 1) * P])
    for i in range(PROJ_ITERS):
        c = FIRST_CHUNK["proj"] + 3 * i
        for n in range(2):
            put(c + n, w["w_proj_a"][:, (4 * i + 2 * n) * P:(4 * i + 2 * n + 2) * P])
        put(c + 2, w["w_proj_b"][:, 4 * i * P:(4 * i + 4) * P])
    for n in range(KD):
        put(FIRST_CHUNK["out"] + n, w["w_out"][:, n * P:(n + 1) * P])
    return out


OUTS = {"y_t": (D, T), "ka_t": (WA, T), "va_t": (WA, T), "lf_t": (NHA, T), "kb_t": (WB, T), "vb_t": (WB, T),
        "buf_b1": (NB, 127, 512), "buf_b2": (NB, 256, 512), "buf_b3": (NB, 256, 512)}


def kernel(**inputs):
    import concourse.bacc as bacc
    from concourse.bass_utils import run_bass_kernel_spmd

    x = {k: np.asarray(v) for k, v in inputs.items()}
    w = {k: x[k][0] for k in x if k.endswith(("w_gate", "w_up", "w_down", "w_out", "w_proj_a", "w_proj_b"))
         or k == "w_in"}
    arrays = dict(shape_constants())
    arrays["x_t"] = np.concatenate([x["x_prompt"][0].T, x["x_sample"][:, 0].T], axis=1)
    gains = [x[n][0] for n in ("ffn1_pre_g", "ffn1_post_g", "mix_pre_g", "mix_post_g", "ffn2_pre_g", "ffn2_post_g")]
    arrays["gains"] = np.stack([g.reshape(KD, P).T for g in gains], axis=1).reshape(P, -1)
    arrays["w_chunks"] = lay_out_weights(w)
    arrays["b_f"] = x["b_f"].reshape(NHA, 1)
    arrays["rel_bias"] = x["rel_bias"]
    arrays["page_table"] = x["page_table"].reshape(1, -1)
    arrays["cache_a_k"] = x["cache_a_k"][0].reshape(-1, PAGE, WA)
    arrays["cache_a_v"] = x["cache_a_v"][0].reshape(-1, PAGE, WA)
    arrays["cache_a_logf"] = x["cache_a_logf"][0]
    for g in (1, 2, 3):
        arrays[f"cache_b{g}"] = x[f"cache_b{g}_kv"][0].reshape(NB, -1, 512)
    nc = bacc.Bacc("TRN2", target_bir_lowering=False, num_devices=1, dynamic_dma_scratch_size=4096)
    A = {}
    for name, a in arrays.items():
        arrays[name] = a = np.ascontiguousarray(a)
        A[name] = nc.dram_tensor(name, a.shape, mybir.dt.from_np(a.dtype), kind="ExternalInput").ap()
    for name, shape in OUTS.items():
        A[name] = nc.dram_tensor(name, shape, F32, kind="ExternalOutput").ap()
    build(nc, A)
    r = run_bass_kernel_spmd(nc, [arrays], core_ids=[0]).results[0]

    def tokens(a, heads):
        a = np.asarray(a).T
        return a[:SEQ].reshape(1, 1, SEQ, heads, -1), a[SEQ:].reshape(1, NB, 1, heads, -1)

    y = np.asarray(r["y_t"]).T
    ka, ka_s = tokens(r["ka_t"], NHA)
    va, va_s = tokens(r["va_t"], NHA)
    lf, lf_s = tokens(r["lf_t"], NHA)
    kb, kb_s = tokens(r["kb_t"], 3 * HPG)
    vb, vb_s = tokens(r["vb_t"], 3 * HPG)
    prompt, sample = [], []
    for g, window in enumerate((128, 512, 2048)):
        hs = slice(g * HPG, (g + 1) * HPG)
        keep = min(window, SEQ)
        prompt.append(np.stack([kb[:, :, SEQ - keep:, hs], vb[:, :, SEQ - keep:, hs]], axis=3))
        old = np.asarray(r[f"buf_b{g + 1}"]).reshape(1, NB, -1, 2, HPG, HD)
        new = np.stack([kb_s[:, :, :, hs], vb_s[:, :, :, hs]], axis=3)
        sample.append(np.concatenate([old, new], axis=2))
    return (y[:SEQ][None], y[SEQ:][:, None], ka, va, lf[..., 0], *prompt, ka_s, va_s, lf_s[..., 0], *sample)
```
